# Optimizing a Trainium2 kernel written in Bass

```python
import jax, jax.numpy as jnp
from jax import lax
import numpy as np

D_MODEL = 1024
BATCH = 1
SEQ = 256
DEPTH = 2

N_META = 16
N_A_LAYERS = DEPTH // 2
N_B_LAYERS = DEPTH - N_A_LAYERS
CONV_W = 3
N_HEADS = 8
QK_NOPE_DIM = 128
QK_ROPE_DIM = 64
V_DIM = 128
Q_RANK = 384
KV_RANK = 256
ROPE_THETA = 10000.0
Q_BLOCK = 128
N_GROUPS = 8
EXPERTS_PER_GROUP = 8
N_EXPERTS = N_GROUPS * EXPERTS_PER_GROUP
TOP_K_IN_GROUP = 2
D_EXPERT = 256
EXPERT_BLOCK = 128
NORM_EPS = 1e-6


def rmsnorm(x, g):
    xf = x.astype(jnp.float32)
    y = xf * lax.rsqrt(jnp.mean(xf * xf, axis=-1, keepdims=True) + NORM_EPS)
    return (y * g.astype(jnp.float32)).astype(x.dtype)

def rope_tables(t):
    inv = ROPE_THETA ** (-jnp.arange(0, QK_ROPE_DIM, 2, dtype=jnp.float32) / QK_ROPE_DIM)
    ang = jnp.arange(t, dtype=jnp.float32)[:, None] * inv[None, :]
    return jnp.cos(ang), jnp.sin(ang)

def apply_rope(x, cos, sin):
    half = x.shape[-1] // 2
    x1, x2 = x[..., :half], x[..., half:]
    cos = cos.astype(x.dtype)
    sin = sin.astype(x.dtype)
    return jnp.concatenate([x1 * cos - x2 * sin, x1 * sin + x2 * cos], axis=-1)

def short_conv_mixer(hn, w_in, conv_w, w_out):
    bcu = hn @ w_in
    b, c, u = jnp.split(bcu, 3, axis=-1)
    z = c * u
    z = lax.conv_general_dilated(z, conv_w.astype(z.dtype), window_strides=(1,),
                                 padding=((CONV_W - 1, 0),),
                                 dimension_numbers=('NWC', 'WIO', 'NWC'),
                                 feature_group_count=z.shape[-1])
    return (b * z) @ w_out

def shared_kv_side(h, kv_g, w_dkv, ckv_g, w_ukv, cos, sin):
    bsz, t, _ = h.shape
    a = rmsnorm(h, kv_g) @ w_dkv
    c_kv = rmsnorm(a[..., :KV_RANK], ckv_g)
    k_rope = apply_rope(a[..., KV_RANK:], cos, sin)
    kv = (c_kv @ w_ukv).reshape(bsz, t, N_HEADS, QK_NOPE_DIM + V_DIM)
    return kv[..., :QK_NOPE_DIM], k_rope, kv[..., QK_NOPE_DIM:]

def causal_block_attention(q_nope, q_rope, k_nope, k_rope, v):
    bsz, t, nh, _ = q_nope.shape
    nqb = -(-t // Q_BLOCK)
    pad = nqb * Q_BLOCK - t
    def blocks(q):
        q = jnp.pad(q, ((0, 0), (0, pad), (0, 0), (0, 0)))
        return q.reshape(bsz, nqb, Q_BLOCK, nh, q.shape[-1]).transpose(1, 0, 2, 3, 4)
    qn, qr = blocks(q_nope), blocks(q_rope)
    kpos = jnp.arange(t)
    scale = (QK_NOPE_DIM + QK_ROPE_DIM) ** -0.5
    def one_block(args):
        qn_b, qr_b, j = args
        qpos = j * Q_BLOCK + jnp.arange(Q_BLOCK)
        s = (jnp.einsum('bqhd,bkhd->bhqk', qn_b, k_nope)
             + jnp.einsum('bqhd,bkd->bhqk', qr_b, k_rope)).astype(jnp.float32) * scale
        s = jnp.where(kpos[None, :] <= qpos[:, None], s, -jnp.inf)
        p = jax.nn.softmax(s, axis=-1).astype(v.dtype)
        return jnp.einsum('bhqk,bkhd->bqhd', p, v)
    o = lax.map(one_block, (qn, qr, jnp.arange(nqb, dtype=jnp.int32)))
    o = o.transpose(1, 0, 2, 3, 4).reshape(bsz, nqb * Q_BLOCK, nh * v.shape[-1])
    return o[:, :t]

def mla_mixer(hn, w_dq, cq_g, w_uq, w_o, k_nope, k_rope, v, cos, sin):
    bsz, t, _ = hn.shape
    cq = rmsnorm(hn @ w_dq, cq_g)
    q = (cq @ w_uq).reshape(bsz, t, N_HEADS, QK_NOPE_DIM + QK_ROPE_DIM)
    q_nope = q[..., :QK_NOPE_DIM]
    q_rope = apply_rope(q[..., QK_NOPE_DIM:], cos[:, None, :], sin[:, None, :])
    o = causal_block_attention(q_nope, q_rope, k_nope, k_rope, v)
    return o @ w_o

def hier_moe(hn, w_grp, w_exp, w_gate, w_up, w_down):
    bsz, t, d = hn.shape
    n = bsz * t
    xf = hn.reshape(n, d)
    g_logits = (xf @ w_grp).astype(jnp.float32)
    p_grp = jax.nn.softmax(g_logits, axis=-1)
    grp = jnp.argmax(g_logits, axis=-1).astype(jnp.int32)
    p_g = jnp.max(p_grp, axis=-1, keepdims=True)
    e_logits = (xf @ w_exp).astype(jnp.float32).reshape(n, N_GROUPS, EXPERTS_PER_GROUP)
    e_in = jnp.einsum('ng,nge->ne', jax.nn.one_hot(grp, N_GROUPS, dtype=jnp.float32), e_logits)
    top_p, top_i = lax.top_k(jax.nn.softmax(e_in, axis=-1), TOP_K_IN_GROUP)
    gate = p_g * top_p / jnp.sum(top_p, axis=-1, keepdims=True)
    expert = grp[:, None] * EXPERTS_PER_GROUP + top_i.astype(jnp.int32)
    a = n * TOP_K_IN_GROUP
    e_a = expert.reshape(a)
    w_a = gate.reshape(a).astype(hn.dtype)
    tok_a = jnp.repeat(jnp.arange(n, dtype=jnp.int32), TOP_K_IN_GROUP)
    counts = jax.ops.segment_sum(jnp.ones((a,), jnp.int32), e_a, num_segments=N_EXPERTS)
    padded = ((counts + EXPERT_BLOCK - 1) // EXPERT_BLOCK) * EXPERT_BLOCK
    pad_end = jnp.cumsum(padded)
    pad_start = pad_end - padded
    start = jnp.cumsum(counts) - counts
    order = jnp.argsort(e_a)
    e_s = e_a[order]
    dest = pad_start[e_s] + jnp.arange(a, dtype=jnp.int32) - start[e_s]
    n_blocks = (a + N_EXPERTS * (EXPERT_BLOCK - 1) + EXPERT_BLOCK - 1) // EXPERT_BLOCK
    p_slots = n_blocks * EXPERT_BLOCK
    slot_tok = jnp.full((p_slots,), n, jnp.int32).at[dest].set(tok_a[order])
    slot_w = jnp.zeros((p_slots,), hn.dtype).at[dest].set(w_a[order])
    blk_expert = jnp.minimum(jnp.searchsorted(pad_end, jnp.arange(n_blocks, dtype=jnp.int32) * EXPERT_BLOCK,
                                              side='right'), N_EXPERTS - 1).astype(jnp.int32)
    x_pad = jnp.concatenate([xf, jnp.zeros((1, d), xf.dtype)], axis=0)
    xs = x_pad[slot_tok].reshape(n_blocks, EXPERT_BLOCK, d)
    def expert_block(args):
        xb, e = args
        hh = jax.nn.silu(xb @ w_gate[e]) * (xb @ w_up[e])
        return hh @ w_down[e]
    ys = lax.map(expert_block, (xs, blk_expert)).reshape(p_slots, d)
    y = jnp.zeros((n + 1, d), ys.dtype).at[slot_tok].add(ys * slot_w[:, None])[:n]
    return y.reshape(bsz, t, d)

def first_inputs(seed: int = 0) -> dict:
    key = jax.random.key(seed)
    ks = jax.random.split(key, 21)
    def nrm(k, shape, scale):
        return jax.random.normal(k, shape, jnp.float32) * scale
    d = D_MODEL
    return {
        'x': nrm(ks[0], (BATCH, SEQ, d), 1.0),
        'meta_tokens': nrm(ks[1], (N_META, d), 1.0),
        'norm_mix_g': 1.0 + nrm(ks[2], (DEPTH, d), 0.02),
        'norm_ffn_g': 1.0 + nrm(ks[3], (DEPTH, d), 0.02),
        'conv_w_in': nrm(ks[4], (N_A_LAYERS, d, 3 * d), d ** -0.5),
        'conv_w': nrm(ks[5], (N_A_LAYERS, CONV_W, 1, d), CONV_W ** -0.5),
        'conv_w_out': nrm(ks[6], (N_A_LAYERS, d, d), d ** -0.5),
        'kv_norm_g': 1.0 + nrm(ks[7], (d,), 0.02),
        'w_dkv': nrm(ks[8], (d, KV_RANK + QK_ROPE_DIM), d ** -0.5),
        'ckv_norm_g': 1.0 + nrm(ks[9], (KV_RANK,), 0.02),
        'w_ukv': nrm(ks[10], (KV_RANK, N_HEADS * (QK_NOPE_DIM + V_DIM)), KV_RANK ** -0.5),
        'w_dq': nrm(ks[11], (N_B_LAYERS, d, Q_RANK), d ** -0.5),
        'cq_norm_g': 1.0 + nrm(ks[12], (N_B_LAYERS, Q_RANK), 0.02),
        'w_uq': nrm(ks[13], (N_B_LAYERS, Q_RANK, N_HEADS * (QK_NOPE_DIM + QK_ROPE_DIM)), Q_RANK ** -0.5),
        'w_o': nrm(ks[14], (N_B_LAYERS, N_HEADS * V_DIM, d), (N_HEADS * V_DIM) ** -0.5),
        'w_grp': nrm(ks[15], (DEPTH, d, N_GROUPS), d ** -0.5),
        'w_exp': nrm(ks[16], (DEPTH, d, N_EXPERTS), d ** -0.5),
        'w_gate': nrm(ks[17], (DEPTH, N_EXPERTS, d, D_EXPERT), d ** -0.5),
        'w_up': nrm(ks[18], (DEPTH, N_EXPERTS, d, D_EXPERT), d ** -0.5),
        'w_down': nrm(ks[19], (DEPTH, N_EXPERTS, D_EXPERT, d), D_EXPERT ** -0.5),
        'final_norm_g': 1.0 + nrm(ks[20], (d,), 0.02),
    }

def first_block(x, meta_tokens, norm_mix_g, norm_ffn_g, conv_w_in, conv_w, conv_w_out,
              kv_norm_g, w_dkv, ckv_norm_g, w_ukv, w_dq, cq_norm_g, w_uq, w_o,
              w_grp, w_exp, w_gate, w_up, w_down, final_norm_g):
    bsz = x.shape[0]
    meta = jnp.broadcast_to(meta_tokens[None].astype(x.dtype), (bsz, N_META, x.shape[-1]))
    h = jnp.concatenate([meta, x], axis=1)
    cos, sin = rope_tables(h.shape[1])
    shared = None
    for i in range(DEPTH):
        if i < N_A_LAYERS:
            h = h + short_conv_mixer(rmsnorm(h, norm_mix_g[i]), conv_w_in[i], conv_w[i], conv_w_out[i])
        else:
            if shared is None:
                shared = shared_kv_side(h, kv_norm_g, w_dkv, ckv_norm_g, w_ukv, cos, sin)
            j = i - N_A_LAYERS
            k_nope, k_rope, v = shared
            h = h + mla_mixer(rmsnorm(h, norm_mix_g[i]), w_dq[j], cq_norm_g[j], w_uq[j], w_o[j],
                              k_nope, k_rope, v, cos, sin)
        h = h + hier_moe(rmsnorm(h, norm_ffn_g[i]), w_grp[i], w_exp[i], w_gate[i], w_up[i], w_down[i])
    return rmsnorm(h, final_norm_g)[:, N_META:]


MIX_WIDTH = 2 * D_MODEL
HEAD_DIM = 128
HGRN_WIDTH = MIX_WIDTH // 2
NSA_WIDTH = MIX_WIDTH - HGRN_WIDTH
HGRN_HEADS = HGRN_WIDTH // HEAD_DIM
NSA_HEADS = NSA_WIDTH // HEAD_DIM
NSA_KV_GROUPS = 2
NSA_HEADS_PER_GROUP = NSA_HEADS // NSA_KV_GROUPS
KV_WIDTH = NSA_KV_GROUPS * HEAD_DIM
N_BRANCHES = 3
HGRN_CHUNK = 64
CMP_BLOCK = 32
CMP_STRIDE = 16
SEL_BLOCK = 64
N_SELECT = 16
WINDOW = 512
ROPE_THETA_2 = 500000.0
ROT_DIM = HEAD_DIM // 4
FORCE_SCORE = 1e4
IN_SPLITS = (HGRN_WIDTH, HGRN_WIDTH, HGRN_WIDTH, HGRN_WIDTH,
             NSA_WIDTH, KV_WIDTH, KV_WIDTH, KV_WIDTH, KV_WIDTH, KV_WIDTH, KV_WIDTH,
             NSA_HEADS * N_BRANCHES, NSA_WIDTH)
IN_COLS = sum(IN_SPLITS)


def rmsnorm_2(x, g):
    xf = x.astype(jnp.float32)
    y = xf * lax.rsqrt(jnp.mean(xf * xf, axis=-1, keepdims=True) + NORM_EPS)
    return (y * g.astype(jnp.float32)).astype(x.dtype)

def partial_rope(x, pos):
    half = ROT_DIM // 2
    inv = ROPE_THETA_2 ** (-2.0 * jnp.arange(half, dtype=jnp.float32) / ROT_DIM)
    ang = pos.astype(jnp.float32)[:, None] * inv[None, :]
    cos = jnp.cos(ang)[None, :, None, :]
    sin = jnp.sin(ang)[None, :, None, :]
    xf = x.astype(jnp.float32)
    x1 = xf[..., :half]
    x2 = xf[..., half:ROT_DIM]
    out = jnp.concatenate([x1 * cos - x2 * sin, x2 * cos + x1 * sin, xf[..., ROT_DIM:]], axis=-1)
    return out.astype(x.dtype)

def masked_softmax(s, mask, axis):
    s = jnp.where(mask, s, -jnp.inf)
    m = jnp.max(s, axis=axis, keepdims=True)
    m = jnp.where(jnp.isfinite(m), m, 0.0)
    p = jnp.exp(s - m)
    return p / jnp.maximum(jnp.sum(p, axis=axis, keepdims=True), 1e-30)

def hgrn2_mixer(q, f_logit, i, lb):
    B, S, H, D = q.shape
    C = HGRN_CHUNK
    N = S // C
    log_f = jnp.logaddexp(jnp.log(lb), jnp.log1p(-lb) + jax.nn.log_sigmoid(f_logit.astype(jnp.float32)))
    k = -jnp.expm1(log_f)

    def chunks(a):
        return a.astype(jnp.float32).reshape(B, N, C, H, D).transpose(1, 0, 3, 2, 4)

    qc, kc, vc = chunks(q), chunks(k), chunks(i)
    bc = jnp.cumsum(chunks(log_f), axis=3)
    causal = jnp.tril(jnp.ones((C, C), dtype=bool))

    def step(state, xs):
        q_, k_, v_, b_ = xs
        o_inter = jnp.einsum('bhtk,bhkv->bhtv', q_ * jnp.exp(b_), state)
        diff = jnp.where(causal[:, :, None], b_[:, :, :, None, :] - b_[:, :, None, :, :], -jnp.inf)
        attn = jnp.einsum('bhtk,bhsk,bhtsk->bhts', q_, k_, jnp.exp(diff))
        o_intra = jnp.einsum('bhts,bhsv->bhtv', attn, v_)
        b_last = b_[:, :, -1:, :]
        state = state * jnp.exp(b_last[:, :, 0, :, None]) + jnp.einsum(
            'bhsk,bhsv->bhkv', k_ * jnp.exp(b_last - b_), v_)
        return state, o_inter + o_intra

    s0 = jnp.zeros((B, H, D, D), jnp.float32)
    _, o = lax.scan(step, s0, (qc, kc, vc, bc))
    return o.transpose(1, 0, 3, 2, 4).reshape(B, S, H, D).astype(q.dtype)

def compress(kv, pos_emb, w1, b1, w2):
    B, S, G, D = kv.shape
    n_cmp = (S - CMP_BLOCK) // CMP_STRIDE + 1
    idx = jnp.arange(n_cmp)[:, None] * CMP_STRIDE + jnp.arange(CMP_BLOCK)[None, :]
    blocks = kv[:, idx] + pos_emb[None, None, :, None, :]
    flat = blocks.transpose(0, 1, 3, 2, 4).reshape(B, n_cmp, G, CMP_BLOCK * D)
    return jax.nn.silu(flat @ w1 + b1) @ w2

def nsa_mixer(q, kc, vc, ks, vs, kw, vw, gate_logits, cmp_k, cmp_v):
    B, S, H, D = q.shape
    G, HG = NSA_KV_GROUPS, NSA_HEADS_PER_GROUP
    pos = jnp.arange(S)
    q = partial_rope(q, pos)
    ks = partial_rope(ks, pos)
    kw = partial_rope(kw, pos)
    k_cmp = compress(kc, *cmp_k)
    v_cmp = compress(vc, *cmp_v).astype(jnp.float32)
    n_cmp = k_cmp.shape[1]
    cmp_start = jnp.arange(n_cmp) * CMP_STRIDE
    cmp_end = cmp_start + CMP_BLOCK - 1
    k_cmp = partial_rope(k_cmp, cmp_end).astype(jnp.float32)
    n_sel_blocks = S // SEL_BLOCK
    n_top = min(N_SELECT, n_sel_blocks)
    sel_start = jnp.arange(n_sel_blocks) * SEL_BLOCK
    overlap = ((cmp_start[:, None] < sel_start[None, :] + SEL_BLOCK)
               & (cmp_start[:, None] + CMP_BLOCK > sel_start[None, :])).astype(jnp.float32)
    ks_blocks = ks.reshape(B, n_sel_blocks, SEL_BLOCK, G, D).transpose(0, 3, 1, 2, 4)
    vs_blocks = vs.reshape(B, n_sel_blocks, SEL_BLOCK, G, D).transpose(0, 3, 1, 2, 4)
    kw_pad = jnp.pad(kw, ((0, 0), (WINDOW, 0), (0, 0), (0, 0)))
    vw_pad = jnp.pad(vw, ((0, 0), (WINDOW, 0), (0, 0), (0, 0)))
    gates = jax.nn.sigmoid(gate_logits.astype(jnp.float32)).reshape(B, S, G, HG, N_BRANCHES)
    scale = HEAD_DIM ** -0.5
    b_idx = jnp.arange(B)[:, None, None, None]
    g_idx = jnp.arange(G)[None, :, None, None]
    blk = jnp.arange(n_sel_blocks)

    def query_block(qb):
        q0 = qb * Q_BLOCK
        t = q0 + jnp.arange(Q_BLOCK)
        qblk = lax.dynamic_slice_in_dim(q, q0, Q_BLOCK, axis=1).reshape(
            B, Q_BLOCK, G, HG, D).astype(jnp.float32)
        s_c = jnp.einsum('btghd,bngd->bghtn', qblk, k_cmp) * scale
        p_c = masked_softmax(s_c, cmp_end[None, :] <= t[:, None], -1)
        o_c = jnp.einsum('bghtn,bngd->btghd', p_c, v_cmp)
        imp = jnp.einsum('bghtn,nj->bgtj', p_c, overlap)
        cur = t // SEL_BLOCK
        forced = (blk[None, :] == 0) | (blk[None, :] == cur[:, None]) | (blk[None, :] == cur[:, None] - 1)
        valid = blk[None, :] * SEL_BLOCK <= t[:, None]
        imp = jnp.where(forced, FORCE_SCORE, jnp.where(valid, imp, -1.0))
        _, top = lax.top_k(imp, n_top)
        k_s = ks_blocks[b_idx, g_idx, top].astype(jnp.float32)
        v_s = vs_blocks[b_idx, g_idx, top].astype(jnp.float32)
        key_pos = top[..., None] * SEL_BLOCK + jnp.arange(SEL_BLOCK)
        mask_s = (key_pos <= t[None, None, :, None, None])[:, :, None]
        s_s = jnp.einsum('btghd,bgtnld->bghtnl', qblk, k_s) * scale
        p_s = masked_softmax(s_s, mask_s, (-2, -1))
        o_s = jnp.einsum('bghtnl,bgtnld->btghd', p_s, v_s)
        k_w = lax.dynamic_slice_in_dim(kw_pad, q0, WINDOW + Q_BLOCK, axis=1).astype(jnp.float32)
        v_w = lax.dynamic_slice_in_dim(vw_pad, q0, WINDOW + Q_BLOCK, axis=1).astype(jnp.float32)
        kp = q0 - WINDOW + jnp.arange(WINDOW + Q_BLOCK)
        mask_w = (kp[None, :] >= 0) & (kp[None, :] <= t[:, None]) & (t[:, None] - kp[None, :] < WINDOW)
        s_w = jnp.einsum('btghd,bkgd->bghtk', qblk, k_w) * scale
        p_w = masked_softmax(s_w, mask_w, -1)
        o_w = jnp.einsum('bghtk,bkgd->btghd', p_w, v_w)
        g = lax.dynamic_slice_in_dim(gates, q0, Q_BLOCK, axis=1)
        o = g[..., 0:1] * o_c + g[..., 1:2] * o_s + g[..., 2:3] * o_w
        return o.reshape(B, Q_BLOCK, H, D)

    out = lax.map(query_block, jnp.arange(S // Q_BLOCK))
    return out.transpose(1, 0, 2, 3, 4).reshape(B, S, H, D).astype(q.dtype)

def second_inputs(seed: int = 0) -> dict:
    key = jax.random.key(seed)
    k = jax.random.split(key, 16)

    def nrm(kk, shape, scale):
        return jax.random.normal(kk, shape, jnp.float32) * scale

    L, D = CMP_BLOCK, HEAD_DIM
    return {
        "x": nrm(k[0], (BATCH, SEQ, D_MODEL), 1.0),
        "pre_norm": 1.0 + nrm(k[1], (DEPTH, D_MODEL), 0.02),
        "post_norm": 1.0 + nrm(k[2], (DEPTH, D_MODEL), 0.02),
        "w_in": nrm(k[3], (DEPTH, D_MODEL, IN_COLS), D_MODEL ** -0.5),
        "hgrn_lb_logits": nrm(k[4], (DEPTH, HGRN_WIDTH), 0.5),
        "hgrn_out_norm": 1.0 + nrm(k[5], (DEPTH, HEAD_DIM), 0.02),
        "cmp_pos_k": nrm(k[6], (DEPTH, L, D), 0.1),
        "cmp_w1_k": nrm(k[7], (DEPTH, L * D, D), (L * D) ** -0.5),
        "cmp_b1_k": nrm(k[8], (DEPTH, D), 0.01),
        "cmp_w2_k": nrm(k[9], (DEPTH, D, D), D ** -0.5),
        "cmp_pos_v": nrm(k[10], (DEPTH, L, D), 0.1),
        "cmp_w1_v": nrm(k[11], (DEPTH, L * D, D), (L * D) ** -0.5),
        "cmp_b1_v": nrm(k[12], (DEPTH, D), 0.01),
        "cmp_w2_v": nrm(k[13], (DEPTH, D, D), D ** -0.5),
        "w_out": nrm(k[14], (DEPTH, MIX_WIDTH, D_MODEL), MIX_WIDTH ** -0.5),
    }

def second_block(x, pre_norm, post_norm, w_in, hgrn_lb_logits, hgrn_out_norm,
              cmp_pos_k, cmp_w1_k, cmp_b1_k, cmp_w2_k,
              cmp_pos_v, cmp_w1_v, cmp_b1_v, cmp_w2_v, w_out):
    B, S, _ = x.shape
    lb_probs = jax.nn.softmax(hgrn_lb_logits.astype(jnp.float32), axis=0)
    lower_bounds = jnp.maximum(jnp.cumsum(lb_probs, axis=0) - lb_probs[0:1], 0.0)
    offsets = np.cumsum(IN_SPLITS)[:-1].tolist()

    def heads(a):
        return a.reshape(B, S, -1, HEAD_DIM)

    for layer in range(DEPTH):
        h = rmsnorm_2(x, pre_norm[layer])
        proj = h @ w_in[layer]
        (hq, hf, hi, hz, nq, kc, vc, ks, vs, kw, vw, ng, nz) = jnp.split(proj, offsets, axis=-1)
        o_h = hgrn2_mixer(heads(hq), heads(hf), heads(hi),
                          lower_bounds[layer].reshape(HGRN_HEADS, HEAD_DIM))
        o_h = rmsnorm_2(o_h, hgrn_out_norm[layer]).reshape(B, S, HGRN_WIDTH) * jax.nn.silu(hz)
        o_n = nsa_mixer(heads(nq), heads(kc), heads(vc), heads(ks), heads(vs), heads(kw), heads(vw), ng,
                        (cmp_pos_k[layer], cmp_w1_k[layer], cmp_b1_k[layer], cmp_w2_k[layer]),
                        (cmp_pos_v[layer], cmp_w1_v[layer], cmp_b1_v[layer], cmp_w2_v[layer]))
        o_n = o_n.reshape(B, S, NSA_WIDTH) * jax.nn.silu(nz)
        y = jnp.concatenate([o_h, o_n], axis=-1).astype(x.dtype) @ w_out[layer]
        x = x + rmsnorm_2(y, post_norm[layer]).astype(x.dtype)
    return x


def setup_inputs(seed=0):
    out = dict(first_inputs(seed))
    for name, value in second_inputs(seed + 1).items():
        if name != "x":
            out[name + "_2"] = value
    return out


def reference(
    x, meta_tokens, norm_mix_g, norm_ffn_g, conv_w_in, conv_w, conv_w_out, kv_norm_g, w_dkv,
    ckv_norm_g, w_ukv, w_dq, cq_norm_g, w_uq, w_o, w_grp, w_exp, w_gate, w_up, w_down,
    final_norm_g, pre_norm_2, post_norm_2, w_in_2, hgrn_lb_logits_2, hgrn_out_norm_2,
    cmp_pos_k_2, cmp_w1_k_2, cmp_b1_k_2, cmp_w2_k_2, cmp_pos_v_2, cmp_w1_v_2, cmp_b1_v_2,
    cmp_w2_v_2, w_out_2,
):
    x = first_block(
        x, meta_tokens, norm_mix_g, norm_ffn_g, conv_w_in, conv_w, conv_w_out, kv_norm_g, w_dkv,
        ckv_norm_g, w_ukv, w_dq, cq_norm_g, w_uq, w_o, w_grp, w_exp, w_gate, w_up, w_down,
        final_norm_g,
    )
    return second_block(
        x, pre_norm_2, post_norm_2, w_in_2, hgrn_lb_logits_2, hgrn_out_norm_2, cmp_pos_k_2,
        cmp_w1_k_2, cmp_b1_k_2, cmp_w2_k_2, cmp_pos_v_2, cmp_w1_v_2, cmp_b1_v_2, cmp_w2_v_2,
        w_out_2,
    )


_drawn_inputs = setup_inputs


def setup_inputs(seed=0):
    import zlib

    import numpy as np

    out = dict(_drawn_inputs(seed))
    spreads = {}
    factors = {'kv_norm_g': 6.676,
     'ckv_norm_g': 6.503,
     'cq_norm_g': 8.0,
     'cmp_pos_k_2': 8.0,
     'cmp_b1_k_2': 64.0,
     'cmp_b1_v_2': 8.0}
    for name, (base, spread) in spreads.items():
        noise = np.random.default_rng([zlib.crc32(name.encode()), seed]).standard_normal(out[name].shape)
        drawn = base * np.exp(spread * noise) if base else spread * noise
        out[name] = __import__('jax').numpy.asarray(drawn.astype(out[name].dtype))
    for name, factor in factors.items():
        out[name] = (out[name] * factor).astype(out[name].dtype)
    return out
```

```python
from contextlib import ExitStack

import concourse.bass as bass
from concourse import mybir

F32 = mybir.dt.float32
I32 = mybir.dt.int32
U32 = mybir.dt.uint32
ALU = mybir.AluOpType
ACT = mybir.ActivationFunctionType
AX = mybir.AxisListType.X

P = 128
D = 1024
DC = D // P
META = 16
SEQ = 256
T = META + SEQ
TT = 3
TP = TT * P
HEADS = 8
EPS = 1e-6
UNIT = 2048
RING = 6
G = 8
EG = 8
NE = G * EG
QUADS = NE // 4
SLOT = 32
ROUNDS = -(-T // SLOT)
QU = 12
MLA_SCALE = 192.0 ** -0.5
NSA_SCALE = 128.0 ** -0.5
NCMP = 15
LEVELS = (64, 32, 16, 8, 4, 2)
CHUNK = 64
PAIRS = 2 * HEADS
LN_LEAST = 2.0 ** -63

CONV_UNITS = 16
MLA_UNITS = 12
L2_UNITS = 42
ARENA = 29810

F_F, F_Q, F_NQ, F_KS, F_KW, F_KC, F_VC, F_HZ, F_NZ = 0, 8, 16, 24, 26, 28, 30, 32, 40
SPLITS = dict(hq=1024, hf=1024, hi=1024, hz=1024, nq=1024, kc=256, vc=256, ks=256, vs=256, kw=256, vw=256, ng=24, nz=1024)


def units_2():
    at, first = 0, {}
    for k, n in SPLITS.items():
        first[k] = at
        at += n
    out = []
    for name, kind, to in (("hf", "f", F_F), ("hq", "f", F_Q), ("hi", "v", 0), ("nq", "f", F_NQ), ("ks", "f", F_KS),
                           ("kw", "f", F_KW), ("kc", "f", F_KC), ("vc", "f", F_VC), ("vs", "v", 4), ("vw", "v", 5),
                           ("hz", "f", F_HZ), ("nz", "f", F_NZ)):
        for u in range(SPLITS[name] // 256):
            out.append((first[name] + 256 * u, kind, to + u * (2 if kind == "f" else 1)))
    return out, first["ng"]


COLUMNS_2, GATE_COLUMN = units_2()
UNITS_2 = [(kind, to) for _, kind, to in COLUMNS_2]

CONST = dict(ident=128, ones=128, upper=128, iota=(ROUNDS + 1) * SLOT, rounds=ROUNDS, revidx=8, valid=3,
             mask=TT * T, cmask=2 * NCMP, cvalid=2 * NCMP, reset=SEQ, lev=7 * P,
             cosm=T, sinm=T, rotm=64, cosn=SEQ, sinn=SEQ, rotn=32, cosc=NCMP, sinc=NCMP)
VEC = dict(mix0=8, mix1=8, ffn0=8, ffn1=8, convw=24, kvg=8, ckvg=2, cqg=3, fing=8,
           pre0=8, pre1=8, post0=8, post1=8, lbl=16, on0=1, on1=1,
           b1k0=1, b1k1=1, b1v0=1, b1v1=1, posk0=32, posk1=32, posv0=32, posv1=32,
           w2k0=128, w2k1=128, w2v0=128, w2v1=128, wng0=192, wng1=192, wr0=576, wr1=576)


def offsets(table):
    at, out = 0, {}
    for k, n in table.items():
        out[k] = (at, n)
        at += n
    return out, at


CONST_AT, CONST_N = offsets(CONST)
VEC_AT, VEC_N = offsets(VEC)


class Turns:

    def __init__(self, eng):
        self.eng, self.seen = eng, {}

    def next(self, sem, k=1):
        self.seen[sem.name] = self.seen.get(sem.name, 0) + k
        self.eng.wait_ge(sem, self.seen[sem.name])


class Chain(Turns):

    def __init__(self, eng, sem):
        super().__init__(eng)
        self.sem = sem

    def link(self, ins, sem=None):
        sem = sem or self.sem
        ins.then_inc(sem, 1)
        self.next(sem)


def build(nc, h_in, consts_in, vecs_in, dense, experts, out):
    with ExitStack() as ctx:
        def sb(name, shape, dt=F32):
            return ctx.enter_context(nc.sbuf_tensor(name, shape, dt))

        def sem(name):
            return ctx.enter_context(nc.semaphore(name))

        ring = sb("ring", [P, RING, UNIT])
        consts = sb("consts", [P, CONST_N])
        vecs = sb("vecs", [P, VEC_N])
        hT = sb("hT", [P, DC, T])
        x2 = sb("x2", [P, DC, SEQ])
        root = sb("root", [P, T])
        eps = sb("eps", [P, 1])
        n_iter = sb("n_iter", [P, 2], I32)
        arena = sb("arena", [P, ARENA])
        psum = ctx.enter_context(nc.psum_tensor("banks", [P, 8, 512], F32))
        flat = psum[:, :, :].rearrange("p b n -> p (b n)")

        def C(name):
            a, n = CONST_AT[name]
            return consts[:, a:a + n]

        def V(name):
            a, n = VEC_AT[name]
            return vecs[:, a:a + n]

        class Place:

            def __init__(self, at=0):
                self.at = at

            def __call__(self, *shape):
                n = 1
                for k in shape:
                    n *= k
                v = arena[:, self.at:self.at + n]
                self.at += n
                assert self.at <= ARENA, self.at
                if len(shape) == 2:
                    v = v.rearrange("p (a b) -> p a b", a=shape[0])
                if len(shape) == 3:
                    v = v.rearrange("p (a b c) -> p a b c", a=shape[0], b=shape[1])
                return v

        const_in = sem("const_in")
        landed = [sem(f"landed{s}") for s in range(RING)]
        nrm_sq, nrm_sum, nrm_root, nrm_out = (sem(n) for n in ("nrm_sq", "nrm_sum", "nrm_root", "nrm_out"))
        dve_chain, act_chain = sem("dve_chain"), sem("act_chain")
        cv_pe, cv_c, cv_y = sem("cv_pe"), sem("cv_c"), sem("cv_y")
        pr_done, pr_add = sem("pr_done"), sem("pr_add")
        MOE = ("landed0 landed1 landed2 landed3 landed4 landed5 used lg_done xr_done xr_ready dg_ready exp_done "
               "route_ready rank_done iter_ready st_ready prep_done xs_ready sw_ready gu_done silu_done h_ready "
               "ht_done ht_ready dn_done ya_ready yd_ready cmb_done add_done").split()
        moe_sem = [{n: sem(f"m{layer}_{n}") for n in MOE} for layer in range(2)]
        ml = {n: sem(f"mla_{n}") for n in ("a_done a_copied pj_done pj_copied rot_done rope_done sc_done sm_ready s_ready "
                                           "e_done p_ready pt_done pt_copied pv_done o_ready").split()}
        b2 = {n: sem(f"b2_{n}") for n in (
            "lb_d lb_e pj_done pj_copied ng_done gate_ready sig_done lin_ready ln_done lv_d lv_e lv_kq lv_mm lv_at "
            "av_done o_copied osq osum oroot z_ready o_h rot_done rope_done kp_ready c1_done c1_ready c2_done c2_copied "
            "crot_done crope_done sc_done sm_ready s_ready e_done p_ready pt_done pt_copied pv_done o_n "
            "wo_done wo_copied x_new").split()}
        stored = sem("stored")

        a = Place()
        cv_n, cv_yt, cv_sq = a(DC, T), a(DC, T), a(DC, T)
        cv_csb, cv_z, cv_t = a(2, T), a(T + 2), a(T)
        a = Place()
        mo_n, mo_row = a(DC, TP), a(TT, D)
        mo_sq = a(DC, T)
        mo_xs, mo_st, mo_stw, mo_sw = a(DC, P), a(TT, 4, SLOT), a(TT, 4, SLOT), a(TP)
        mo_silu, mo_h, mo_ht, mo_y = a(2 * P), a(2 * P), a(2, P), a(D)
        mo_rank, mo_w, mo_a, mo_tmp = a(TT, NE), a(TT, NE), a(TT, NE), a(TT, NE)
        r8 = [a(TT, 8) for _ in range(10)]
        r1 = [a(TT) for _ in range(10)]
        r_c, r_gt, r_n = a(1), a(ROUNDS), a(1)
        a = Place()
        ml_kv, ml_q, ml_sq = a(DC, T), a(DC, T), a(DC, T)
        ml_ckv, ml_ckvn, ml_cq, ml_cqn = a(2, T), a(2, T), a(3, T), a(3, T)
        ml_kr, ml_rt = a(T), a(4, T)
        ml_kn, ml_v = a(HEADS, T), a(TT, D)
        ml_qn, ml_qr = a(HEADS, TP), a(HEADS, TP)
        a = Place()
        ml_s, ml_pt = [a(TT, T), a(TT, T)], a(2 * T)
        ml_st = [a(TT) for _ in range(6)]
        ml_o = a(HEADS, T)
        assert a.at <= 3 * DC * T
        a = Place()
        b_n, b_p, b_v = a(DC, SEQ), a(48, SEQ), a(6, 2, SEQ)
        over = a.at
        b_g, b_k, b_b, b_ke, b_qe = (a(HEADS, SEQ) for _ in range(5))
        under = a.at
        b_at = a(PAIRS, P)
        b_lb, b_lbi, b_lbt, b_bl, n_gate = a(2, 8), a(2, 8), a(2, 8), a(8), a(2, 24)
        b_d = hT[:, :, :].rearrange("p c t -> p (c t)")[:, 0:HEADS * SEQ]
        ax = VEC_AT["wr0"][0]
        b_ax = vecs[:, ax:ax + HEADS * P].rearrange("p (h t) -> p h t", h=HEADS)
        a = Place(over)
        n_kp = [a(32, 2, NCMP), a(32, 2, NCMP)]
        n_rt = a(12, SEQ)
        n_c1 = [a(2, NCMP), a(2, NCMP)]
        n_kc, n_vc, n_crt = a(2, NCMP), a(2, P), a(2, NCMP)
        n_st = [a(6) for _ in range(6)]
        n_s = [a(4 * SEQ + 2 * NCMP) for _ in range(2)]
        n_pt = [a(4 * SEQ) for _ in range(2)]
        assert a.at <= under, (a.at, under)

        def wide(v):
            return v.rearrange("p a b -> p (a b)")

        block = ctx.enter_context(nc.Block())

        @block.sync
        def _(sp):
            sp.dma_start(consts[:, :], consts_in).then_inc(const_in, 16)
            sp.dma_start(vecs[:, :], vecs_in).then_inc(const_in, 16)
            sp.dma_start(wide(hT[:, :, :]), h_in).then_inc(const_in, 16)
            free = [None] * RING
            n_dense = 0

            def load_dense(*uses):
                nonlocal n_dense
                for use in uses:
                    s = n_dense % RING
                    if free[s]:
                        sp.wait_ge(*free[s])
                    sp.dma_start(ring[:, s, :], dense[n_dense]).then_inc(landed[s], 16)
                    n_dense += 1
                    free[s] = use

            def load_experts(layer):
                m = moe_sem[layer]
                slots = [(n_dense + u) % RING for u in range(RING)]
                for u in range(RING):
                    if free[slots[u]]:
                        sp.wait_ge(*free[slots[u]])
                    sp.dma_start(ring[:, slots[u], :], experts[layer, 0, u]).then_inc(m[f"landed{u}"], 16)
                sp.wait_ge(m["iter_ready"], 1)
                n = sp.value_load(n_iter[0:1, layer:layer + 1], min_val=QUADS, max_val=QUADS * ROUNDS)
                with sp.Fori(0, n) as i:
                    for u in range(QU):
                        quad = i % QUADS if u < RING else (i + 1) % QUADS
                        sp.wait_ge(m["used"], i * QU + (u + 1))
                        sp.dma_start(ring[:, slots[u % RING], :], experts[layer, quad, (u + RING) % QU])\
                          .then_inc(m[f"landed{u % RING}"], 16)
                for u in range(RING):
                    sp.wait_ge(m[f"landed{u}"], n * 32 + 16)
                    free[slots[u]] = None

            load_dense(*[(cv_pe, 2 * u + 2) for u in range(12)])
            load_dense(*[(pr_done, 2 * u + 2) for u in range(4)])
            load_experts(0)
            load_dense(*[(ml["a_done"], u + 1) for u in range(3)])
            load_dense(*[(ml["pj_done"], n) for n in (8, 14, 19, 22, 30)])
            load_dense(*[(pr_done, 8 + 2 * u + 2) for u in range(4)])
            load_experts(1)
            for layer in range(2):
                load_dense(*[(b2["pj_done"], 60 * layer + 2 * u + 2) for u in range(30)])
                load_dense(*[(b2["c1_done"], 4 * layer + u + 1) for u in range(4)])
                load_dense(*[(b2["wo_done"], 12 * layer + 3 * (u // 2) + (1, 3)[u % 2]) for u in range(8)])
            sp.wait_ge(b2["x_new"], 2)
            sp.dma_start(out, wide(x2[:, :, :])).then_inc(stored, 16)
            sp.wait_ge(stored, 16)

        @block.tensor
        def _(pe):
            t = Turns(pe)
            n_unit, n_res, n_tile = 0, 0, 0

            def mm(o, lhsT, rhs, k, n):
                return pe.matmul(o, lhsT, rhs, start=(k == 0), stop=(k == n - 1))

            def unit(a, b):
                nonlocal n_unit
                s = n_unit % RING
                n_unit += 1
                pe.wait_ge(landed[s], 16 * ((n_unit - 1) // RING + 1))
                return ring[:, s, 0:a * b].rearrange("p (a b) -> p a b", a=a)

            def norm_sum(sq, n, w, bank):
                t.next(nrm_sq)
                for c in range(n):
                    m = mm(psum[:, bank, 0:w], C("ones"), sq[:, c, :], c, n)
                m.then_inc(nrm_sum, 1)

            def residual(src):
                nonlocal n_res
                for u in range(4):
                    w = unit(8, 256)
                    for half in range(2):
                        if n_res >= 2:
                            pe.wait_ge(pr_add, n_res - 1)
                        for k in range(8):
                            m = mm(psum[:, 6 + n_res % 2, 0:T], w[:, k, half * P:half * P + P], src[:, k, :], k, 8)
                        m.then_inc(pr_done, 1)
                        n_res += 1

            def conv():
                t.next(const_in, 48)
                norm_sum(cv_sq, DC, T, 7)
                t.next(nrm_out)
                for j in range(4):
                    for part in range(3):
                        w = unit(8, 256)
                        for half in range(2):
                            if j and part == 0:
                                pe.wait_ge(cv_y, 2 * (j - 1) + half + 1)
                            for k in range(8):
                                m = mm(psum[:, 3 * half + part, 0:T], w[:, k, half * P:half * P + P], cv_n[:, k, :], k, 8)
                            m.then_inc(cv_pe, 1)
                t.next(cv_y, 8)
                residual(cv_yt)

            def moe(layer):
                s = moe_sem[layer]
                slots = [(n_unit + u) % RING for u in range(RING)]
                norm_sum(mo_sq, DC, T, 7)
                t.next(nrm_out)
                wr = V(f"wr{layer}").rearrange("p (k n) -> p k n", k=8)
                for i in range(TT):
                    for k in range(8):
                        m = mm(psum[:, 0, i * 72:i * 72 + 72], mo_n[:, k, i * P:i * P + P], wr[:, k, :], k, 8)
                m.then_inc(s["lg_done"], 1)
                for i in range(TT):
                    for c in range(DC):
                        at = 512 + i * D + c * P
                        m = pe.transpose(flat[:, at:at + P], mo_n[:, c, i * P:i * P + P], C("ident"))
                m.then_inc(s["xr_done"], 1)
                pe.wait_ge(s["route_ready"], 1)
                for i in range(TT + 1):
                    n = min(i, TT - 1) + 1
                    for j in range(n):
                        m = mm(psum[:, 7, i * NE:i * NE + NE], C("upper") if j == i else C("ones"), mo_a[:, j, :], j, n)
                m.then_inc(s["rank_done"], 1)
                pe.wait_ge(s["xr_ready"], 1)

                def prep(n):
                    pe.wait_ge(s["st_ready"], n * 2)
                    for i in range(TT):
                        pe.transpose(psum[:, 2, i * P:i * P + P], wide(mo_stw[:, i]), C("ident"))
                    for c in range(DC):
                        for i in range(TT):
                            m = mm(flat[:, c * P:c * P + P], mo_row[:, i, c * P:c * P + P], wide(mo_st[:, i]), i, TT)
                    m.then_inc(s["prep_done"], 1)

                prep(1)
                pe.wait_ge(s["iter_ready"], 1)
                n = pe.value_load(n_iter[0:1, layer:layer + 1], min_val=QUADS, max_val=QUADS * ROUNDS)
                with pe.Fori(0, n) as i:
                    def weights(u):
                        pe.wait_ge(s[f"landed{u % RING}"], i * 32 + 16 * (u // RING + 1))
                        return ring[:, slots[u % RING], :].rearrange("p (e n) -> p e n", e=4)

                    pe.wait_ge(s["xs_ready"], i + 1)
                    for k in range(8):
                        w = weights(k)
                        for e in range(4):
                            m = pe.matmul(psum[32 * e:32 * e + 32, 3, :], mo_xs[:, k, 32 * e:32 * e + 32], w[:, e, :],
                                          start=(k == 0), stop=(k == 7), tile_position=(0, 32 * e))
                        m.then_inc(s["used"], 1)
                    pe.wait_ge(s["sw_ready"], i + 1)
                    prep(i + 2)
                    pe.wait_ge(s["h_ready"], i + 1)
                    for k in range(2):
                        m = pe.transpose(psum[:, 3, k * P:k * P + P], mo_h[:, k * P:k * P + P], C("ident"))
                    m.then_inc(s["ht_done"], 1)
                    pe.wait_ge(s["ht_ready"], i + 1)
                    for half in range(2):
                        for k in range(2):
                            w = weights(8 + 2 * half + k)
                            for e in range(4):
                                m = pe.matmul(psum[32 * e:32 * e + 32, 4 + half, :], mo_ht[:, k, 32 * e:32 * e + 32], w[:, e, :],
                                              start=(k == 0), stop=(k == 1), tile_position=(0, 32 * e))
                            m.then_inc(s["used"], 1)
                    pe.wait_ge(s["ya_ready"], i + 1)
                    pe.wait_ge(s["yd_ready"], i + 1)
                    for c in range(DC):
                        pe.wait_ge(s["add_done"], i * DC + (c if c >= 2 else 1))
                        pe.matmul(psum[:, 6 + c % 2, 0:T], mo_y[:, c * P:c * P + P], mo_sw[:, 0:T],
                                  start=True, stop=True).then_inc(s["cmb_done"], 1)

            def mla():
                norm_sum(ml_sq, DC, T, 7)
                t.next(nrm_out)
                w = unit(8, 256)
                for c in range(2):
                    for k in range(8):
                        m = mm(psum[:, c, 0:T], w[:, k, c * P:c * P + P], ml_kv[:, k, :], k, 8)
                m.then_inc(ml["a_done"], 1)
                w = unit(8, 192)
                for k in range(8):
                    mm(psum[0:64, 2, 0:T], w[:, k, 0:64], ml_kv[:, k, :], k, 8)
                for k in range(8):
                    m = mm(psum[:, 5, 0:T], w[:, k, 64:192], ml_q[:, k, :], k, 8)
                m.then_inc(ml["a_done"], 1)
                w = unit(8, 256)
                for c in range(2):
                    for k in range(8):
                        m = mm(psum[:, 3 + c, 0:T], w[:, k, c * P:c * P + P], ml_q[:, k, :], k, 8)
                m.then_inc(ml["a_done"], 1)
                norm_sum(ml_sq[:, 0:2], 2, T, 7)
                norm_sum(ml_sq[:, 2:5], 3, T, 6)
                mm(psum[0:64, 5, 0:T], C("rotm")[0:64, :], ml_kr[0:64, :], 0, 1).then_inc(ml["rot_done"], 1)
                n_out = 0

                def bank():
                    nonlocal n_out
                    if n_out >= 4:
                        pe.wait_ge(ml["pj_copied"], n_out - 3)
                    n_out += 1
                    return (n_out - 1) % 4

                t.next(nrm_out)
                w = unit(2, D)
                for h in range(HEADS):
                    b = bank()
                    for k in range(2):
                        m = mm(psum[:, b, 0:T], w[:, k, h * P:h * P + P], ml_ckvn[:, k, :], k, 2)
                    m.then_inc(ml["pj_done"], 1)
                w = unit(2, D)
                for i in range(TT):
                    n = min(P, T - i * P)
                    for half in range(2):
                        b = bank()
                        for k in range(2):
                            m = mm(psum[0:n, b, :], ml_ckvn[:, k, i * P:i * P + n], w[:, k, half * 512:half * 512 + 512], k, 2)
                        m.then_inc(ml["pj_done"], 1)
                t.next(nrm_out)
                for heads in (5, 3):
                    w = unit(3, heads * P)
                    for h in range(heads):
                        b = bank()
                        for k in range(3):
                            m = mm(psum[:, b, 0:T], w[:, k, h * P:h * P + P], ml_cqn[:, k, :], k, 3)
                        m.then_inc(ml["pj_done"], 1)
                w = unit(3, 512)
                for h in range(HEADS):
                    b = bank()
                    for k in range(3):
                        m = mm(psum[0:64, b, 0:T], w[:, k, h * 64:h * 64 + 64], ml_cqn[:, k, :], k, 3)
                    m.then_inc(ml["pj_done"], 1)
                t.next(ml["pj_copied"], 30)
                t.next(ml["rope_done"])
                for part in range(2):
                    for h in range(4):
                        m = mm(psum[0:64, 4 * (1 - part) + h, 0:T], C("rotm")[0:64, :], ml_qr[0:64, 4 * part + h, 0:T], 0, 1)
                    m.then_inc(ml["rot_done"], 1)
                t.next(ml["rope_done"], 2)

                def scores(h):
                    if h >= 2:
                        pe.wait_ge(ml["sm_ready"], h - 1)
                    for i in range(TT):
                        o = psum[:, 3 * (h % 2) + i, 0:T]
                        mm(o, ml_qn[:, h, i * P:i * P + P], ml_kn[:, h, :], 0, 2)
                        m = mm(o, ml_qr[0:64, h, i * P:i * P + P], ml_kr[0:64, :], 1, 2)
                    m.then_inc(ml["sc_done"], 1)

                scores(0)
                for h in range(HEADS):
                    if h + 1 < HEADS:
                        scores(h + 1)
                    pe.wait_ge(ml["p_ready"], h + 1)
                    for j in range(TT):
                        n = min(P, T - j * P)
                        for i in range(j, TT):
                            rows = min(P, T - i * P)
                            at = (0, T, 2 * T - P)[j] + (i - j) * P
                            m = pe.transpose(psum[0:n, 6, at:at + rows], ml_s[h % 2][0:rows, i, j * P:j * P + n],
                                             C("ident")[0:rows, 0:rows])
                    m.then_inc(ml["pt_done"], 1)
                    pe.wait_ge(ml["pt_copied"], 2 * h + 2)
                    if h:
                        pe.wait_ge(ml["o_ready"], h)
                    for j in range(TT):
                        n = min(P, T - j * P)
                        at = (0, T, 2 * T - P)[j]
                        m = mm(psum[:, 7, j * P:T], ml_v[0:n, j, h * P:h * P + P], ml_pt[0:n, at:at + T - j * P], j, TT)
                    m.then_inc(ml["pv_done"], 1)
                t.next(ml["o_ready"], HEADS)
                residual(ml_o)

            def layer2(layer):
                nonlocal n_tile
                norm_sum(b_qe, DC, SEQ, 7)
                t.next(nrm_out)

                def project(tokens_first):
                    nonlocal n_tile
                    w = unit(8, 256)
                    for half in range(2):
                        if n_tile >= 4:
                            pe.wait_ge(b2["pj_copied"], n_tile - 3)
                        cut = slice(half * P, half * P + P)
                        for k in range(8):
                            if tokens_first:
                                m = mm(psum[:, n_tile % 4, 0:SEQ], b_n[:, k, cut], w[:, k, :], k, 8)
                            else:
                                m = mm(psum[:, n_tile % 4, 0:SEQ], w[:, k, cut], b_n[:, k, :], k, 8)
                        m.then_inc(b2["pj_done"], 1)
                        n_tile += 1

                for kind, _ in UNITS_2[:12]:
                    project(kind == "v")
                wng = V(f"wng{layer}").rearrange("p (k n) -> p k n", k=8)
                for i in range(2):
                    for k in range(8):
                        m = mm(psum[:, 4, i * 24:i * 24 + 24], b_n[:, k, i * P:i * P + P], wng[:, k, :], k, 8)
                m.then_inc(b2["ng_done"], 1)
                t.next(b2["gate_ready"])
                for job in range(9):
                    for kind, _ in UNITS_2[12 + 2 * job:14 + 2 * job]:
                        project(kind == "v")
                    if job:
                        pe.wait_ge(b2["lv_at"], 9 * layer + job)
                    if job == 7:
                        t.next(b2["lv_kq"])
                        for h in range(HEADS):
                            m = mm(flat[:, 2048 + h * P:2048 + h * P + P], b_ke[:, h, 0:P], b_qe[:, h, P:SEQ], 0, 1)
                    else:
                        if job < 7:
                            t.next(b2["lv_kq"])
                        keys, queries = (b_ke, b_qe) if job < 7 else (b_k, b_p[:, F_Q:F_Q + HEADS])
                        for h in range(HEADS):
                            for i in range(2):
                                at = 2048 + (2 * h + i) * P
                                m = mm(flat[:, at:at + P], keys[:, h, i * P:i * P + P], queries[:, h, i * P:i * P + P], 0, 1)
                    m.then_inc(b2["lv_mm"], 1)
                t.next(b2["lv_at"], 9)
                t.next(b2["pj_copied"], 60)
                for h in range(HEADS):
                    v = [b_v[:, h // 2, i, (h % 2) * P:(h % 2) * P + P] for i in range(2)]
                    mm(flat[:, h * SEQ:h * SEQ + P], v[0], b_at[:, 2 * h, :], 0, 1)
                    mm(flat[:, h * SEQ + P:h * SEQ + SEQ], v[0], b_ax[:, h, :], 0, 2)
                    m = mm(flat[:, h * SEQ + P:h * SEQ + SEQ], v[1], b_at[:, 2 * h + 1, :], 1, 2)
                m.then_inc(b2["av_done"], 1)
                t.next(b2["osq"])
                for i in range(4):
                    m = mm(psum[:, 4 + i, :], C("ones"), b_d[:, i * 512:i * 512 + 512], 0, 1)
                m.then_inc(b2["osum"], 1)
                t.next(b2["oroot"])
                for i in range(6):
                    m = mm(psum[0:32, i, :], C("rotn")[0:32, :], wide(b_p[0:32, F_NQ + 2 * i:F_NQ + 2 * i + 2, :]), 0, 1)
                m.then_inc(b2["rot_done"], 1)
                for kv in range(2):
                    t.next(b2["kp_ready"])
                    for part in range(2):
                        w = unit(16, P)
                        for k in range(16):
                            m = mm(psum[:, 6 + kv, 0:2 * NCMP], w[:, k, :], wide(n_kp[kv][:, 16 * part + k]), 16 * part + k, 32)
                        m.then_inc(b2["c1_done"], 1)
                t.next(b2["c1_ready"], 2)
                mm(psum[:, 6, 64:64 + 2 * NCMP], V(f"w2k{layer}"), wide(n_c1[0]), 0, 1)
                for g in range(2):
                    m = mm(psum[0:NCMP, 7, 64 + g * P:64 + g * P + P], n_c1[1][:, g, :], V(f"w2v{layer}"), 0, 1)
                m.then_inc(b2["c2_done"], 1)
                t.next(b2["c2_copied"], 2)
                mm(psum[0:32, 6, 128:128 + 2 * NCMP], C("rotn")[0:32, :], wide(n_kc[0:32]), 0, 1).then_inc(b2["crot_done"], 1)
                t.next(b2["rope_done"])
                t.next(b2["crope_done"])

                def scores(h):
                    if h:
                        pe.wait_ge(b2["sm_ready"], HEADS * layer + h)
                    g = h // 4
                    for i in range(2):
                        q = b_p[:, F_NQ + h, i * P:i * P + P]
                        mm(psum[:, 0, i * SEQ:i * SEQ + SEQ], q, b_p[:, F_KS + g, :], 0, 1)
                        mm(psum[:, 1, i * SEQ:i * SEQ + SEQ], q, b_p[:, F_KW + g, :], 0, 1)
                        m = mm(psum[:, 2, i * NCMP:i * NCMP + NCMP], q, n_kc[:, g, :], 0, 1)
                    m.then_inc(b2["sc_done"], 1)

                scores(0)
                for h in range(HEADS):
                    if h + 1 < HEADS:
                        scores(h + 1)
                    g, n = h // 4, HEADS * layer + h
                    e, pt = n_s[h % 2], n_pt[h % 2]
                    pe.wait_ge(b2["p_ready"], n + 1)
                    if h:
                        pe.wait_ge(b2["pt_copied"], 3 * n)
                    for br in range(2):
                        for i in range(2):
                            at = br * 512 + i * SEQ
                            pe.transpose(psum[:, 3, br * SEQ + i * P:br * SEQ + i * P + P], e[:, at:at + P], C("ident"))
                        pe.transpose(psum[:, 4, br * P:br * P + P], e[:, br * 512 + 384:br * 512 + 512], C("ident"))
                    for i in range(2):
                        at = 4 * SEQ + i * NCMP
                        m = pe.transpose(psum[0:NCMP, 4, SEQ + i * P:SEQ + i * P + P], e[:, at:at + NCMP], C("ident"))
                    m.then_inc(b2["pt_done"], 1)
                    pe.wait_ge(b2["pt_copied"], 3 * n + 3)
                    if h:
                        pe.wait_ge(b2["o_n"], n)
                    o = psum[:, 5, 0:SEQ]
                    cut = slice(g * P, g * P + P)
                    mm(o, b_v[:, 4, 0, cut], pt[:, 0:SEQ], 0, 5)
                    mm(o, b_v[:, 5, 0, cut], pt[:, SEQ:2 * SEQ], 1, 5)
                    mm(o, n_vc[0:NCMP, g, :], pt[0:NCMP, 3 * SEQ:4 * SEQ], 2, 5)
                    mm(o[:, P:SEQ], b_v[:, 4, 1, cut], pt[:, 2 * SEQ:2 * SEQ + P], 3, 5)
                    mm(o[:, P:SEQ], b_v[:, 5, 1, cut], pt[:, 2 * SEQ + P:3 * SEQ], 4, 5).then_inc(b2["pv_done"], 1)
                t.next(b2["o_h"])
                t.next(b2["o_n"], HEADS)
                for j in range(4):
                    banks = (0, 1) if j % 2 else (6, 7)
                    if j >= 2:
                        pe.wait_ge(b2["wo_copied"], 8 * layer + 2 * (j - 1))
                    for part in range(2):
                        w = unit(8, 256)
                        for half in range(2):
                            for k in range(8):
                                m = mm(psum[:, banks[half], 0:SEQ], w[:, k, half * P:half * P + P],
                                       b_p[:, F_HZ + 8 * part + k, :], 8 * part + k, 16)
                            if part or half:
                                m.then_inc(b2["wo_done"], 1)
                norm_sum(b_qe, DC, SEQ, 5)

            conv()
            moe(0)
            mla()
            moe(1)
            norm_sum(b_qe, DC, SEQ, 0)
            layer2(0)
            layer2(1)

        @block.scalar
        def _(act):
            t = Chain(act, act_chain)

            def norm_root(n, w, bank):
                t.next(nrm_sum)
                act.activation(root[:, 0:w], psum[:, bank, 0:w], ACT.Sqrt, scale=1.0 / n, bias=eps[:, :]).then_inc(nrm_root, 1)

            def copy(o, i):
                return act.activation(o, i, ACT.Copy)

            def conv():
                t.next(const_in, 48)
                norm_root(D, T, 7)
                for j in range(4):
                    for half in range(2):
                        act.wait_ge(cv_pe, 6 * j + 3 + half)
                        copy(cv_csb[:, half, :], psum[:, 3 * half + 1, 0:T]).then_inc(cv_c, 1)

            def moe(layer):
                s = moe_sem[layer]
                norm_root(D, T, 7)
                act.wait_ge(s["xr_done"], 1)
                for i in range(TT):
                    m = copy(mo_row[:, i, :], flat[:, 512 + i * D:512 + i * D + D])
                m.then_inc(s["xr_ready"], 1)
                for n in range(2):
                    act.wait_ge(s["dg_ready"], n + 1)
                    act.activation(wide(r8[2 + 4 * n]), wide(r8[1 + 4 * n]), ACT.Exp).then_inc(s["exp_done"], 1)

                def tokens(n):
                    act.wait_ge(s["prep_done"], n)
                    copy(wide(mo_xs), flat[:, 0:D]).then_inc(s["xs_ready"], 1)

                tokens(1)
                copy(mo_sw[:, :], psum[:, 2, 0:TP]).then_inc(s["sw_ready"], 1)
                act.wait_ge(s["iter_ready"], 1)
                n = act.value_load(n_iter[0:1, layer:layer + 1], min_val=QUADS, max_val=QUADS * ROUNDS)
                with act.Fori(0, n) as i:
                    act.wait_ge(s["used"], i * QU + 8)
                    act.activation(mo_silu[:, :], psum[:, 3, 0:256], ACT.Silu).then_inc(s["silu_done"], 1)
                    tokens(i + 2)
                    act.wait_ge(s["used"], i * QU + 10)
                    copy(mo_y[:, 0:512], psum[:, 4, :]).then_inc(s["ya_ready"], 1)
                    act.wait_ge(s["cmb_done"], i * DC + DC)
                    copy(mo_sw[:, :], psum[:, 2, 0:TP]).then_inc(s["sw_ready"], 1)

            def mla():
                norm_root(D, T, 7)
                t.next(ml["a_done"], 3)
                for i in range(2):
                    copy(ml_ckv[:, i, :], psum[:, i, 0:T])
                copy(ml_kr[0:64, :], psum[0:64, 2, 0:T])
                for i in range(3):
                    m = copy(ml_cq[:, i, :], psum[:, 3 + i, 0:T])
                m.then_inc(ml["a_copied"], 1)
                norm_root(256, T, 7)
                act.wait_ge(nrm_out, 4)
                norm_root(384, T, 6)
                to = [(ml_kn[:, h, :], P, T) for h in range(HEADS)]
                to += [(ml_v[0:min(P, T - i * P), i, half * 512:half * 512 + 512], min(P, T - i * P), 512)
                       for i in range(TT) for half in range(2)]
                to += [(ml_qn[:, h, 0:T], P, T) for h in range(HEADS)]
                to += [(ml_qr[0:64, h, 0:T], 64, T) for h in range(HEADS)]
                for n, (o, rows, w) in enumerate(to):
                    t.next(ml["pj_done"])
                    copy(o, psum[0:rows, n % 4, 0:w]).then_inc(ml["pj_copied"], 1)
                for h in range(HEADS):
                    t.next(ml["s_ready"])
                    act.activation(wide(ml_s[h % 2]), wide(ml_s[h % 2]), ACT.Exp).then_inc(ml["e_done"], 1)
                    if h:
                        outputs(h - 1)
                outputs(HEADS - 1)

            def outputs(h):
                t.next(ml["pt_done"])
                copy(ml_pt[:, 0:2 * T - P], psum[:, 6, 0:2 * T - P]).then_inc(ml["pt_copied"], 1)
                n = T - 2 * P
                copy(ml_pt[0:n, 2 * T - P:2 * T - P + n], psum[0:n, 6, 2 * T - P:2 * T - P + n]).then_inc(ml["pt_copied"], 1)
                t.next(ml["pv_done"])
                copy(ml_o[:, h, :], psum[:, 7, 0:T]).then_inc(ml["o_ready"], 1)

            n_tile = 0

            def copy_tiles(units):
                nonlocal n_tile
                for kind, to in units:
                    for half in range(2):
                        t.next(b2["pj_done"])
                        o = b_v[:, to, half, :] if kind == "v" else b_p[:, to + half, :]
                        copy(o, psum[:, n_tile % 4, 0:SEQ]).then_inc(b2["pj_copied"], 1)
                        n_tile += 1

            def layer2(layer):
                norm_root(D, SEQ, 7)
                copy_tiles(UNITS_2[:4])
                t.next(b2["lin_ready"])
                f = wide(b_p[:, F_F:F_F + HEADS, :])
                act.wait_ge(b2["pj_copied"], 60 * layer + 8)
                act.activation(wide(b_g), f, ACT.Sigmoid)
                act.activation(wide(b_k), f, ACT.Sigmoid, scale=-1.0).then_inc(b2["sig_done"], 1)
                copy_tiles(UNITS_2[4:8])
                t.next(b2["lin_ready"])
                act.activation(wide(b_g), wide(b_g), ACT.Ln).then_inc(b2["ln_done"], 1)
                copy_tiles(UNITS_2[8:12])
                t.next(b2["ng_done"])
                act.activation(wide(n_gate), psum[:, 4, 0:48], ACT.Sigmoid).then_inc(b2["gate_ready"], 1)
                for job in range(9):
                    if job < 8:
                        t.next(b2["lv_d"])
                        t.link(act.activation(b_d, b_d, ACT.Abs))
                        act.activation(b_d, b_d, ACT.Exp, scale=-1.0).then_inc(b2["lv_e"], 1)
                    copy_tiles(UNITS_2[12 + 2 * job:14 + 2 * job])
                t.next(b2["av_done"])
                copy(wide(b_ke), flat[:, 0:2048]).then_inc(b2["o_copied"], 1)
                t.next(b2["osum"])
                t.link(act.activation(wide(b_qe), flat[:, 2048:4096], ACT.Ln, scale=1.0 / P, bias=eps[:, :]))
                act.activation(wide(b_qe), wide(b_qe), ACT.Exp, scale=-0.5).then_inc(b2["oroot"], 1)
                act.wait_ge(b2["pj_copied"], 60 * layer + 60)
                z = wide(b_p[:, F_HZ:F_HZ + 16, :])
                act.activation(z, z, ACT.Silu).then_inc(b2["z_ready"], 1)
                for kv in range(2):
                    t.next(b2["c1_done"], 2)
                    act.activation(wide(n_c1[kv]), psum[:, 6 + kv, 0:2 * NCMP], ACT.Silu,
                                   bias=V(f"b1{'kv'[kv]}{layer}")).then_inc(b2["c1_ready"], 1)
                t.next(b2["c2_done"])
                copy(wide(n_kc), psum[:, 6, 64:64 + 2 * NCMP]).then_inc(b2["c2_copied"], 1)
                copy(wide(n_vc[0:NCMP]), psum[0:NCMP, 7, 64:64 + 2 * P]).then_inc(b2["c2_copied"], 1)

                def probabilities(h):
                    t.next(b2["pt_done"])
                    pt = n_pt[h % 2]
                    copy(pt[:, 0:512], psum[:, 3, :]).then_inc(b2["pt_copied"], 1)
                    copy(pt[:, 512:768], psum[:, 4, 0:256]).then_inc(b2["pt_copied"], 1)
                    copy(pt[0:NCMP, 768:1024], psum[0:NCMP, 4, 256:512]).then_inc(b2["pt_copied"], 1)

                for h in range(HEADS):
                    t.next(b2["s_ready"])
                    act.activation(n_s[h % 2], n_s[h % 2], ACT.Exp).then_inc(b2["e_done"], 1)
                    if h:
                        probabilities(h - 1)
                probabilities(HEADS - 1)
                for j in range(4):
                    for half in range(2):
                        bank = ((6, 7), (0, 1))[j % 2][half]
                        act.wait_ge(b2["wo_done"], 12 * layer + 3 * j + 2 + half)
                        copy(b_p[:, 2 * j + half, :], psum[:, bank, 0:SEQ]).then_inc(b2["wo_copied"], 1)
                norm_root(D, SEQ, 5)

            conv()
            moe(0)
            mla()
            moe(1)
            norm_root(D, SEQ, 0)
            t.next(b2["lb_d"])
            act.activation(wide(b_lbt), wide(b_lbt), ACT.Exp).then_inc(b2["lb_e"], 1)
            layer2(0)
            layer2(1)

        @block.vector
        def _(v):
            t = Chain(v, dve_chain)

            def norm(x, n, w, sq, outs, first=None, last=nrm_out):
                t.link(v.tensor_tensor(sq, x, x, ALU.mult), nrm_sq)
                t.next(nrm_root)
                t.link(v.reciprocal(root[:, 0:w], root[:, 0:w]))
                for o, gain in outs:
                    for c in range(n):
                        m = v.scalar_tensor_tensor(o[:, c, 0:w], x[:, c, :], gain[:, c:c + 1], root[:, 0:w], ALU.mult, ALU.mult)
                t.link(m, last)

            def tt(o, a, b, op, sem=None):
                t.link(v.tensor_tensor(o, a, b, op), sem)

            def ts(o, a, s1, op1, s2=None, op2=None, sem=None):
                t.link(v.tensor_scalar(o, a, s1, s2, op1, op2) if op2 else v.tensor_scalar(o, a, s1, None, op1), sem)

            def stt(o, a, s, b, op1, op2, sem=None):
                t.link(v.scalar_tensor_tensor(o, a, s, b, op1, op2), sem)

            def red(o, a, op, sem=None):
                t.link(v.tensor_reduce(o, a, AX, op), sem)

            def rep(a, n):
                return a.unsqueeze(len(a.shape)).to_broadcast([*a.shape, n])

            def rep_mid(a, n):
                return a.unsqueeze(1).to_broadcast([a.shape[0], n, a.shape[1]])

            def residual():
                for c in range(DC):
                    t.next(pr_done)
                    tt(hT[:, c, :], hT[:, c, :], psum[:, 6 + c % 2, 0:T], ALU.add, pr_add)

            def conv():
                t.link(v.memset(eps[:, :], EPS))
                t.link(v.memset(cv_z[:, 0:2], 0.0))
                t.next(const_in, 48)
                norm(hT[:, :, :], DC, T, cv_sq, [(cv_n, V("mix0"))])
                cw = V("convw").rearrange("p (k c) -> p k c", k=3)
                for j in range(4):
                    for half in range(2):
                        c = 2 * j + half
                        t.next(cv_c)
                        v.wait_ge(cv_pe, 6 * j + 5 + half)
                        tt(cv_z[:, 2:T + 2], cv_csb[:, half, :], psum[:, 3 * half + 2, 0:T], ALU.mult)
                        ts(cv_t, cv_z[:, 0:T], cw[:, 0, c:c + 1], ALU.mult)
                        for k in range(1, 3):
                            stt(cv_t, cv_z[:, k:T + k], cw[:, k, c:c + 1], cv_t, ALU.mult, ALU.add)
                        tt(cv_yt[:, c, :], cv_t, psum[:, 3 * half, 0:T], ALU.mult, cv_y)
                residual()

            def moe(layer):
                s = moe_sem[layer]
                t.link(v.memset(mo_n[:, :, T:TP], 0.0))
                norm(hT[:, :, :], DC, T, mo_sq, [(mo_n, V(f"ffn{layer}"))])
                v.wait_ge(s["lg_done"], 1)
                lg = psum[:, 0, 0:TT * 72].rearrange("p (t n) -> p t n", t=TT)
                revidx = rep_mid(C("revidx"), TT)

                def first(oh, hit, i):
                    tt(r8[9], hit, revidx, ALU.mult)
                    red(r1[i], r8[9], ALU.max)
                    tt(oh, r8[9], rep(r1[i], 8), ALU.is_equal)

                gmax, gsum, pg = r1[0], r1[1], r1[2]
                red(gmax, lg[:, :, 0:8], ALU.max)
                tt(r8[1], lg[:, :, 0:8], rep(gmax, 8), ALU.subtract, s["dg_ready"])
                ts(r8[0], r8[1], 0.0, ALU.is_equal)
                grp = r8[3]
                first(grp, r8[0], 9)
                tt(grp, grp, rep(C("valid"), 8), ALU.mult)
                t.next(s["exp_done"])
                red(gsum, r8[2], ALU.add)
                t.link(v.reciprocal(pg, gsum))
                part = flat_tmp.rearrange("p (t g e) -> p t g e", t=TT, g=G)
                tt(part, lg[:, :, 8:72].rearrange("p t (g e) -> p t g e", g=G), rep(grp, 8), ALU.mult)
                red(r8[4], part.rearrange("p t g e -> p t e g"), ALU.add)
                red(r1[3], r8[4], ALU.max)
                tt(r8[5], r8[4], rep(r1[3], 8), ALU.subtract, s["dg_ready"])
                t.next(s["exp_done"])
                prob, one, two = r8[6], r8[7], r8[8]
                red(r1[4], prob, ALU.add)
                t.link(v.reciprocal(r1[4], r1[4]))
                tt(prob, prob, rep(r1[4], 8), ALU.mult)
                red(r1[5], prob, ALU.max)
                tt(r8[0], prob, rep(r1[5], 8), ALU.is_equal)
                first(one, r8[0], 9)
                stt(prob, one, -4.0, prob, ALU.mult, ALU.add)
                red(r1[6], prob, ALU.max)
                tt(r8[0], prob, rep(r1[6], 8), ALU.is_equal)
                first(two, r8[0], 9)
                tt(r1[7], r1[5], r1[6], ALU.add)
                t.link(v.reciprocal(r1[7], r1[7]))
                tt(r1[7], r1[7], pg, ALU.mult)
                tt(r1[5], r1[5], r1[7], ALU.mult)
                tt(r1[6], r1[6], r1[7], ALU.mult)
                tt(r8[0], one, two, ALU.add)
                tt(one, one, rep(r1[5], 8), ALU.mult)
                tt(two, two, rep(r1[6], 8), ALU.mult)
                tt(one, one, two, ALU.add)
                for o, src, signal in ((mo_w, one, None), (mo_a, r8[0], s["route_ready"])):
                    tt(o.rearrange("p t (g e) -> p t g e", g=G), rep(grp, 8),
                       src.unsqueeze(2).to_broadcast([P, TT, G, 8]), ALU.mult, signal)
                v.wait_ge(s["rank_done"], 1)
                rank = psum[:, 7, 0:TT * NE].rearrange("p (t n) -> p t n", t=TT)
                stt(mo_tmp, rank, 1.0, mo_a, ALU.add, ALU.mult)
                ts(mo_rank, mo_tmp, -1.0, ALU.add, sem=s["add_done"])
                red(r_c, psum[:, 7, TT * NE:TT * NE + NE], ALU.max)
                ts(r_gt, C("rounds"), r_c[:, 0:1], ALU.is_lt)
                red(r_n, r_gt, ALU.add)
                ts(r_n, r_n, float(QUADS), ALU.mult)
                t.link(v.tensor_copy(n_iter[:, layer:layer + 1], r_n), s["iter_ready"])

                def slots(quad4, base):
                    which = rep(mo_rank[:, :, bass.ds(quad4, 4)], SLOT)
                    place = C("iota")[:, bass.ds(base, SLOT)]
                    place = place.unsqueeze(1).unsqueeze(1).to_broadcast([P, TT, 4, SLOT])
                    v.tensor_tensor(mo_st, which, place, ALU.is_equal).then_inc(s["st_ready"], 1)

                def weighted(quad4, n):
                    v.wait_ge(s["st_ready"], n)
                    v.tensor_tensor(mo_stw, mo_st, rep(mo_w[:, :, bass.ds(quad4, 4)], SLOT), ALU.mult).then_inc(s["st_ready"], 1)

                slots(0, 0)
                weighted(0, 1)
                v.wait_ge(s["iter_ready"], 1)
                n = v.value_load(n_iter[0:1, layer:layer + 1], min_val=QUADS, max_val=QUADS * ROUNDS)
                with v.Fori(0, n) as i:
                    v.wait_ge(s["prep_done"], i + 1)
                    quad4, base = ((i + 1) % QUADS) * 4, ((i + 1) // QUADS) * SLOT
                    slots(quad4, base)
                    weighted(quad4, i * 2 + 3)
                    v.wait_ge(s["silu_done"], i + 1)
                    v.tensor_tensor(mo_h, mo_silu, psum[:, 3, 256:512], ALU.mult).then_inc(s["h_ready"], 1)
                    v.wait_ge(s["ht_done"], i + 1)
                    v.tensor_copy(wide(mo_ht), psum[:, 3, 0:256]).then_inc(s["ht_ready"], 1)
                    v.wait_ge(s["used"], i * QU + QU)
                    v.tensor_copy(mo_y[:, 512:1024], psum[:, 5, :]).then_inc(s["yd_ready"], 1)
                    v.wait_ge(s["add_done"], i * DC + 1)
                    for c in range(DC):
                        v.wait_ge(s["cmb_done"], i * DC + c + 1)
                        v.tensor_tensor(hT[:, c, :], hT[:, c, :], psum[:, 6 + c % 2, 0:T], ALU.add).then_inc(s["add_done"], 1)
                v.wait_ge(s["add_done"], n * DC + 1)

            def rope(x, rot, cos, sin, tmp, sem):
                tt(tmp, rot, sin, ALU.mult)
                tt(x, x, cos, ALU.mult)
                tt(x, x, tmp, ALU.add, sem)

            def mla():
                t.link(v.memset(ml_qn[:, :, T:TP], 0.0))
                t.link(v.memset(ml_qr[0:64, :, T:TP], 0.0))
                norm(hT[:, :, :], DC, T, ml_sq, [(ml_kv, V("kvg")), (ml_q, V("mix1"))])
                t.next(ml["a_copied"])
                t.link(v.tensor_tensor(ml_sq[:, 0:2], ml_ckv, ml_ckv, ALU.mult), nrm_sq)
                t.link(v.tensor_tensor(ml_sq[:, 2:5], ml_cq, ml_cq, ALU.mult), nrm_sq)
                for x, n, o, gain in ((ml_ckv, 2, ml_ckvn, V("ckvg")), (ml_cq, 3, ml_cqn, V("cqg"))):
                    t.next(nrm_root)
                    t.link(v.reciprocal(root[:, :], root[:, :]))
                    for c in range(n):
                        m = v.scalar_tensor_tensor(o[:, c, :], x[:, c, :], gain[:, c:c + 1], root[:, :], ALU.mult, ALU.mult)
                    t.link(m, nrm_out)
                cos, sin = C("cosm")[0:64, :], C("sinm")[0:64, :]
                t.next(ml["rot_done"])
                rope(ml_kr[0:64, :], psum[0:64, 5, 0:T], cos, sin, ml_rt[0:64, 0, :], ml["rope_done"])
                for part in range(2):
                    t.next(ml["rot_done"])
                    rope(ml_qr[0:64, 4 * part:4 * part + 4, 0:T], psum[0:64, 4 * (1 - part):4 * (1 - part) + 4, 0:T],
                         rep_mid(cos, 4), rep_mid(sin, 4), ml_rt[0:64], ml["rope_done"])
                mask = C("mask").rearrange("p (i k) -> p i k", i=TT)

                def front(h):
                    e, (mx, *_) = ml_s[h % 2], ml_st[3 * (h % 2):3 * (h % 2) + 3]
                    t.next(ml["sc_done"])
                    if h >= 2:
                        v.wait_ge(ml["pt_done"], h - 1)
                    stt(e, psum[:, 3 * (h % 2):3 * (h % 2) + 3, 0:T], MLA_SCALE, mask, ALU.mult, ALU.add, ml["sm_ready"])
                    red(mx, e, ALU.max)
                    tt(e, e, rep(mx, T), ALU.subtract, ml["s_ready"])

                front(0)
                for h in range(HEADS):
                    if h + 1 < HEADS:
                        front(h + 1)
                    e, (_, total, _) = ml_s[h % 2], ml_st[3 * (h % 2):3 * (h % 2) + 3]
                    t.next(ml["e_done"])
                    red(total, e, ALU.add)
                    t.link(v.reciprocal(total, total))
                    tt(e, e, rep(total, T), ALU.mult, ml["p_ready"])
                residual()

            def bounds():
                lg = V("lbl").rearrange("p (l c) -> p l c", l=2)
                tt(b_bl, lg[:, 0], lg[:, 1], ALU.max)
                tt(b_lbt, lg, rep_mid(b_bl, 2), ALU.subtract, b2["lb_d"])
                t.next(b2["lb_e"])
                tt(b_bl, b_lbt[:, 0], b_lbt[:, 1], ALU.add)
                t.link(v.reciprocal(b_bl, b_bl))
                tt(b_lbt, b_lbt, rep_mid(b_bl, 2), ALU.mult)
                tt(b_lb[:, 0], b_lbt[:, 0], b_lbt[:, 0], ALU.subtract)
                tt(b_lb[:, 1], b_lbt[:, 0], b_lbt[:, 1], ALU.add)
                tt(b_lb[:, 1], b_lb[:, 1], b_lbt[:, 0], ALU.subtract)
                ts(b_lb, b_lb, 0.0, ALU.max)
                ts(b_lbi, b_lb, -1.0, ALU.mult, 1.0, ALU.add)

            def layer2(layer):
                norm(x2[:, :, :], DC, SEQ, b_qe, [(b_n, V(f"pre{layer}"))])
                t.link(v.memset(wide(b_at), 0.0), b2["lin_ready"])
                t.next(b2["sig_done"])
                tt(b_g, b_g, rep(b_lbi[:, layer], SEQ), ALU.mult)
                tt(b_g, b_g, rep(b_lb[:, layer], SEQ), ALU.add)
                ts(b_g, b_g, LN_LEAST, ALU.max, sem=b2["lin_ready"])
                tt(b_k, b_k, rep(b_lbi[:, layer], SEQ), ALU.mult)
                t.next(b2["ln_done"])
                for h in range(HEADS):
                    m = v.tensor_tensor_scan(b_b[:, h, :], C("reset"), b_g[:, h, :], 0.0, ALU.mult, ALU.add)
                t.link(m)
                q = b_p[:, F_Q:F_Q + HEADS, :]
                v.wait_ge(b2["pj_copied"], 60 * layer + 16)
                masks = C("lev").rearrange("p (j t) -> p j t", j=7).bitcast(U32)

                def decay(job):
                    if job < len(LEVELS):
                        n = LEVELS[job]
                        x = wide(b_b).rearrange("p (k n) -> p k n", n=n)
                        ref = x[:, :, n // 2 - 1:n // 2].to_broadcast([P, HEADS * SEQ // n, n])
                        tt(b_d.rearrange("p (k n) -> p k n", n=n), x, ref, ALU.subtract, b2["lv_d"])
                        return
                    end = CHUNK - 1
                    if job == 6:
                        x = wide(b_b).rearrange("p (k c n) -> p k c n", c=2, n=CHUNK)
                        o = b_d.rearrange("p (k c n) -> p k c n", c=2, n=CHUNK)
                        tt(o[:, :, 0], x[:, :, 0], x[:, :, 0, end:].to_broadcast([P, PAIRS, CHUNK]), ALU.subtract)
                        t.link(v.tensor_copy(o[:, :, 1], x[:, :, 1]), b2["lv_d"])
                        return
                    x = wide(b_b).rearrange("p (h c n) -> p h c n", c=4, n=CHUNK)
                    o = b_d.rearrange("p (h c n) -> p h c n", c=4, n=CHUNK)
                    tt(b_bl, x[:, :, 0, end], x[:, :, 1, end], ALU.add)
                    tt(o[:, :, 0], x[:, :, 0], rep(b_bl, CHUNK), ALU.subtract)
                    tt(o[:, :, 1], x[:, :, 1], x[:, :, 1, end:].to_broadcast([P, HEADS, CHUNK]), ALU.subtract)
                    t.link(v.tensor_copy(o[:, :, 2], x[:, :, 2]))
                    tt(o[:, :, 3], x[:, :, 3], x[:, :, 2, end:].to_broadcast([P, HEADS, CHUNK]), ALU.add, b2["lv_d"])

                def gather(job):
                    t.next(b2["lv_mm"])
                    if job == 7:
                        t.link(v.tensor_copy(wide(b_ax), flat[:, 2048:2048 + HEADS * P]), b2["lv_at"])
                        return
                    mask = masks[:, job, :] if job < 7 else C("ident").bitcast(U32)
                    t.link(v.copy_predicated(b_at, rep_mid(mask, PAIRS),
                                             flat[:, 2048:4096].rearrange("p (k t) -> p k t", k=PAIRS)), b2["lv_at"])

                for job in range(9):
                    if job < 8:
                        decay(job)
                    if job:
                        gather(job - 1)
                    if job < 8:
                        t.next(b2["lv_e"])
                        e = b_d.rearrange("p (h n) -> p h n", h=HEADS)
                        cut = (slice(0, SEQ), slice(0, SEQ)) if job < 7 else (slice(0, P), slice(P, SEQ))
                        tt(b_ke[:, :, cut[0]], b_k[:, :, cut[0]], e[:, :, cut[0]], ALU.mult)
                        tt(b_qe[:, :, cut[1]], q[:, :, cut[1]], e[:, :, cut[1]], ALU.mult, b2["lv_kq"])
                gather(8)
                t.next(b2["o_copied"])
                tt(b_d, wide(b_ke), wide(b_ke), ALU.mult, b2["osq"])
                for kv, tile in ((0, F_KC), (1, F_VC)):
                    x = b_p[:, tile:tile + 2, :]
                    pos = V(f"pos{'kv'[kv]}{layer}").rearrange("p (l o) -> p l o", l=2)
                    for part in range(2):
                        src = x[:, :, 16 * part:16 * part + 16 * NCMP].rearrange("p g (n l) -> p l g n", l=16)
                        at = pos[:, part].unsqueeze(2).unsqueeze(3).to_broadcast([P, 16, 2, NCMP])
                        m = v.tensor_tensor(n_kp[kv][:, 16 * part:16 * part + 16], src, at, ALU.add)
                    t.link(m, b2["kp_ready"])
                t.next(b2["oroot"])
                stt(wide(b_ke), wide(b_ke), V(f"on{layer}"), wide(b_qe), ALU.mult, ALU.mult)
                t.next(b2["z_ready"])
                hz = b_p[:, F_HZ:F_HZ + HEADS, :]
                tt(hz, hz, b_ke, ALU.mult, b2["o_h"])
                t.next(b2["rot_done"])
                rope(b_p[0:32, F_NQ:F_NQ + 12, :], flat[0:32, 0:12 * SEQ].rearrange("p (k t) -> p k t", k=12),
                     rep_mid(C("cosn")[0:32, :], 12), rep_mid(C("sinn")[0:32, :], 12), n_rt[0:32], b2["rope_done"])
                t.next(b2["crot_done"])
                rope(n_kc[0:32], psum[0:32, 6, 128:128 + 2 * NCMP].rearrange("p (g n) -> p g n", g=2),
                     rep_mid(C("cosc")[0:32, :], 2), rep_mid(C("sinc")[0:32, :], 2), n_crt[0:32], b2["crope_done"])
                mask = C("mask").rearrange("p (i k) -> p i k", i=TT)[:, 0:2, 0:SEQ]
                long = 4 * SEQ

                def halves(h):
                    e = n_s[h % 2]
                    return (e[:, 0:long].rearrange("p (s k) -> p s k", s=4),
                            e[:, long:].rearrange("p (s k) -> p s k", s=2))

                def front(h):
                    el, ec = halves(h)
                    mx = n_st[3 * (h % 2)]
                    t.next(b2["sc_done"])
                    if h >= 2:
                        v.wait_ge(b2["pt_done"], HEADS * layer + h - 1)
                    for br in range(2):
                        stt(el[:, 2 * br:2 * br + 2], psum[:, br, :].rearrange("p (i k) -> p i k", i=2), NSA_SCALE, mask,
                            ALU.mult, ALU.add)
                    stt(wide(ec), psum[:, 2, 0:2 * NCMP], NSA_SCALE, C("cmask"), ALU.mult, ALU.add, b2["sm_ready"])
                    red(mx[:, 0:4], el, ALU.max)
                    red(mx[:, 4:6], ec, ALU.max)
                    tt(el, el, rep(mx[:, 0:4], SEQ), ALU.subtract)
                    tt(ec, ec, rep(mx[:, 4:6], NCMP), ALU.subtract, b2["s_ready"])

                def output(h):
                    t.next(b2["pv_done"])
                    tile = b_p[:, F_NZ + h, :]
                    tt(tile, tile, psum[:, 5, 0:SEQ], ALU.mult, b2["o_n"])

                front(0)
                for h in range(HEADS):
                    if h + 1 < HEADS:
                        front(h + 1)
                    el, ec = halves(h)
                    total = n_st[3 * (h % 2) + 1]
                    t.next(b2["e_done"])
                    tt(wide(ec), wide(ec), C("cvalid"), ALU.mult)
                    red(total[:, 0:4], el, ALU.add)
                    red(total[:, 4:6], ec, ALU.add)
                    ts(total, total, 1e-30, ALU.max)
                    t.link(v.reciprocal(total, total))
                    gate = n_gate[:, :, 3 * h:3 * h + 3].rearrange("p i b -> p b i")
                    tt(total[:, 0:4].rearrange("p (b i) -> p b i", b=2), total[:, 0:4].rearrange("p (b i) -> p b i", b=2),
                       gate[:, 1:3], ALU.mult)
                    tt(total[:, 4:6], total[:, 4:6], gate[:, 0], ALU.mult)
                    tt(ec, ec, rep(total[:, 4:6], NCMP), ALU.mult)
                    tt(el, el, rep(total[:, 0:4], SEQ), ALU.mult, b2["p_ready"])
                    if h:
                        output(h - 1)
                output(HEADS - 1)
                t.next(b2["wo_copied"], 8)
                y = b_p[:, 0:DC, :]
                norm(y, DC, SEQ, b_qe, [(y, V(f"post{layer}"))], last=None)
                tt(x2[:, :, :], x2[:, :, :], y, ALU.add, b2["x_new"])

            flat_tmp = wide(mo_tmp)
            conv()
            moe(0)
            mla()
            moe(1)
            norm(hT[:, :, META:T], DC, SEQ, b_qe, [(x2[:, :, :], V("fing"))], last=None)
            bounds()
            layer2(0)
            layer2(1)


def constants():
    import numpy as np

    f = np.float32
    p = np.arange(P)
    out = {}
    out["ident"] = np.eye(P)
    out["ones"] = np.ones((P, P))
    out["upper"] = np.triu(np.ones((P, P)), 1)
    out["iota"] = np.broadcast_to(np.arange((ROUNDS + 1) * SLOT), (P, (ROUNDS + 1) * SLOT))
    out["rounds"] = np.broadcast_to(np.arange(ROUNDS) * SLOT, (P, ROUNDS))
    out["revidx"] = np.broadcast_to(8 - np.arange(8), (P, 8))
    out["valid"] = (p[:, None] + P * np.arange(TT) < T)
    token = p[:, None] + P * np.arange(TT)
    out["mask"] = np.where(np.arange(T) <= token[:, :, None], 0.0, -1e30).reshape(P, -1)
    ended = 16 * np.arange(NCMP) + 31 <= token[:, :2, None]
    out["cmask"] = np.where(ended, 0.0, -1e30).reshape(P, -1)
    out["cvalid"] = ended.reshape(P, -1)
    out["reset"] = np.broadcast_to(np.arange(SEQ) % CHUNK != 0, (P, SEQ))
    levels = [(p[:, None] // n == p // n) & (p[:, None] % n < n // 2) & (p % n >= n // 2) for n in LEVELS + (P,)]
    out["lev"] = np.concatenate(levels, axis=1)

    def rotation(half):
        m = np.zeros((P, 2 * half))
        m[np.arange(half) + half, np.arange(half)] = -1
        m[np.arange(half), np.arange(half) + half] = 1
        return m

    def tables(theta, dim, at):
        inv = f(theta) ** (-np.arange(0, dim, 2, dtype=f) / f(dim))
        ang = (at.astype(f)[None, :] * inv[:, None]).astype(f)
        rows = np.zeros((2, P, len(at)))
        rows[0, :dim] = np.tile(np.cos(ang.astype(np.float64)), (2, 1))
        rows[1, :dim] = np.tile(np.sin(ang.astype(np.float64)), (2, 1))
        return rows

    out["cosm"], out["sinm"] = tables(10000.0, 64, np.arange(T))
    out["cosn"], out["sinn"] = tables(500000.0, 32, np.arange(SEQ))
    out["cosc"], out["sinc"] = tables(500000.0, 32, 16 * np.arange(NCMP) + 31)
    out["rotm"], out["rotn"] = rotation(32), rotation(16)
    return np.concatenate([np.asarray(out[k], f).reshape(P, n) for k, n in CONST.items()], axis=1)


def laid_out(x):
    import numpy as np

    x = {k: np.asarray(a) for k, a in x.items()}

    def columns(a):
        return a.reshape(-1, P).T

    def rows(a):
        return a.reshape(-1, P, a.shape[-1]).transpose(1, 0, 2).reshape(P, -1)

    def unit(a):
        a = rows(a)
        return np.pad(a, ((0, 0), (0, UNIT - a.shape[1])))

    v = {"convw": np.concatenate([columns(w) for w in x["conv_w"][0, :, 0]], axis=1),
         "kvg": columns(x["kv_norm_g"]), "ckvg": columns(x["ckv_norm_g"]), "cqg": columns(x["cq_norm_g"][0]),
         "fing": columns(x["final_norm_g"]),
         "lbl": np.concatenate([columns(a) for a in x["hgrn_lb_logits_2"]], axis=1)}
    for i in range(2):
        v[f"mix{i}"], v[f"ffn{i}"] = columns(x["norm_mix_g"][i]), columns(x["norm_ffn_g"][i])
        v[f"pre{i}"], v[f"post{i}"] = columns(x["pre_norm_2"][i]), columns(x["post_norm_2"][i])
        v[f"on{i}"] = columns(x["hgrn_out_norm_2"][i])
        for kv in "kv":
            v[f"b1{kv}{i}"] = columns(x[f"cmp_b1_{kv}_2"][i])
            v[f"pos{kv}{i}"] = x[f"cmp_pos_{kv}_2"][i].T
            v[f"w2{kv}{i}"] = x[f"cmp_w2_{kv}_2"][i]
        v[f"wng{i}"] = rows(x["w_in_2"][i][:, GATE_COLUMN:GATE_COLUMN + 24])
        v[f"wr{i}"] = rows(np.concatenate([x["w_grp"][i], x["w_exp"][i]], axis=1))
    vecs = np.concatenate([v[k].reshape(P, n) for k, n in VEC.items()], axis=1)

    w = x["conv_w_in"][0]
    dense = [unit(w[:, part * D + 256 * j:part * D + 256 * j + 256]) for j in range(4) for part in range(3)]
    dense += [unit(x["conv_w_out"][0][:, 256 * j:256 * j + 256]) for j in range(4)]
    dkv, dq = x["w_dkv"], x["w_dq"][0]
    dense += [unit(dkv[:, :256]), unit(np.concatenate([dkv[:, 256:], dq[:, 256:]], axis=1)), unit(dq[:, :256])]
    ukv = x["w_ukv"].reshape(256, HEADS, 256)
    dense += [unit(ukv[:, :, :P].reshape(256, -1)), unit(ukv[:, :, P:].reshape(256, -1))]
    uq = x["w_uq"][0].reshape(384, HEADS, 192)
    dense += [unit(uq[:, :5, :P].reshape(384, -1)), unit(uq[:, 5:, :P].reshape(384, -1)), unit(uq[:, :, P:].reshape(384, -1))]
    dense += [unit(x["w_o"][0][:, 256 * j:256 * j + 256]) for j in range(4)]
    for i in range(2):
        dense += [unit(x["w_in_2"][i][:, c:c + 256]) for c, _, _ in COLUMNS_2]
        for kv in "kv":
            w1 = x[f"cmp_w1_{kv}_2"][i]
            dense += [unit(w1[:D * 2]), unit(w1[D * 2:])]
        w = x["w_out_2"][i]
        dense += [unit(w[part * D:part * D + D, 256 * j:256 * j + 256]) for j in range(4) for part in range(2)]

    gate = x["w_gate"].reshape(2, QUADS, 4, 8, P, 256)
    up = x["w_up"].reshape(2, QUADS, 4, 8, P, 256)
    both = np.stack([gate, up], axis=5).transpose(0, 1, 3, 4, 2, 5, 6).reshape(2, QUADS, 8, P, UNIT)
    down = x["w_down"].reshape(2, QUADS, 4, 2, P, 2, 512).transpose(0, 1, 5, 3, 4, 2, 6).reshape(2, QUADS, 4, P, UNIT)
    h = np.concatenate([x["meta_tokens"], x["x"][0]], axis=0).T
    return {"h_in": rows(h), "consts_in": constants(), "vecs_in": vecs, "dense": np.stack(dense),
            "experts": np.concatenate([both, down], axis=2)}


def kernel(**inputs):
    import numpy as np
    import concourse.bacc as bacc
    from concourse.bass_utils import run_bass_kernel_spmd

    nc = bacc.Bacc("TRN2", target_bir_lowering=False, num_devices=1)
    arrays = {k: np.ascontiguousarray(a) for k, a in laid_out(inputs).items()}
    args = [nc.dram_tensor(k, a.shape, mybir.dt.from_np(a.dtype), kind="ExternalInput").ap() for k, a in arrays.items()]
    out = nc.dram_tensor("out_0", (P, DC * SEQ), F32, kind="ExternalOutput").ap()
    build(nc, *args, out)
    r = run_bass_kernel_spmd(nc, [arrays], core_ids=[0])
    return r.results[0]["out_0"].reshape(P, DC, SEQ).transpose(2, 1, 0).reshape(1, SEQ, D)
```

```python
from contextlib import ExitStack

import concourse.bass as bass
from concourse import mybir

F32 = mybir.dt.float32
F32R = mybir.dt.float32r
I32 = mybir.dt.int32
U32 = mybir.dt.uint32
ALU = mybir.AluOpType
ACT = mybir.ActivationFunctionType
AX = mybir.AxisListType.X

P = 128
D = 1024
DC = D // P
META = 16
SEQ = 256
T = META + SEQ
TT = 3
TP = TT * P
HEADS = 8
EPS = 1e-6
UNIT = 2048
RING = 6
PAIRS_OF_SLOTS = RING // 2
G = 8
EG = 8
NE = G * EG
QUADS = NE // 4
SLOT = 32
ROUNDS = -(-T // SLOT)
QU = 12
MLA_SCALE = 192.0 ** -0.5
NSA_SCALE = 128.0 ** -0.5
MASKED = -1e30
NCMP = 15
LEVELS = (64, 32, 16, 8, 4, 2)
CHUNK = 64
PAIRS = 2 * HEADS
LN_LEAST = 2.0 ** -63

CONV_UNITS = 16
MLA_UNITS = 12
L2_UNITS = 42
ARENA = 30440

F_F, F_Q, F_NQ, F_KS, F_KW, F_KC, F_VC, F_HZ, F_NZ = 0, 8, 16, 24, 26, 28, 30, 32, 40
SPLITS = dict(hq=1024, hf=1024, hi=1024, hz=1024, nq=1024, kc=256, vc=256, ks=256, vs=256, kw=256, vw=256, ng=24, nz=1024)


def units_2():
    at, first = 0, {}
    for k, n in SPLITS.items():
        first[k] = at
        at += n
    out = []
    for name, kind, to in (("hf", "f", F_F), ("hq", "f", F_Q), ("hi", "v", 0), ("kc", "f", F_KC), ("vc", "f", F_VC),
                           ("ks", "f", F_KS), ("kw", "f", F_KW), ("nq", "f", F_NQ), ("vs", "v", 4), ("vw", "v", 5),
                           ("nz", "f", F_NZ), ("hz", "f", F_HZ)):
        for u in range(SPLITS[name] // 256):
            out.append((first[name] + 256 * u, kind, to + u * (2 if kind == "f" else 1)))
    return out, first["ng"]


COLUMNS_2, GATE_COLUMN = units_2()
UNITS_2 = [(kind, to) for _, kind, to in COLUMNS_2]
U_HF, U_HI, U_KC, U_VC, U_KS, U_KW, U_NQ, U_VS, U_VW, U_NZ, U_HZ = 0, 8, 12, 13, 14, 15, 16, 20, 21, 22, 26
FIRST = [("unit", u) for u in range(U_KC)]
JOBS = [[("unit", U_KC), ("unit", U_VC)],
        [("unit", U_KS)],
        [("unit", U_KW), ("rot", U_KS)],
        [("c1", 0), ("unit", U_NQ), ("rot", U_KW)],
        [("c1", 1), ("unit", U_NQ + 1), ("rot", U_NQ)],
        [("unit", U_NQ + 2), ("rot", U_NQ + 1)],
        [("c2", 0), ("c2", 1), ("unit", U_NQ + 3), ("rot", U_NQ + 2)],
        [("unit", U_VS), ("crot", 0), ("rot", U_NQ + 3)],
        [("unit", U_VW)]]
BEFORE_HEADS = [("unit", U_NZ), ("unit", U_HZ)]
IN_HEADS = [("unit", u) for u in (U_NZ + 1, U_HZ + 1, U_NZ + 2, U_HZ + 2, U_HZ + 3, U_NZ + 3)]
GATED = {1: (0, 1), 3: (2, 3), 4: (4,), 5: (5,)}
HGRN_AT = {0: 0, 2: 1, 4: 2, 5: 3}
MAKES = FIRST + [m for job in JOBS for m in job] + BEFORE_HEADS + IN_HEADS


def tiles_2():
    at, out = 0, {}
    for what, n in MAKES:
        at += 2 if what == "unit" else 1
        out[what, n] = at
    return out, at


MADE, LAYER_TILES = tiles_2()


def fetched_2():
    at, out = 0, {}
    for what, n in MAKES:
        at += {"unit": 1, "c1": 2}.get(what, 0)
        out[what, n] = at
    return out, at


FETCHED, LAST_FETCHED = fetched_2()


def splits_2(layer):
    at = layer * L2_UNITS
    return [at + FETCHED[m] - 1 for m in MAKES if m[0] == "unit"] + [at + LAST_FETCHED + u for u in range(8)]


CONST = dict(ident=128, ones=128, upper=128, iota=(ROUNDS + 1) * SLOT, rounds=ROUNDS, revidx=8, valid=3,
             mask=P, cmask=2 * NCMP, cvalid=2 * NCMP, reset=SEQ, lev=7 * P,
             cosm=T, sinm=T, rotm=P, cosn=SEQ, sinn=SEQ, rotn=32, cosc=NCMP, sinc=NCMP)
VEC = dict(mix0=8, mix1=8, ffn0=8, ffn1=8, convw=24, kvg=8, ckvg=2, cqg=3, fing=8,
           pre0=8, pre1=8, post0=8, post1=8, lbl=16, on0=1, on1=1,
           b1k0=1, b1k1=1, b1v0=1, b1v1=1, posk0=32, posk1=32, posv0=32, posv1=32,
           w2k0=128, w2k1=128, w2v0=128, w2v1=128, wng0=192, wng1=192, wr0=576, wr1=576)


def offsets(table):
    at, out = 0, {}
    for k, n in table.items():
        out[k] = (at, n)
        at += n
    return out, at


CONST_AT, CONST_N = offsets(CONST)
VEC_AT, VEC_N = offsets(VEC)


class Turns:

    def __init__(self, eng):
        self.eng, self.seen = eng, {}

    def next(self, sem, k=1):
        self.seen[sem.name] = self.seen.get(sem.name, 0) + k
        self.eng.wait_ge(sem, self.seen[sem.name])


class Chain(Turns):

    def __init__(self, eng, sem):
        super().__init__(eng)
        self.sem = sem

    def link(self, ins, sem=None):
        sem = sem or self.sem
        ins.then_inc(sem, 1)
        self.next(sem)


def build(nc, h_in, consts_in, vecs_in, dense, experts, out):
    with ExitStack() as ctx:
        def sb(name, shape, dt=F32):
            return ctx.enter_context(nc.sbuf_tensor(name, shape, dt))

        def sem(name):
            return ctx.enter_context(nc.semaphore(name))

        def sb_both(name, shape, split=None):
            with nc.sbuf_tensor(name + "_parts", split or shape, F32R) as parts:
                pass
            return sb(name, shape), parts

        ring, ring_parts = sb_both("ring", [P, RING, UNIT])
        consts = sb("consts", [P, CONST_N])
        vecs, vecs_parts = sb_both("vecs", [P, VEC_N])
        hT = sb("hT", [P, DC, T])
        x2_flat = sb("x2", [P, DC * T])
        x2 = x2_flat[:, 0:DC * SEQ].rearrange("p (c t) -> p c t", c=DC)
        squares = x2_flat[:, :].rearrange("p (c t) -> p c t", c=DC)
        root = sb("root", [P, T])
        eps = sb("eps", [P, 1])
        n_iter = sb("n_iter", [P, 2], I32)
        wng_hi = sb("wng_hi", [P, VEC["wng0"]], F32R)
        n_last = sb("n_last", [P, 2], I32)
        arena, arena_parts = sb_both("arena", [P, ARENA], [P, (DC + 48 + 12) * SEQ])
        psum = ctx.enter_context(nc.psum_tensor("banks", [P, 8, 512], F32))
        flat = psum[:, :, :].rearrange("p b n -> p (b n)")

        def C(name):
            a, n = CONST_AT[name]
            return consts[:, a:a + n]

        def V(name, of=vecs):
            a, n = VEC_AT[name]
            return of[:, a:a + n]

        class Place:

            def __init__(self, at=0, of=None):
                self.at, self.of = at, arena if of is None else of

            def __call__(self, *shape):
                n = 1
                for k in shape:
                    n *= k
                v = self.of[:, self.at:self.at + n]
                self.at += n
                assert self.at <= ARENA, self.at
                if len(shape) == 2:
                    v = v.rearrange("p (a b) -> p a b", a=shape[0])
                if len(shape) == 3:
                    v = v.rearrange("p (a b c) -> p a b c", a=shape[0], b=shape[1])
                return v

        eps_set, tokens_in, const_in = sem("eps_set"), sem("tokens_in"), sem("const_in")
        landed = [sem(f"landed{s}") for s in range(RING)]
        nrm_sq, nrm_sum, nrm_root, nrm_out = (sem(n) for n in ("nrm_sq", "nrm_sum", "nrm_root", "nrm_out"))
        dve_chain, act_chain = sem("dve_chain"), sem("act_chain")
        cv_pe, cv_c, cv_y = sem("cv_pe"), sem("cv_c"), sem("cv_y")
        pr_done, pr_add = sem("pr_done"), sem("pr_add")
        MOE = ("landed0 landed1 landed2 landed3 landed4 landed5 used lg_done xr_done xr_ready dg_ready exp_done "
               "route_ready rank_done iter_ready st_ready stw_ready stw_done prep_done xs_ready sw_ready silu_done h_ready "
               "ht_done ht_ready dn_done ya_ready yd_ready cmb_done add_done").split()
        moe_sem = [{n: sem(f"m{layer}_{n}") for n in MOE} for layer in range(2)]
        ml = {n: sem(f"mla_{n}") for n in ("a_done a_copied kr_copied pj_done pj_copied krot_done kr_ready rot_done q_ready sc_done "
                                           "mx_ready e_done p_ready pt_done pt_copied pv_done o_ready").split()}
        b2 = {n: sem(f"b2_{n}") for n in (
            "lb_d lb_e pj_done pj_copied ng_done gate_ready sig_done lin_ready ln_done lv_d lv_e lv_kq lv_mm lv_at "
            "av_done o_copied osq osum oroot o_h rope_done kp_ready crope_done csc_done cs_ready ce_done c1_exp c1_ready z_ready "
            "sc_done mx_ready e_done p_ready pt_done pta_copied ptb_copied pv_done o_n "
            "wo_done wo_copied x_new landed0 landed1 landed2 g_hi w_hi w_ready n_new n_hi n_lo oh_hi oh_lo on_hi on_lo").split()}
        stored = sem("stored")

        a = Place()
        cv_n, cv_yt = a(DC, T), a(DC, T)
        cv_csb, cv_z, cv_t = a(2, T), a(T + 2), a(T)
        a = Place()
        mo_n, mo_row = a(DC, TP), a(TT, D)
        mo_xs, mo_st, mo_stw, mo_sw = a(DC, P), a(TT, 4, SLOT), a(TT, 4, SLOT), a(TP)
        mo_silu, mo_h, mo_ht, mo_y = a(2 * P), a(2 * P), a(2, P), a(D)
        mo_rank, mo_w, mo_a, mo_tmp = a(TT, NE), a(TT, NE), a(TT, NE), a(TT, NE)
        r8 = [a(TT, 8) for _ in range(10)]
        r1 = [a(TT) for _ in range(10)]
        r_c, r_gt, r_n = a(1), a(ROUNDS), a(1)
        a = Place()
        ml_kv, ml_q = a(DC, T), a(DC, T)
        ml_ckv, ml_ckvn, ml_cq, ml_cqn, ml_sq = a(2, T), a(2, T), a(3, T), a(3, T), a(5, T)
        ml_kr, ml_krz, ml_rt = a(T), a(2, T), a(4, T)
        ml_kn, ml_v, ml_qn = a(HEADS, T), a(TT, D), a(HEADS, T)
        ml_qr = a(HEADS // 2, T)
        ml_e, ml_pt = [a(3 * P + T), a(3 * P + T)], [a(2 * T), a(2 * T)]
        ml_st = [(a(TT), a(TT), a(TT)) for _ in range(2)]
        ml_o = a(HEADS, T)
        a = Place()
        b_at_0 = a.at
        b_n, b_p, b_v = a(DC, SEQ), a(48, SEQ), a(6, 2, SEQ)
        over = a.at
        b_g, b_k, b_b, b_ke, b_qe = (a(HEADS, SEQ) for _ in range(5))
        under = a.at
        b_at = a(PAIRS, P)
        b_lb, b_lbi, b_lbt, b_bl, n_gate = a(2, 8), a(2, 8), a(2, 8), a(8), a(2, 24)
        n_rt = a(2, SEQ)
        n_c1, n_ce = [a(2, NCMP), a(2, NCMP)], a(2, NCMP)
        b_d = hT[:, :, :].rearrange("p c t -> p (c t)")[:, 0:HEADS * SEQ]
        ax = VEC_AT["wr0"][0]
        b_ax = vecs[:, ax:ax + HEADS * P].rearrange("p (h t) -> p h t", h=HEADS)
        a = Place(b_at_0, arena_parts)
        n_parts, p_parts, v_parts = a(DC, SEQ), a(48, SEQ), a(12, SEQ)
        b_ns = [p_parts[:, F_F:F_F + DC, :], n_parts]
        b_ohs = [p_parts[:, F_Q:F_Q + HEADS, :], p_parts[:, F_HZ:F_HZ + HEADS, :]]
        b_ons = [v_parts[:, 0:HEADS, :], p_parts[:, F_NZ:F_NZ + HEADS, :]]
        a = Place(over)
        n_kp = [a(32, 2, NCMP), a(32, 2, NCMP)]
        assert a.at <= over + HEADS * SEQ
        a = Place(over)
        n_kc, n_vc, n_crt = a(2, NCMP), a(2, P), a(2, NCMP)
        a = Place(over + HEADS * SEQ)
        n_e = [a(2, 3 * P) for _ in range(2)]
        n_pt = [a(2, 4 * P) for _ in range(2)]
        n_st = [(a(4), a(4), a(4)) for _ in range(2)]
        n_cs, n_cmx, n_csum = a(2, HEADS * NCMP), a(2 * HEADS), a(2 * HEADS)
        assert a.at <= over + 3 * HEADS * SEQ

        def wide(v):
            return v.rearrange("p a b -> p (a b)")

        block = ctx.enter_context(nc.Block())

        @block.sync
        def _(sp):
            sp.dma_start(wide(hT[:, :, :]), h_in).then_inc(tokens_in, 16)
            sp.dma_start(consts[:, :], consts_in).then_inc(const_in, 16)
            sp.dma_start(vecs[:, :], vecs_in).then_inc(const_in, 16)
            free = [None] * RING
            n_dense = 0

            def load_dense(*uses):
                nonlocal n_dense
                for use in uses:
                    s = n_dense % RING
                    if free[s]:
                        sp.wait_ge(*free[s])
                    sp.dma_start(ring[:, s, :], dense[n_dense]).then_inc(landed[s], 16)
                    n_dense += 1
                    free[s] = use

            def load_experts(layer):
                m = moe_sem[layer]
                slots = [(n_dense + u) % RING for u in range(RING)]
                for u in range(RING):
                    if free[slots[u]]:
                        sp.wait_ge(*free[slots[u]])
                    sp.dma_start(ring[:, slots[u], :], experts[layer, 0, u]).then_inc(m[f"landed{u}"], 16)
                sp.wait_ge(m["iter_ready"], 1)
                last = sp.value_load(n_last[0:1, layer:layer + 1], min_val=QUADS - 1, max_val=QUADS * ROUNDS - 1)

                def load(i, u):
                    quad = i % QUADS if u < RING else (i + 1) % QUADS
                    sp.wait_ge(m["used"], i * QU + (u + 1))
                    sp.dma_start(ring[:, slots[u % RING], :], experts[layer, quad, (u + RING) % QU])\
                      .then_inc(m[f"landed{u % RING}"], 16)

                with sp.Fori(0, last) as i:
                    for u in range(QU):
                        load(i, u)
                for u in range(RING):
                    load(last, u)
                    free[slots[u]] = (m["used"], last * QU + (RING + u + 1))

            load_dense(*[(cv_pe, 2 * u + 2) for u in range(12)])
            load_dense(*[(pr_done, 2 * u + 2) for u in range(4)])
            load_experts(0)
            load_dense(*[(ml["a_done"], u + 1) for u in range(3)])
            load_dense(*[(ml["pj_done"], n) for n in (8, 14, 18, 23, 26)])
            load_dense(*[(pr_done, 8 + 2 * u + 2) for u in range(4)])
            load_experts(1)
            n_2 = 0

            def load_2(use):
                nonlocal n_2
                slot = n_2 % PAIRS_OF_SLOTS
                sp.wait_ge(*free[slot])
                sp.dma_start(ring[:, slot, :], dense[n_dense + n_2]).then_inc(b2[f"landed{slot}"], 16)
                n_2 += 1
                free[slot] = use

            for layer in range(2):
                for what, n in MAKES:
                    if what in ("unit", "c1"):
                        for _ in range(1 if what == "unit" else 2):
                            load_2((b2["pj_done"], LAYER_TILES * layer + MADE[what, n]))
                for u in range(8):
                    load_2((b2["wo_done"], 16 * layer + 2 * u + 2))
            for c in range(0, DC, 2):
                sp.wait_ge(b2["x_new"], 2 * DC + c + 2)
                sp.dma_start(out[:, c * SEQ:(c + 2) * SEQ], wide(x2[:, c:c + 2, :])).then_inc(stored, 16)
            sp.wait_ge(stored, 16 * DC // 2)

        @block.tensor
        def _(pe):
            t = Turns(pe)
            n_unit, n_res, n_tile, n_2, n_split = 0, 0, 0, 0, 0

            def mm(o, lhsT, rhs, k, n):
                return pe.matmul(o, lhsT, rhs, start=(k == 0), stop=(k == n - 1))

            def unit(a, b):
                nonlocal n_unit
                s = n_unit % RING
                n_unit += 1
                pe.wait_ge(landed[s], 16 * ((n_unit - 1) // RING + 1))
                return ring[:, s, 0:a * b].rearrange("p (a b) -> p a b", a=a)

            def mm3(o, lhsT, rhs, k, n):
                pe.matmul(o, lhsT[0], rhs[0], start=(k == 0), stop=False)
                pe.matmul(o, lhsT[0], rhs[1], start=False, stop=False)
                return pe.matmul(o, lhsT[1], rhs[0], start=False, stop=(k == n - 1))

            def unit_2(a, b):
                nonlocal n_2
                slot, n_2 = n_2 % PAIRS_OF_SLOTS, n_2 + 1
                pe.wait_ge(b2[f"landed{slot}"], 16 * ((n_2 - 1) // PAIRS_OF_SLOTS + 1))
                return ring[:, slot, 0:a * b].rearrange("p (a b) -> p a b", a=a)

            def split_unit():
                nonlocal n_2, n_split
                slot, n_2, n_split = n_2 % PAIRS_OF_SLOTS, n_2 + 1, n_split + 1
                pe.wait_ge(b2["w_ready"], n_split)
                return [ring_parts[:, x, :].rearrange("p (a b) -> p a b", a=8) for x in (PAIRS_OF_SLOTS + slot, slot)]

            def norm_sum(sq, n, w, bank):
                for c in range(n):
                    t.next(nrm_sq)
                    m = mm(psum[:, bank, 0:w], C("ones"), sq[:, c, :], c, n)
                m.then_inc(nrm_sum, 1)

            def normed(n):
                for _ in range(n):
                    t.next(nrm_out)
                    yield

            def residual(src):
                nonlocal n_res
                for u in range(4):
                    w = unit(8, 256)
                    for half in range(2):
                        if n_res >= 2:
                            pe.wait_ge(pr_add, n_res - 1)
                        for k in range(8):
                            m = mm(psum[:, 6 + n_res % 2, 0:T], w[:, k, half * P:half * P + P], src[:, k, :], k, 8)
                        m.then_inc(pr_done, 1)
                        n_res += 1

            def conv():
                t.next(const_in, 32)
                norm_sum(squares, DC, T, 7)
                ready = normed(DC)
                for j in range(4):
                    for part in range(3):
                        w = unit(8, 256)
                        for half in range(2):
                            if j and part == 0:
                                pe.wait_ge(cv_y, 2 * (j - 1) + half + 1)
                            for k in range(8):
                                next(ready, None)
                                m = mm(psum[:, 3 * half + part, 0:T], w[:, k, half * P:half * P + P], cv_n[:, k, :], k, 8)
                            m.then_inc(cv_pe, 1)
                t.next(cv_y, 8)
                residual(cv_yt)

            def moe(layer):
                s = moe_sem[layer]
                slots = [(n_unit + u) % RING for u in range(RING)]
                norm_sum(squares, DC, T, 5)
                ready = normed(DC)
                wr = V(f"wr{layer}").rearrange("p (k n) -> p k n", k=8)
                for i in range(TT):
                    for k in range(8):
                        next(ready, None)
                        m = mm(psum[:, 0, i * 72:i * 72 + 72], mo_n[:, k, i * P:i * P + P], wr[:, k, :], k, 8)
                m.then_inc(s["lg_done"], 1)
                for i in range(TT):
                    for c in range(DC):
                        at = 512 + i * D + c * P
                        m = pe.transpose(flat[:, at:at + P], mo_n[:, c, i * P:i * P + P], C("ident"))
                m.then_inc(s["xr_done"], 1)
                pe.wait_ge(s["route_ready"], 1)
                for i in range(TT + 1):
                    n = min(i, TT - 1) + 1
                    for j in range(n):
                        m = mm(psum[:, 7, i * NE:i * NE + NE], C("upper") if j == i else C("ones"), mo_a[:, j, :], j, n)
                m.then_inc(s["rank_done"], 1)
                pe.wait_ge(s["xr_ready"], 1)

                def prep(n):
                    pe.wait_ge(s["st_ready"], n)
                    for c in range(DC):
                        for i in range(TT):
                            m = mm(flat[:, c * P:c * P + P], mo_row[:, i, c * P:c * P + P], wide(mo_st[:, i]), i, TT)
                    m.then_inc(s["prep_done"], 1)

                def combine(i):
                    pe.wait_ge(s["ya_ready"], i + 1)
                    pe.wait_ge(s["yd_ready"], i + 1)
                    pe.wait_ge(s["sw_ready"], i + 1)
                    for c in range(DC):
                        pe.wait_ge(s["add_done"], i * DC + (c if c >= 2 else 1))
                        pe.matmul(psum[:, 6 + c % 2, 0:T], mo_y[:, c * P:c * P + P], mo_sw[:, 0:T],
                                  start=True, stop=True).then_inc(s["cmb_done"], 1)

                prep(1)
                pe.wait_ge(s["iter_ready"], 1)
                n = pe.value_load(n_iter[0:1, layer:layer + 1], min_val=QUADS, max_val=QUADS * ROUNDS)
                with pe.Fori(0, n) as i:
                    def weights(u):
                        pe.wait_ge(s[f"landed{u % RING}"], i * 32 + 16 * (u // RING + 1))
                        return ring[:, slots[u % RING], :].rearrange("p (e n) -> p e n", e=4)

                    pe.wait_ge(s["xs_ready"], i + 1)
                    for k in range(8):
                        w = weights(k)
                        for e in range(4):
                            m = pe.matmul(psum[32 * e:32 * e + 32, 3, :], mo_xs[:, k, 32 * e:32 * e + 32], w[:, e, :],
                                          start=(k == 0), stop=(k == 7), tile_position=(0, 32 * e))
                        m.then_inc(s["used"], 1)
                    prep(i + 2)
                    pe.wait_ge(s["h_ready"], i + 1)
                    for k in range(2):
                        m = pe.transpose(psum[:, 3, k * P:k * P + P], mo_h[:, k * P:k * P + P], C("ident"))
                    m.then_inc(s["ht_done"], 1)
                    combine(i)
                    pe.wait_ge(s["stw_ready"], i + 1)
                    for j in range(TT):
                        m = pe.transpose(psum[:, 2, j * P:j * P + P], wide(mo_stw[:, j]), C("ident"))
                    m.then_inc(s["stw_done"], 1)
                    pe.wait_ge(s["ht_ready"], i + 1)
                    for half in range(2):
                        for k in range(2):
                            w = weights(8 + 2 * half + k)
                            for e in range(4):
                                m = pe.matmul(psum[32 * e:32 * e + 32, 4 + half, :], mo_ht[:, k, 32 * e:32 * e + 32], w[:, e, :],
                                              start=(k == 0), stop=(k == 1), tile_position=(0, 32 * e))
                            m.then_inc(s["used"], 1)
                combine(n)

            def mla():
                norm_sum(squares, DC, T, 5)
                ready = normed(DC)
                w = unit(8, 256)
                for c in range(2):
                    for k in range(8):
                        next(ready, None)
                        m = mm(psum[:, c, 0:T], w[:, k, c * P:c * P + P], ml_kv[:, k, :], k, 8)
                m.then_inc(ml["a_done"], 1)
                ready = normed(DC)
                w = unit(8, 256)
                for c in range(2):
                    for k in range(8):
                        if c:
                            next(ready, None)
                        m = mm(psum[:, 2 + c, 0:T], w[:, k, c * P:c * P + P], (ml_kv, ml_q)[c][:, k, :], k, 8)
                m.then_inc(ml["a_done"], 1)
                norm_sum(ml_sq[:, 0:2], 2, T, 7)
                w = unit(8, 256)
                for c in range(2):
                    for k in range(8):
                        m = mm(psum[:, 4 + c, 0:T], w[:, k, c * P:c * P + P], ml_q[:, k, :], k, 8)
                m.then_inc(ml["a_done"], 1)
                t.next(ml["kr_copied"])
                mm(psum[:, 6, 0:T], C("rotm"), ml_kr, 0, 1).then_inc(ml["krot_done"], 1)
                n_out = 0

                def tile(n=4):
                    nonlocal n_out
                    if n_out >= n:
                        pe.wait_ge(ml["pj_copied"], n_out - n + 1)
                    n_out += 1
                    return 7 if n == 1 else (n_out - 1) % 4

                t.next(ml["a_copied"])
                ready = normed(2)
                w = unit(2, D)
                for h in range(HEADS):
                    b = tile()
                    for k in range(2):
                        next(ready, None)
                        m = mm(psum[:, b, 0:T], w[:, k, h * P:h * P + P], ml_ckvn[:, k, :], k, 2)
                    m.then_inc(ml["pj_done"], 1)
                norm_sum(ml_sq[:, 2:5], 3, T, 7)
                w = unit(2, D)
                for i in range(TT):
                    n = min(P, T - i * P)
                    for half in range(2):
                        b = tile()
                        for k in range(2):
                            m = mm(psum[0:n, b, :], ml_ckvn[:, k, i * P:i * P + n], w[:, k, half * 512:half * 512 + 512], k, 2)
                        m.then_inc(ml["pj_done"], 1)
                ready = normed(3)
                w = unit(3, 512)
                for h in range(HEADS // 2):
                    b = tile()
                    for k in range(3):
                        next(ready, None)
                        m = mm(psum[:, b, 0:T], w[:, k, h * P:h * P + P], ml_cqn[:, k, :], k, 3)
                    m.then_inc(ml["pj_done"], 1)
                heads = [(h, 5) for h in range(5)] + [(h, 3) for h in range(3)]

                def queries(h, n=4):
                    nonlocal w
                    at, of = heads[h]
                    if at == 0:
                        w = unit(3, of * P)
                    b = tile(n)
                    for k in range(3):
                        m = mm(psum[:, b, 0:T], w[:, k, at * P:at * P + P], ml_cqn[:, k, :], k, 3)
                    m.then_inc(ml["pj_done"], 1)

                queries(0)
                queries(1)
                t.next(ml["pj_copied"], 18)
                t.next(ml["kr_ready"])
                for h in range(HEADS // 2):
                    m = mm(psum[:, 4 + h, 0:T], C("rotm"), ml_qr[:, h, :], 0, 1)
                m.then_inc(ml["rot_done"], 1)
                queries(2)
                t.next(ml["pj_copied"], 3)
                t.next(ml["q_ready"])
                diagonal = C("mask")

                def scores(h):
                    if h >= 2:
                        pe.wait_ge(ml["e_done"], h - 1)
                        pe.wait_ge(ml["pj_copied"], 19 + h)
                    for i in range(TT):
                        n, keys = min(P, T - i * P), min(T, i * P + P)
                        b, at = 2 * (h % 2) + i // 2, (0, P, 0)[i]
                        o, q = psum[0:n, b, at:at + keys], slice(i * P, i * P + n)
                        mm(o, ml_qn[:, h, q], ml_kn[:, h, 0:keys], 0, 3)
                        mm(o, ml_qr[:, h // 2, q], ml_krz[:, h % 2, 0:keys], 1, 3)
                        m = pe.matmul(psum[0:n, b, at + i * P:at + i * P + n], C("ident")[:, 0:n], diagonal[:, 0:n],
                                      start=False, stop=True)
                    m.then_inc(ml["sc_done"], 1)

                scores(0)
                scores(1)
                for h in range(HEADS):
                    pe.wait_ge(ml["p_ready"], h + 1)
                    for j in range(TT):
                        n = min(P, T - j * P)
                        for i in range(j, TT):
                            rows = min(P, T - i * P)
                            at = (0, T, 2 * T - P)[j] + (i - j) * P
                            e = (0, P, 3 * P)[i] + j * P
                            m = pe.transpose(psum[0:n, 4 + h % 2, at:at + rows], ml_e[h % 2][0:rows, e:e + n],
                                             C("ident")[0:rows, 0:rows])
                    m.then_inc(ml["pt_done"], 1)
                    if h + 3 < HEADS:
                        queries(h + 3, 1)
                    if h + 2 < HEADS:
                        scores(h + 2)
                    pe.wait_ge(ml["pt_copied"], 2 * h + 2)
                    if h:
                        pe.wait_ge(ml["o_ready"], h)
                    for j in range(TT):
                        n = min(P, T - j * P)
                        at = (0, T, 2 * T - P)[j]
                        m = mm(psum[:, 6, j * P:T], ml_v[0:n, j, h * P:h * P + P], ml_pt[h % 2][0:n, at:at + T - j * P], j, TT)
                    m.then_inc(ml["pv_done"], 1)
                t.next(ml["o_ready"], HEADS)
                residual(ml_o)

            def layer2(layer):
                nonlocal n_tile
                first_tile = n_tile
                norm_sum(b_qe, DC, SEQ, 7)
                fresh = [True] * DC
                w = None

                def both(views, index):
                    return [x[index] for x in views]

                def normed_2(k):
                    if fresh[k]:
                        t.next(b2["n_lo"])
                        fresh[k] = False

                def bank(only=None):
                    nonlocal n_tile
                    n_tile += 1
                    if only is None:
                        if n_tile > 4:
                            pe.wait_ge(b2["pj_copied"], n_tile - 4)
                        return (n_tile - 1 - first_tile) % 4
                    pe.wait_ge(b2["pj_copied"], n_tile - 1)
                    return only

                def tile(u, half, only=None):
                    nonlocal w
                    if half == 0:
                        w = split_unit()
                    o = psum[:, bank(only), 0:SEQ]
                    cut = slice(half * P, half * P + P)
                    for k in range(8):
                        normed_2(k)
                        every = (slice(None), k, slice(None))
                        if UNITS_2[u][0] == "v":
                            m = mm3(o, both(b_ns, (slice(None), k, cut)), both(w, every), k, 8)
                        else:
                            m = mm3(o, both(w, (slice(None), k, cut)), both(b_ns, every), k, 8)
                    m.then_inc(b2["pj_done"], 1)

                def make(what, n):
                    if what == "unit":
                        tile(n, 0)
                        tile(n, 1)
                        return
                    if what == "rot":
                        pe.wait_ge(b2["pj_copied"], first_tile + MADE["unit", n])
                        src = b_p[0:32, UNITS_2[n][1]:UNITS_2[n][1] + 2, :]
                        m = mm(psum[0:32, bank(), :], C("rotn")[0:32, :], wide(src), 0, 1)
                    if what == "c1":
                        o = psum[:, bank(), 0:2 * NCMP]
                        t.next(b2["kp_ready"])
                        for part in range(2):
                            v = unit_2(16, P)
                            for k in range(16):
                                m = mm(o, v[:, k, :], wide(n_kp[n][:, 16 * part + k]), 16 * part + k, 32)
                    if what == "c2":
                        o = psum[:, bank(), :]
                        t.next(b2["c1_ready"])
                        if n == 0:
                            m = mm(o[:, 0:2 * NCMP], V(f"w2k{layer}"), wide(n_c1[0]), 0, 1)
                        else:
                            for g in range(2):
                                m = mm(o[0:NCMP, g * P:g * P + P], n_c1[1][:, g, :], V(f"w2v{layer}"), 0, 1)
                    if what == "crot":
                        o = psum[0:32, bank(), 0:2 * NCMP]
                        pe.wait_ge(b2["pj_copied"], first_tile + MADE["c2", 0])
                        m = mm(o, C("rotn")[0:32, :], wide(n_kc[0:32]), 0, 1)
                    m.then_inc(b2["pj_done"], 1)

                for m in FIRST:
                    make(*m)
                wng = [x.rearrange("p (k n) -> p k n", k=8) for x in (wng_hi[:, :], V(f"wng{layer}", vecs_parts))]
                for i in range(2):
                    for k in range(8):
                        m = mm3(psum[:, 4, i * 24:i * 24 + 24], both(b_ns, (slice(None), k, slice(i * P, i * P + P))),
                                both(wng, (slice(None), k, slice(None))), k, 8)
                m.then_inc(b2["ng_done"], 1)
                t.next(b2["gate_ready"])
                for job in range(9):
                    for m in JOBS[job]:
                        make(*m)
                    for part in range(2):
                        heads = range(4 * part, 4 * part + 4)
                        if job:
                            pe.wait_ge(b2["lv_at"], 18 * layer + 2 * job - (part == 0 and job < 8))
                        if job < 8:
                            t.next(b2["lv_kq"])
                        keys, queries = (b_ke, b_qe) if job < 8 else (b_k, b_p[:, F_Q:F_Q + HEADS])
                        for h in heads:
                            if job == 7:
                                m = mm(flat[:, 2048 + h * P:2048 + h * P + P], b_ke[:, h, 0:P], b_qe[:, h, P:SEQ], 0, 1)
                                continue
                            for i in range(2):
                                at = 2048 + (2 * h + i) * P
                                m = mm(flat[:, at:at + P], keys[:, h, i * P:i * P + P], queries[:, h, i * P:i * P + P], 0, 1)
                        m.then_inc(b2["lv_mm"], 1)
                make(*BEFORE_HEADS[0])
                t.next(b2["lv_at"], 18)
                for h in range(HEADS):
                    v = [b_v[:, h // 2, i, (h % 2) * P:(h % 2) * P + P] for i in range(2)]
                    at = 2048 + h * SEQ
                    mm(flat[:, at:at + P], v[0], b_at[:, 2 * h, :], 0, 1)
                    mm(flat[:, at + P:at + SEQ], v[0], b_ax[:, h, :], 0, 2)
                    m = mm(flat[:, at + P:at + SEQ], v[1], b_at[:, 2 * h + 1, :], 1, 2)
                m.then_inc(b2["av_done"], 1)
                make(*BEFORE_HEADS[1])
                t.next(b2["osq"])
                for i in range(4):
                    m = mm(psum[:, 4 + i, :], C("ones"), b_d[:, i * 512:i * 512 + 512], 0, 1)
                m.then_inc(b2["osum"], 1)

                def scores(h):
                    if h >= 2:
                        pe.wait_ge(b2["e_done"], HEADS * layer + h - 1)
                    for br, keys in ((0, F_KS), (1, F_KW)):
                        k = b_p[:, keys + h // 4, :]
                        for i, at, n in ((0, 0, P), (1, P, SEQ)):
                            b = 2 * (h % 2) + br
                            mm(psum[:, b, at:at + n], b_p[:, F_NQ + h, i * P:i * P + P], k[:, 0:n], 0, 2)
                            m = pe.matmul(psum[:, b, at + n - P:at + n], C("ident"), C("mask"), start=False, stop=True)
                    m.then_inc(b2["sc_done"], 1)

                t.next(b2["rope_done"], 6)
                pe.wait_ge(b2["pj_copied"], n_tile)
                scores(0)
                scores(1)
                t.next(b2["crope_done"])
                t.next(b2["oroot"])
                for i in range(2):
                    for h in range(HEADS):
                        at = (i * HEADS + h) * NCMP
                        m = mm(psum[:, 6, at:at + NCMP], b_p[:, F_NQ + h, i * P:i * P + P], n_kc[:, h // 4, :], 0, 1)
                m.then_inc(b2["csc_done"], 1)

                def part_out(u, half, source, b):
                    nonlocal w
                    if half == 0:
                        w = split_unit()
                    for k in range(8):
                        if source and u == half == 0:
                            t.next(b2["on_lo"])
                        m = mm3(psum[:, b, 0:SEQ], both(w, (slice(None), k, slice(half * P, half * P + P))),
                                both((b_ohs, b_ons)[source], (slice(None), k, slice(None))), 8 * source + k, 16)
                    m.then_inc(b2["wo_done"], 1)

                def beside(h, half):
                    if h < len(IN_HEADS):
                        tile(IN_HEADS[h][1], half, 7)
                    elif half:
                        if h == len(IN_HEADS):
                            t.next(b2["oh_lo"], 4)
                        u = h - len(IN_HEADS)
                        part_out(u, 0, 0, 2 * u)
                        part_out(u, 1, 0, 2 * u + 1)

                for h in range(HEADS):
                    g, n = h // 4, HEADS * layer + h
                    e, pt = n_e[h % 2], n_pt[h % 2]
                    beside(h, 0)
                    pe.wait_ge(b2["p_ready"], n + 1)
                    for br in range(2):
                        b = 4 + br
                        pe.transpose(psum[:, b, 0:P], e[:, br, 0:P], C("ident"))
                        pe.transpose(psum[:, b, P:2 * P], e[:, br, P:2 * P], C("ident"))
                        pe.transpose(psum[:, b, 2 * P:3 * P], e[:, br, 2 * P:3 * P], C("ident"))
                        m = pe.transpose(psum[0:NCMP, b, 3 * P:4 * P], n_cs[:, br, h * NCMP:h * NCMP + NCMP], C("ident"))
                    m.then_inc(b2["pt_done"], 1)
                    if h + 2 < HEADS:
                        scores(h + 2)
                    beside(h, 1)
                    pe.wait_ge(b2["pta_copied"], 2 * n + 2)
                    pe.wait_ge(b2["ptb_copied"], 2 * n + 2)
                    if h:
                        pe.wait_ge(b2["o_n"], n)
                    o = psum[:, 6, 0:SEQ]
                    cut = slice(g * P, g * P + P)
                    mm(o, b_v[:, 4, 0, cut], pt[:, 0, 0:SEQ], 0, 6)
                    mm(o, b_v[:, 5, 0, cut], pt[:, 1, 0:SEQ], 1, 6)
                    mm(o[:, P:SEQ], b_v[:, 4, 1, cut], pt[:, 0, SEQ:SEQ + P], 2, 6)
                    mm(o[:, P:SEQ], b_v[:, 5, 1, cut], pt[:, 1, SEQ:SEQ + P], 3, 6)
                    for i in range(2):
                        m = mm(o[:, i * P:i * P + P], n_vc[0:NCMP, g, :], pt[0:NCMP, i, 3 * P:4 * P], 4 + i, 6)
                    m.then_inc(b2["pv_done"], 1)
                for u in range(2, 4):
                    if u == 3:
                        t.next(b2["o_n"], HEADS)
                        pe.wait_ge(b2["pj_copied"], n_tile)
                    part_out(u, 0, 0, 2 * u)
                    part_out(u, 1, 0, 2 * u + 1)
                for u in range(4):
                    part_out(u, 0, 1, 2 * u)
                    part_out(u, 1, 1, 2 * u + 1)
                pe.wait_ge(b2["wo_copied"], DC * layer + 1)
                norm_sum(b_qe, DC, SEQ, 0)

            conv()
            moe(0)
            mla()
            moe(1)
            norm_sum(squares[:, :, 0:SEQ], DC, SEQ, 0)
            layer2(0)
            layer2(1)

        @block.scalar
        def _(act):
            t = Chain(act, act_chain)

            def square(o, i):
                act.activation(o, i, ACT.Square).then_inc(nrm_sq, 1)

            def norm_root(n, w, bank):
                t.next(nrm_sum)
                act.activation(root[:, 0:w], psum[:, bank, 0:w], ACT.Sqrt, scale=1.0 / n, bias=eps[:, :]).then_inc(nrm_root, 1)

            def copy(o, i):
                return act.activation(o, i, ACT.Copy)

            def conv():
                t.next(tokens_in, 16)
                for c in range(DC):
                    square(squares[:, c, :], hT[:, c, :])
                t.next(eps_set)
                norm_root(D, T, 7)
                for j in range(4):
                    for half in range(2):
                        act.wait_ge(cv_pe, 6 * j + 3 + half)
                        copy(cv_csb[:, half, :], psum[:, 3 * half + 1, 0:T]).then_inc(cv_c, 1)

            def moe(layer):
                s = moe_sem[layer]
                for c in range(DC):
                    t.next(pr_add)
                    square(squares[:, c, :], hT[:, c, :])
                norm_root(D, T, 5)
                act.wait_ge(s["xr_done"], 1)
                for i in range(TT):
                    m = copy(mo_row[:, i, :], flat[:, 512 + i * D:512 + i * D + D])
                m.then_inc(s["xr_ready"], 1)
                for n in range(2):
                    act.wait_ge(s["dg_ready"], n + 1)
                    act.activation(wide(r8[2 + 4 * n]), wide(r8[1 + 4 * n]), ACT.Exp).then_inc(s["exp_done"], 1)

                def tokens(n):
                    act.wait_ge(s["prep_done"], n)
                    copy(wide(mo_xs), flat[:, 0:D]).then_inc(s["xs_ready"], 1)

                tokens(1)
                act.wait_ge(s["iter_ready"], 1)
                n = act.value_load(n_iter[0:1, layer:layer + 1], min_val=QUADS, max_val=QUADS * ROUNDS)
                with act.Fori(0, n) as i:
                    act.wait_ge(s["used"], i * QU + 8)
                    act.activation(mo_silu[:, :], psum[:, 3, 0:256], ACT.Silu).then_inc(s["silu_done"], 1)
                    tokens(i + 2)
                    act.wait_ge(s["stw_done"], i + 2)
                    copy(mo_sw[:, :], psum[:, 2, 0:TP]).then_inc(s["sw_ready"], 1)
                    act.wait_ge(s["used"], i * QU + 10)
                    copy(mo_y[:, 0:512], psum[:, 4, :]).then_inc(s["ya_ready"], 1)

                for c in range(DC):
                    act.wait_ge(s["add_done"], n * DC + (c + 2))
                    if layer:
                        square(squares[:, c, 0:SEQ], hT[:, c, META:T])
                    else:
                        square(squares[:, c, :], hT[:, c, :])

            def mla():
                norm_root(D, T, 5)
                t.next(ml["a_done"])
                for i in range(2):
                    copy(ml_ckv[:, i, :], psum[:, i, 0:T])
                    square(ml_sq[:, i, :], psum[:, i, 0:T])
                t.next(ml["a_done"])
                copy(ml_kr[:, :], psum[:, 2, 0:T]).then_inc(ml["kr_copied"], 1)
                copy(ml_cq[:, 2, :], psum[:, 3, 0:T]).then_inc(ml["a_copied"], 1)
                act.wait_ge(nrm_out, 4 * DC)
                norm_root(256, T, 7)
                t.next(ml["a_copied"])
                t.next(ml["a_done"])
                for i in range(2):
                    copy(ml_cq[:, i, :], psum[:, 4 + i, 0:T])
                    square(ml_sq[:, 2 + i, :], psum[:, 4 + i, 0:T])
                square(ml_sq[:, 4, :], ml_cq[:, 2, :])
                to = [(ml_kn[:, h, :], P, T) for h in range(HEADS)]
                to += [(ml_v[0:min(P, T - i * P), i, half * 512:half * 512 + 512], min(P, T - i * P), 512)
                       for i in range(TT) for half in range(2)]
                to += [(ml_qr[:, h, :], P, T) for h in range(HEADS // 2)]
                to += [(ml_qn[:, h, :], P, T) for h in range(HEADS)]
                n_out = 0

                def copy_next(only=None):
                    nonlocal n_out
                    o, rows, w = to[n_out]
                    t.next(ml["pj_done"])
                    copy(o, psum[0:rows, n_out % 4 if only is None else only, 0:w]).then_inc(ml["pj_copied"], 1)
                    n_out += 1

                def exps(h):
                    _, least, total = ml_st[h % 2]
                    t.next(ml["mx_ready"])
                    for i in range(TT):
                        n, keys = min(P, T - i * P), min(T, i * P + P)
                        b, at, to_ = 2 * (h % 2) + i // 2, (0, P, 0)[i], (0, P, 3 * P)[i]
                        m = act.activation(ml_e[h % 2][0:n, to_:to_ + keys], psum[0:n, b, at:at + keys], ACT.Exp,
                                           scale=MLA_SCALE, bias=least[0:n, i:i + 1], accum_out=total[0:n, i:i + 1])
                    m.then_inc(ml["e_done"], 1)

                for k in range(21):
                    if k == HEADS:
                        act.wait_ge(nrm_out, 4 * DC + 2)
                        norm_root(384, T, 7)
                    copy_next()
                exps(0)
                exps(1)
                for h in range(HEADS):
                    t.next(ml["pt_done"])
                    pt, b = ml_pt[h % 2], 4 + h % 2
                    copy(pt[:, 0:2 * T - P], psum[:, b, 0:2 * T - P]).then_inc(ml["pt_copied"], 1)
                    n = T - 2 * P
                    copy(pt[0:n, 2 * T - P:2 * T - P + n], psum[0:n, b, 2 * T - P:2 * T - P + n]).then_inc(ml["pt_copied"], 1)
                    if h + 3 < HEADS:
                        copy_next(7)
                    if h + 2 < HEADS:
                        exps(h + 2)
                    t.next(ml["pv_done"])
                    copy(ml_o[:, h, :], psum[:, 6, 0:T]).then_inc(ml["o_ready"], 1)

            n_tile = 0

            to_split = [n for layer in range(2) for n in splits_2(layer)]

            def upper(last):
                while to_split and to_split[0] <= last:
                    n = to_split.pop(0)
                    slot = n % PAIRS_OF_SLOTS
                    act.wait_ge(b2[f"landed{slot}"], 16 * (n // PAIRS_OF_SLOTS + 1))
                    copy(ring_parts[:, PAIRS_OF_SLOTS + slot, :], ring[:, slot, :]).then_inc(b2["w_hi"], 1)

            def land(what, n, layer, halves=(0, 1), only=None):
                nonlocal n_tile
                if what in ("unit", "c1") and 0 in halves:
                    upper(L2_UNITS * layer + FETCHED[what, n] + 1)
                for half in halves if what == "unit" else (0,):
                    b = (n_tile - LAYER_TILES * layer) % 4 if only is None else only
                    t.next(b2["pj_done"])
                    n_tile += 1
                    if what == "unit":
                        kind, to = UNITS_2[n]
                        o = b_v[:, to, half, :] if kind == "v" else (b_ke if n < U_HF + 4 else b_p)[:, to + half, :]
                        m = copy(o, psum[:, b, 0:SEQ])
                    if what == "rot":
                        if n != U_KS:
                            t.next(b2["rope_done"])
                        m = copy(wide(n_rt[0:32]), psum[0:32, b, :])
                    if what == "c1":
                        act.activation(wide(n_c1[n]), psum[:, b, 0:2 * NCMP], ACT.Identity, bias=V(f"b1{'kv'[n]}{layer}"))\
                           .then_inc(b2["pj_copied"], 1)
                        act.wait_ge(b2["pj_copied"], n_tile)
                        if n:
                            act.wait_ge(b2["c1_ready"], 2 * layer + 1)
                        act.activation(wide(n_ce), wide(n_c1[n]), ACT.Exp, scale=-1.0).then_inc(b2["c1_exp"], 1)
                        continue
                    if what == "c2":
                        if n == 0:
                            m = copy(wide(n_kc), psum[:, b, 0:2 * NCMP])
                        else:
                            m = copy(wide(n_vc[0:NCMP]), psum[0:NCMP, b, 0:2 * P])
                    if what == "crot":
                        m = copy(wide(n_crt[0:32]), psum[0:32, b, 0:2 * NCMP])
                    m.then_inc(b2["pj_copied"], 1)

            def layer2(layer):
                for c in range(DC):
                    t.next(b2["x_new"])
                    square(b_qe[:, c, :], x2[:, c, :])
                if layer == 0:
                    upper(1)
                norm_root(D, SEQ, 7)
                for c in range(DC):
                    t.next(b2["n_new"])
                    copy(b_ns[0][:, c, :], b_n[:, c, :]).then_inc(b2["n_hi"], 1)
                for m in FIRST[:4]:
                    land(*m, layer)
                t.next(b2["lin_ready"])
                f = wide(b_ke)
                act.wait_ge(b2["pj_copied"], LAYER_TILES * layer + 8)
                act.activation(wide(b_g), f, ACT.Sigmoid)
                act.activation(wide(b_k), f, ACT.Sigmoid, scale=-1.0).then_inc(b2["sig_done"], 1)
                for m in FIRST[4:8]:
                    land(*m, layer)
                t.next(b2["lin_ready"])
                act.activation(wide(b_g), wide(b_g), ACT.Ln).then_inc(b2["ln_done"], 1)
                for m in FIRST[8:]:
                    land(*m, layer)
                t.next(b2["ng_done"])
                act.activation(wide(n_gate), psum[:, 4, 0:48], ACT.Sigmoid).then_inc(b2["gate_ready"], 1)
                half_d = [b_d[:, part * D:part * D + D] for part in range(2)]
                for job in range(9):
                    if job < 8:
                        for x in half_d:
                            t.next(b2["lv_d"])
                            act.activation(x, x, ACT.Exp).then_inc(b2["lv_e"], 1)
                    for m in JOBS[job]:
                        land(*m, layer)
                t.next(b2["rope_done"])
                def gate(units):
                    act.wait_ge(b2["pj_copied"], n_tile)
                    for _, u in units:
                        x = wide(b_p[:, UNITS_2[u][1]:UNITS_2[u][1] + 2, :])
                        act.activation(x, x, ACT.Silu).then_inc(b2["z_ready"], 1)

                land(*BEFORE_HEADS[0], layer)
                t.next(b2["av_done"])
                copy(wide(b_ke), flat[:, 2048:4096]).then_inc(b2["o_copied"], 1)
                land(*BEFORE_HEADS[1], layer)
                gate(BEFORE_HEADS)
                t.next(b2["osum"])
                t.link(act.activation(wide(b_qe), flat[:, 2048:4096], ACT.Ln, scale=1.0 / P, bias=eps[:, :]))
                act.activation(wide(b_qe), wide(b_qe), ACT.Exp, scale=-0.5).then_inc(b2["oroot"], 1)

                def exps(h):
                    _, least, total = n_st[h % 2]
                    t.next(b2["mx_ready"])
                    for br in range(2):
                        for i, at, n in ((0, 0, P), (1, P, SEQ)):
                            c = 2 * br + i
                            m = act.activation(n_e[h % 2][:, br, at:at + n], psum[:, 2 * (h % 2) + br, at:at + n], ACT.Exp,
                                               scale=NSA_SCALE, bias=least[:, c:c + 1], accum_out=total[:, c:c + 1])
                    m.then_inc(b2["e_done"], 1)

                exps(0)
                t.next(b2["cs_ready"])
                act.activation(wide(n_cs), wide(n_cs), ACT.Exp).then_inc(b2["ce_done"], 1)
                exps(1)
                for h in range(HEADS):
                    pt = n_pt[h % 2]
                    if h < len(IN_HEADS):
                        land(*IN_HEADS[h], layer, halves=(0,), only=7)
                    t.next(b2["pt_done"])
                    copy(pt[:, 0, 0:3 * P], psum[:, 4, 0:3 * P]).then_inc(b2["pta_copied"], 1)
                    copy(pt[0:NCMP, 0, 3 * P:4 * P], psum[0:NCMP, 4, 3 * P:4 * P]).then_inc(b2["pta_copied"], 1)
                    if h + 2 < HEADS:
                        exps(h + 2)
                    if h < len(IN_HEADS):
                        land(*IN_HEADS[h], layer, halves=(1,), only=7)
                    if h >= len(IN_HEADS):
                        upper(L2_UNITS * layer + LAST_FETCHED + h - len(IN_HEADS) + 2)
                    if h in GATED:
                        gate([IN_HEADS[n] for n in GATED[h]])
                    if h in HGRN_AT:
                        t.next(b2["o_h"])
                        at = HGRN_AT[h]
                        copy(b_ohs[0][:, 2 * at:2 * at + 2, :], b_p[:, F_HZ + 2 * at:F_HZ + 2 * at + 2, :]).then_inc(b2["oh_hi"], 1)
                    t.next(b2["o_n"])
                    copy(b_ons[0][:, h, :], b_p[:, F_NZ + h, :]).then_inc(b2["on_hi"], 1)
                upper(L2_UNITS * layer + LAST_FETCHED + 4)
                upper(L2_UNITS * layer + LAST_FETCHED + 5)
                for c in range(DC):
                    upper(L2_UNITS * layer + LAST_FETCHED + 6 + c // 2)
                    act.wait_ge(b2["wo_done"], 16 * layer + DC + c + 1)
                    square(b_qe[:, c, :], psum[:, c, 0:SEQ])
                    copy(b_p[:, c, :], psum[:, c, 0:SEQ]).then_inc(b2["wo_copied"], 1)
                norm_root(D, SEQ, 0)

            conv()
            moe(0)
            mla()
            moe(1)
            norm_root(D, SEQ, 0)
            t.next(b2["lb_d"])
            act.activation(wide(b_lbt), wide(b_lbt), ACT.Exp).then_inc(b2["lb_e"], 1)
            layer2(0)
            layer2(1)

        @block.gpsimd
        def _(gp):
            t = Turns(gp)
            n_2 = 0

            def lower(lo, whole, hi):
                return gp.tensor_tensor(lo, whole, hi, ALU.subtract)

            def split_unit():
                nonlocal n_2
                slot, n_2 = n_2 % PAIRS_OF_SLOTS, n_2 + 1
                t.next(b2["w_hi"])
                lower(ring_parts[:, slot, :], ring[:, slot, :], ring_parts[:, PAIRS_OF_SLOTS + slot, :])\
                    .then_inc(b2["w_ready"], 1)

            def layer2(layer):
                nonlocal n_2
                t.next(b2["x_new"], DC if layer else 1)
                gates, hi = V(f"wng{layer}"), wng_hi[:, :]
                gp.tensor_copy(hi, gates).then_inc(b2["g_hi"], 1)
                t.next(b2["g_hi"])
                lower(V(f"wng{layer}", vecs_parts), gates, hi)
                units = 0
                for what, n in FIRST + [m for job in JOBS for m in job] + BEFORE_HEADS + IN_HEADS[:2]:
                    if what == "c1":
                        n_2 += 2
                    if what == "unit":
                        split_unit()
                        units += 1
                        if units == 2:
                            for c in range(DC):
                                t.next(b2["n_hi"])
                                lower(b_ns[1][:, c, :], b_n[:, c, :], b_ns[0][:, c, :]).then_inc(b2["n_lo"], 1)
                for h in range(HEADS):
                    if h in HGRN_AT:
                        t.next(b2["oh_hi"])
                        at = slice(2 * HGRN_AT[h], 2 * HGRN_AT[h] + 2)
                        lower(b_ohs[1][:, at, :], b_p[:, F_HZ + at.start:F_HZ + at.stop, :], b_ohs[0][:, at, :])\
                            .then_inc(b2["oh_lo"], 1)
                    split_unit()
                    t.next(b2["on_hi"])
                    lower(b_ons[1][:, h, :], b_p[:, F_NZ + h, :], b_ons[0][:, h, :]).then_inc(b2["on_lo"], 1)
                for _ in range(4):
                    split_unit()

            layer2(0)
            t.next(b2["x_new"], DC - 1)
            layer2(1)

        @block.vector
        def _(v):
            t = Chain(v, dve_chain)

            def norm(x, n, w, outs):
                t.next(nrm_root)
                t.link(v.reciprocal(root[:, 0:w], root[:, 0:w]))
                for o, gain, signal in outs:
                    for c in range(n):
                        v.scalar_tensor_tensor(o[:, c, 0:w], x[:, c, :], gain[:, c:c + 1], root[:, 0:w], ALU.mult, ALU.mult)\
                         .then_inc(signal, 1)
                    t.next(signal, n)

            def tt(o, a, b, op, sem=None):
                t.link(v.tensor_tensor(o, a, b, op), sem)

            def ts(o, a, s1, op1, s2=None, op2=None, sem=None):
                t.link(v.tensor_scalar(o, a, s1, s2, op1, op2) if op2 else v.tensor_scalar(o, a, s1, None, op1), sem)

            def stt(o, a, s, b, op1, op2, sem=None):
                t.link(v.scalar_tensor_tensor(o, a, s, b, op1, op2), sem)

            def red(o, a, op, sem=None):
                t.link(v.tensor_reduce(o, a, AX, op), sem)

            def rep(a, n):
                return a.unsqueeze(len(a.shape)).to_broadcast([*a.shape, n])

            def rep_mid(a, n):
                return a.unsqueeze(1).to_broadcast([a.shape[0], n, a.shape[1]])

            def residual():
                for c in range(DC):
                    t.next(pr_done)
                    tt(hT[:, c, :], hT[:, c, :], psum[:, 6 + c % 2, 0:T], ALU.add, pr_add)

            def conv():
                t.link(v.memset(eps[:, :], EPS), eps_set)
                t.link(v.memset(cv_z[:, 0:2], 0.0))
                t.next(tokens_in, 16)
                t.next(const_in, 32)
                norm(hT[:, :, :], DC, T, [(cv_n, V("mix0"), nrm_out)])
                cw = V("convw").rearrange("p (k c) -> p k c", k=3)
                for j in range(4):
                    for half in range(2):
                        c = 2 * j + half
                        t.next(cv_c)
                        v.wait_ge(cv_pe, 6 * j + 5 + half)
                        tt(cv_z[:, 2:T + 2], cv_csb[:, half, :], psum[:, 3 * half + 2, 0:T], ALU.mult)
                        ts(cv_t, cv_z[:, 0:T], cw[:, 0, c:c + 1], ALU.mult)
                        for k in range(1, 3):
                            stt(cv_t, cv_z[:, k:T + k], cw[:, k, c:c + 1], cv_t, ALU.mult, ALU.add)
                        tt(cv_yt[:, c, :], cv_t, psum[:, 3 * half, 0:T], ALU.mult, cv_y)
                residual()

            def moe(layer):
                s = moe_sem[layer]
                t.link(v.memset(mo_n[:, :, T:TP], 0.0))
                norm(hT[:, :, :], DC, T, [(mo_n, V(f"ffn{layer}"), nrm_out)])
                v.wait_ge(s["lg_done"], 1)
                lg = psum[:, 0, 0:TT * 72].rearrange("p (t n) -> p t n", t=TT)
                revidx = rep_mid(C("revidx"), TT)

                def first(oh, hit, i):
                    tt(r8[9], hit, revidx, ALU.mult)
                    red(r1[i], r8[9], ALU.max)
                    tt(oh, r8[9], rep(r1[i], 8), ALU.is_equal)

                gmax, gsum, pg = r1[0], r1[1], r1[2]
                red(gmax, lg[:, :, 0:8], ALU.max)
                tt(r8[1], lg[:, :, 0:8], rep(gmax, 8), ALU.subtract, s["dg_ready"])
                ts(r8[0], r8[1], 0.0, ALU.is_equal)
                grp = r8[3]
                first(grp, r8[0], 9)
                tt(grp, grp, rep(C("valid"), 8), ALU.mult)
                t.next(s["exp_done"])
                red(gsum, r8[2], ALU.add)
                t.link(v.reciprocal(pg, gsum))
                part = flat_tmp.rearrange("p (t g e) -> p t g e", t=TT, g=G)
                tt(part, lg[:, :, 8:72].rearrange("p t (g e) -> p t g e", g=G), rep(grp, 8), ALU.mult)
                red(r8[4], part.rearrange("p t g e -> p t e g"), ALU.add)
                red(r1[3], r8[4], ALU.max)
                tt(r8[5], r8[4], rep(r1[3], 8), ALU.subtract, s["dg_ready"])
                t.next(s["exp_done"])
                prob, one, two = r8[6], r8[7], r8[8]
                red(r1[4], prob, ALU.add)
                t.link(v.reciprocal(r1[4], r1[4]))
                tt(prob, prob, rep(r1[4], 8), ALU.mult)
                red(r1[5], prob, ALU.max)
                tt(r8[0], prob, rep(r1[5], 8), ALU.is_equal)
                first(one, r8[0], 9)
                stt(prob, one, -4.0, prob, ALU.mult, ALU.add)
                red(r1[6], prob, ALU.max)
                tt(r8[0], prob, rep(r1[6], 8), ALU.is_equal)
                first(two, r8[0], 9)
                tt(r1[7], r1[5], r1[6], ALU.add)
                t.link(v.reciprocal(r1[7], r1[7]))
                tt(r1[7], r1[7], pg, ALU.mult)
                tt(r1[5], r1[5], r1[7], ALU.mult)
                tt(r1[6], r1[6], r1[7], ALU.mult)
                tt(r8[0], one, two, ALU.add)
                tt(one, one, rep(r1[5], 8), ALU.mult)
                tt(two, two, rep(r1[6], 8), ALU.mult)
                tt(one, one, two, ALU.add)
                for o, src, signal in ((mo_w, one, None), (mo_a, r8[0], s["route_ready"])):
                    tt(o.rearrange("p t (g e) -> p t g e", g=G), rep(grp, 8),
                       src.unsqueeze(2).to_broadcast([P, TT, G, 8]), ALU.mult, signal)
                v.wait_ge(s["rank_done"], 1)
                rank = psum[:, 7, 0:TT * NE].rearrange("p (t n) -> p t n", t=TT)
                stt(mo_tmp, rank, 1.0, mo_a, ALU.add, ALU.mult)
                ts(mo_rank, mo_tmp, -1.0, ALU.add, sem=s["add_done"])
                red(r_c, psum[:, 7, TT * NE:TT * NE + NE], ALU.max)
                ts(r_gt, C("rounds"), r_c[:, 0:1], ALU.is_lt)
                red(r_n, r_gt, ALU.add)
                ts(r_n, r_n, float(QUADS), ALU.mult)
                ts(r_c, r_n, -1.0, ALU.add)
                t.link(v.tensor_copy(n_last[:, layer:layer + 1], r_c))
                t.link(v.tensor_copy(n_iter[:, layer:layer + 1], r_n), s["iter_ready"])

                v.memset(mo_sw[:, :], 0.0).then_inc(s["sw_ready"], 1)
                v.memset(mo_stw, 0.0).then_inc(s["stw_done"], 1)
                v.memset(mo_y[:, 0:512], 0.0).then_inc(s["ya_ready"], 1)
                v.memset(mo_y[:, 512:1024], 0.0).then_inc(s["yd_ready"], 1)

                def slots(quad4, base):
                    which = rep(mo_rank[:, :, bass.ds(quad4, 4)], SLOT)
                    place = C("iota")[:, bass.ds(base, SLOT)]
                    place = place.unsqueeze(1).unsqueeze(1).to_broadcast([P, TT, 4, SLOT])
                    v.tensor_tensor(mo_st, which, place, ALU.is_equal).then_inc(s["st_ready"], 1)

                def add(i, c):
                    v.wait_ge(s["cmb_done"], i * DC + c + 1)
                    v.tensor_tensor(hT[:, c, :], hT[:, c, :], psum[:, 6 + c % 2, 0:T], ALU.add).then_inc(s["add_done"], 1)

                slots(0, 0)
                v.wait_ge(s["iter_ready"], 1)
                n = v.value_load(n_iter[0:1, layer:layer + 1], min_val=QUADS, max_val=QUADS * ROUNDS)
                with v.Fori(0, n) as i:
                    v.wait_ge(s["st_ready"], i + 1)
                    v.wait_ge(s["stw_done"], i + 1)
                    v.tensor_tensor(mo_stw, mo_st, rep(mo_w[:, :, bass.ds((i % QUADS) * 4, 4)], SLOT), ALU.mult)\
                     .then_inc(s["stw_ready"], 1)
                    v.wait_ge(s["prep_done"], i + 1)
                    v.wait_ge(s["stw_ready"], i + 1)
                    slots(((i + 1) % QUADS) * 4, ((i + 1) // QUADS) * SLOT)
                    v.wait_ge(s["silu_done"], i + 1)
                    v.tensor_tensor(mo_h, mo_silu, psum[:, 3, 256:512], ALU.mult).then_inc(s["h_ready"], 1)
                    v.wait_ge(s["ht_done"], i + 1)
                    v.tensor_copy(wide(mo_ht), psum[:, 3, 0:256]).then_inc(s["ht_ready"], 1)
                    v.wait_ge(s["add_done"], i * DC + 1)
                    for c in range(DC):
                        add(i, c)
                    v.wait_ge(s["used"], i * QU + QU)
                    v.tensor_copy(mo_y[:, 512:1024], psum[:, 5, :]).then_inc(s["yd_ready"], 1)
                v.wait_ge(s["add_done"], n * DC + 1)
                for c in range(DC):
                    add(n, c)
                v.wait_ge(s["add_done"], n * DC + (DC + 1))

            def rope(x, rot, cos, sin, tmp, sem=None):
                tt(tmp, rot, sin, ALU.mult)
                tt(x, x, cos, ALU.mult)
                tt(x, x, tmp, ALU.add, sem)

            def mla():
                for st in ml_st:
                    for x in st:
                        v.memset(x, 1.0)
                t.link(v.memset(ml_krz, 0.0))
                norm(hT[:, :, :], DC, T, [(ml_kv, V("kvg"), nrm_out), (ml_q, V("mix1"), nrm_out)])
                norm(ml_ckv, 2, T, [(ml_ckvn, V("ckvg"), nrm_out)])
                t.next(ml["krot_done"])
                rope(ml_kr, psum[:, 6, 0:T], C("cosm"), C("sinm"), ml_rt[:, 0, :])
                t.link(v.tensor_copy(ml_krz[0:64, 0, :], ml_kr[0:64, :]))
                t.link(v.tensor_copy(ml_krz[64:P, 1, :], ml_kr[64:P, :]), ml["kr_ready"])
                norm(ml_cq, 3, T, [(ml_cqn, V("cqg"), nrm_out)])
                t.next(ml["rot_done"])
                rope(ml_qr, psum[:, 4:8, 0:T], rep_mid(C("cosm"), 4), rep_mid(C("sinm"), 4), ml_rt, ml["q_ready"])

                def maxima(h):
                    mx, least, _ = ml_st[h % 2]
                    t.next(ml["sc_done"])
                    for i in range(TT):
                        n, keys = min(P, T - i * P), min(T, i * P + P)
                        b, at = 2 * (h % 2) + i // 2, (0, P, 0)[i]
                        m = v.tensor_reduce(mx[0:n, i:i + 1], psum[0:n, b, at:at + keys], AX, ALU.max)
                    t.link(m)
                    ts(least, mx, -MLA_SCALE, ALU.mult, sem=ml["mx_ready"])

                maxima(0)
                maxima(1)
                for h in range(HEADS):
                    e, (_, _, total) = ml_e[h % 2], ml_st[h % 2]
                    t.next(ml["e_done"])
                    t.link(v.reciprocal(total, total))
                    for i in range(TT):
                        n, keys, at = min(P, T - i * P), min(T, i * P + P), (0, P, 3 * P)[i]
                        m = v.tensor_scalar(e[0:n, at:at + keys], e[0:n, at:at + keys], total[0:n, i:i + 1], None, ALU.mult)
                    t.link(m, ml["p_ready"])
                    if h + 2 < HEADS:
                        maxima(h + 2)
                residual()

            def bounds():
                lg = V("lbl").rearrange("p (l c) -> p l c", l=2)
                tt(b_bl, lg[:, 0], lg[:, 1], ALU.max)
                tt(b_lbt, lg, rep_mid(b_bl, 2), ALU.subtract, b2["lb_d"])
                t.next(b2["lb_e"])
                tt(b_bl, b_lbt[:, 0], b_lbt[:, 1], ALU.add)
                t.link(v.reciprocal(b_bl, b_bl))
                tt(b_lbt, b_lbt, rep_mid(b_bl, 2), ALU.mult)
                tt(b_lb[:, 0], b_lbt[:, 0], b_lbt[:, 0], ALU.subtract)
                tt(b_lb[:, 1], b_lbt[:, 0], b_lbt[:, 1], ALU.add)
                tt(b_lb[:, 1], b_lb[:, 1], b_lbt[:, 0], ALU.subtract)
                ts(b_lb, b_lb, 0.0, ALU.max)
                ts(b_lbi, b_lb, -1.0, ALU.mult, 1.0, ALU.add)

            def layer2(layer):
                made = LAYER_TILES * layer

                def landed_by(what, n):
                    v.wait_ge(b2["pj_copied"], made + MADE[what, n])

                norm(x2, DC, SEQ, [(b_n, V(f"pre{layer}"), b2["n_new"])])
                t.link(v.memset(wide(b_at), 0.0), b2["lin_ready"])
                t.next(b2["sig_done"])
                tt(b_g, b_g, rep(b_lbi[:, layer], SEQ), ALU.mult)
                tt(b_g, b_g, rep(b_lb[:, layer], SEQ), ALU.add)
                ts(b_g, b_g, LN_LEAST, ALU.max, sem=b2["lin_ready"])
                tt(b_k, b_k, rep(b_lbi[:, layer], SEQ), ALU.mult)
                t.next(b2["ln_done"])
                for h in range(HEADS):
                    m = v.tensor_tensor_scan(b_b[:, h, :], C("reset"), b_g[:, h, :], 0.0, ALU.mult, ALU.add)
                t.link(m)
                q = b_p[:, F_Q:F_Q + HEADS, :]
                landed_by("unit", 7)
                masks = C("lev").rearrange("p (j t) -> p j t", j=7).bitcast(U32)

                def decay(job, part):
                    b, d = wide(b_b[:, 4 * part:4 * part + 4, :]), b_d[:, part * D:part * D + D]
                    if job < len(LEVELS):
                        n = LEVELS[job]
                        x, o = (y.rearrange("p (k n) -> p k n", n=n) for y in (b, d))
                        ref = x[:, :, n // 2 - 1:n // 2].to_broadcast([P, D // n, n // 2])
                        v.tensor_tensor(o[:, :, 0:n // 2], ref, x[:, :, 0:n // 2], ALU.subtract)
                        tt(o[:, :, n // 2:n], x[:, :, n // 2:n], ref, ALU.subtract, b2["lv_d"])
                        return
                    end = CHUNK - 1
                    if job == 6:
                        x, o = (y.rearrange("p (k c n) -> p k c n", c=2, n=CHUNK) for y in (b, d))
                        v.tensor_tensor(o[:, :, 0], x[:, :, 0, end:].to_broadcast([P, PAIRS // 2, CHUNK]), x[:, :, 0], ALU.subtract)
                        t.link(v.tensor_copy(o[:, :, 1], x[:, :, 1]), b2["lv_d"])
                        return
                    x, o = (y.rearrange("p (h c n) -> p h c n", c=4, n=CHUNK) for y in (b, d))
                    tt(b_bl[:, 0:4], x[:, :, 0, end], x[:, :, 1, end], ALU.add)
                    v.tensor_tensor(o[:, :, 0], rep(b_bl[:, 0:4], CHUNK), x[:, :, 0], ALU.subtract)
                    v.tensor_tensor(o[:, :, 1], x[:, :, 1, end:].to_broadcast([P, 4, CHUNK]), x[:, :, 1], ALU.subtract)
                    v.tensor_copy(o[:, :, 2], x[:, :, 2])
                    tt(o[:, :, 3], x[:, :, 3], x[:, :, 2, end:].to_broadcast([P, 4, CHUNK]), ALU.add, b2["lv_d"])

                def gather(job):
                    for part in range(2):
                        t.next(b2["lv_mm"])
                        if job == 7:
                            at = 2048 + part * 4 * P
                            t.link(v.tensor_copy(wide(b_ax[:, 4 * part:4 * part + 4, :]), flat[:, at:at + 4 * P]), b2["lv_at"])
                            continue
                        mask = masks[:, job, :] if job < 7 else C("ident").bitcast(U32)
                        at = 2048 + part * D
                        t.link(v.copy_predicated(b_at[:, 8 * part:8 * part + 8, :], rep_mid(mask, 8),
                                                 flat[:, at:at + D].rearrange("p (k t) -> p k t", k=8)), b2["lv_at"])

                def rope_unit(u):
                    landed_by("rot", u)
                    x = b_p[0:32, UNITS_2[u][1]:UNITS_2[u][1] + 2, :]
                    rope(x, n_rt[0:32], rep_mid(C("cosn")[0:32, :], 2), rep_mid(C("sinn")[0:32, :], 2), n_rt[0:32], b2["rope_done"])

                def positions(kv):
                    landed_by("unit", (U_KC, U_VC)[kv])
                    x = b_p[:, (F_KC, F_VC)[kv]:(F_KC, F_VC)[kv] + 2, :]
                    pos = V(f"pos{'kv'[kv]}{layer}").rearrange("p (l o) -> p l o", l=2)
                    for part in range(2):
                        src = x[:, :, 16 * part:16 * part + 16 * NCMP].rearrange("p g (n l) -> p l g n", l=16)
                        at = pos[:, part].unsqueeze(2).unsqueeze(3).to_broadcast([P, 16, 2, NCMP])
                        m = v.tensor_tensor(n_kp[kv][:, 16 * part:16 * part + 16], src, at, ALU.add)
                    t.link(m, b2["kp_ready"])

                for job in range(9):
                    if job < 8:
                        decay(job, 0)
                        decay(job, 1)
                    if job in (1, 2):
                        positions(job - 1)
                    for what, n in JOBS[job - 1] if job else []:
                        if what == "rot":
                            rope_unit(n)
                        if what == "c1":
                            t.next(b2["c1_exp"])
                            ts(n_ce, n_ce, 1.0, ALU.add)
                            t.link(v.reciprocal(n_ce, n_ce))
                            tt(n_c1[n], n_c1[n], n_ce, ALU.mult, b2["c1_ready"])
                        if what == "crot":
                            landed_by("crot", 0)
                            rope(n_kc[0:32], n_crt[0:32], rep_mid(C("cosc")[0:32, :], 2), rep_mid(C("sinc")[0:32, :], 2),
                                 n_crt[0:32], b2["crope_done"])
                    if job:
                        gather(job - 1)
                    if job < 8:
                        n = (LEVELS + (P, SEQ))[job]
                        for part in range(2):
                            t.next(b2["lv_e"])
                            hs = slice(4 * part, 4 * part + 4)
                            e = b_d[:, part * D:part * D + D].rearrange("p (k n) -> p k n", n=n)
                            ke, qe, k_, q_ = (wide(x[:, hs, :]).rearrange("p (k n) -> p k n", n=n) for x in (b_ke, b_qe, b_k, q))
                            v.tensor_tensor(ke[:, :, 0:n // 2], k_[:, :, 0:n // 2], e[:, :, 0:n // 2], ALU.mult)
                            tt(qe[:, :, n // 2:n], q_[:, :, n // 2:n], e[:, :, n // 2:n], ALU.mult, b2["lv_kq"])
                gather(8)
                t.next(b2["o_copied"])
                tt(b_d, wide(b_ke), wide(b_ke), ALU.mult, b2["osq"])

                def maxima(h):
                    mx, least, _ = n_st[h % 2]
                    t.next(b2["sc_done"])
                    for br in range(2):
                        for i, at, n in ((0, 0, P), (1, P, SEQ)):
                            c = 2 * br + i
                            m = v.tensor_reduce(mx[:, c:c + 1], psum[:, 2 * (h % 2) + br, at:at + n], AX, ALU.max)
                    t.link(m)
                    ts(least, mx, -NSA_SCALE, ALU.mult, sem=b2["mx_ready"])

                maxima(0)
                t.next(b2["csc_done"])
                scores = psum[:, 6, 0:2 * HEADS * NCMP].rearrange("p (i h n) -> p i h n", i=2, h=HEADS)
                ec = n_cs.rearrange("p i (h n) -> p i h n", h=HEADS)
                each = wide(n_cs).rearrange("p (k n) -> p k n", n=NCMP)
                cmask, cvalid = (C(n).rearrange("p (i n) -> p i n", i=2) for n in ("cmask", "cvalid"))
                for i in range(2):
                    m = v.scalar_tensor_tensor(ec[:, i], scores[:, i], NSA_SCALE, rep_mid(cmask[:, i], HEADS), ALU.mult, ALU.add)
                t.link(m)
                red(n_cmx, each, ALU.max)
                tt(each, each, rep(n_cmx, NCMP), ALU.subtract, b2["cs_ready"])
                maxima(1)
                t.next(b2["oroot"])
                stt(wide(b_ke), wide(b_ke), V(f"on{layer}"), wide(b_qe), ALU.mult, ALU.mult)
                t.next(b2["ce_done"])
                for i in range(2):
                    m = v.tensor_tensor(ec[:, i], ec[:, i], rep_mid(cvalid[:, i], HEADS), ALU.mult)
                t.link(m)
                red(n_csum, each, ALU.add)
                ts(n_csum, n_csum, 1e-30, ALU.max)
                t.link(v.reciprocal(n_csum, n_csum))
                gates = n_gate.rearrange("p i (h b) -> p i h b", b=3)
                tt(n_csum.rearrange("p (i h) -> p i h", i=2), n_csum.rearrange("p (i h) -> p i h", i=2), gates[:, :, :, 0], ALU.mult)
                tt(each, each, rep(n_csum, NCMP), ALU.mult)

                def gated(u):
                    v.wait_ge(b2["z_ready"], 8 * layer + (BEFORE_HEADS + IN_HEADS).index(("unit", u)) + 1)

                def output(h):
                    t.next(b2["pv_done"])
                    tile = b_p[:, F_NZ + h, :]
                    gated(U_NZ + h // 2)
                    tt(tile, tile, psum[:, 6, 0:SEQ], ALU.mult, b2["o_n"])

                for h in range(HEADS):
                    e, (_, _, total), pt = n_e[h % 2], n_st[h % 2], n_pt[h % 2]
                    t.next(b2["e_done"])
                    t.link(v.reciprocal(total, total))
                    total = total.rearrange("p (b i) -> p b i", b=2)
                    tt(total, total, n_gate[:, :, 3 * h + 1:3 * h + 3].rearrange("p i b -> p b i"), ALU.mult)
                    v.tensor_tensor(e[:, :, 0:P], e[:, :, 0:P], rep(total[:, :, 0], P), ALU.mult)
                    tt(e[:, :, P:3 * P], e[:, :, P:3 * P], rep(total[:, :, 1], SEQ), ALU.mult, b2["p_ready"])
                    if h in HGRN_AT:
                        u = HGRN_AT[h]
                        gated(U_HZ + u)
                        hz = b_p[:, F_HZ + 2 * u:F_HZ + 2 * u + 2, :]
                        tt(hz, hz, b_ke[:, 2 * u:2 * u + 2, :], ALU.mult, b2["o_h"])
                    t.next(b2["pt_done"])
                    v.tensor_copy(pt[:, 1, 0:3 * P], psum[:, 5, 0:3 * P]).then_inc(b2["ptb_copied"], 1)
                    v.tensor_copy(pt[0:NCMP, 1, 3 * P:4 * P], psum[0:NCMP, 5, 3 * P:4 * P]).then_inc(b2["ptb_copied"], 1)
                    if h + 2 < HEADS:
                        maxima(h + 2)
                    output(h)
                t.next(b2["wo_copied"], DC)
                y = b_p[:, 0:DC, :]
                t.next(nrm_root)
                t.link(v.reciprocal(root[:, 0:SEQ], root[:, 0:SEQ]))
                gain = V(f"post{layer}")
                for c in range(DC):
                    v.scalar_tensor_tensor(y[:, c, :], y[:, c, :], gain[:, c:c + 1], root[:, 0:SEQ], ALU.mult, ALU.mult)\
                     .then_inc(dve_chain, 1)
                for c in range(DC):
                    t.next(dve_chain)
                    v.tensor_tensor(x2[:, c, :], x2[:, c, :], y[:, c, :], ALU.add).then_inc(b2["x_new"], 1)
                t.next(b2["x_new"], DC)

            flat_tmp = wide(mo_tmp)
            conv()
            moe(0)
            mla()
            moe(1)
            norm(hT[:, :, META:T], DC, SEQ, [(x2, V("fing"), b2["x_new"])])
            bounds()
            layer2(0)
            layer2(1)


def constants():
    import numpy as np

    f = np.float32
    p = np.arange(P)
    out = {}
    out["ident"] = np.eye(P)
    out["ones"] = np.ones((P, P))
    out["upper"] = np.triu(np.ones((P, P)), 1)
    out["iota"] = np.broadcast_to(np.arange((ROUNDS + 1) * SLOT), (P, (ROUNDS + 1) * SLOT))
    out["rounds"] = np.broadcast_to(np.arange(ROUNDS) * SLOT, (P, ROUNDS))
    out["revidx"] = np.broadcast_to(8 - np.arange(8), (P, 8))
    out["valid"] = (p[:, None] + P * np.arange(TT) < T)
    token = p[:, None] + P * np.arange(TT)
    out["mask"] = np.where(p <= p[:, None], 0.0, MASKED)
    ended = 16 * np.arange(NCMP) + 31 <= token[:, :2, None]
    out["cmask"] = np.where(ended, 0.0, MASKED).reshape(P, -1)
    out["cvalid"] = ended.reshape(P, -1)
    out["reset"] = np.broadcast_to(np.arange(SEQ) % CHUNK != 0, (P, SEQ))
    levels = [(p[:, None] // n == p // n) & (p[:, None] % n < n // 2) & (p % n >= n // 2) for n in LEVELS + (P,)]
    out["lev"] = np.concatenate(levels, axis=1)

    def rotation(half, heads=1):
        m = np.zeros((P, 2 * half * heads))
        for h in range(heads):
            at = np.arange(half) + 2 * half * h
            m[at + half, at] = -1
            m[at, at + half] = 1
        return m

    def tables(theta, dim, at, heads=1):
        inv = f(theta) ** (-np.arange(0, dim, 2, dtype=f) / f(dim))
        ang = (at.astype(f)[None, :] * inv[:, None]).astype(f)
        rows = np.zeros((2, P, len(at)))
        rows[0, :dim * heads] = np.tile(np.cos(ang.astype(np.float64)), (2 * heads, 1))
        rows[1, :dim * heads] = np.tile(np.sin(ang.astype(np.float64)), (2 * heads, 1))
        return rows

    out["cosm"], out["sinm"] = tables(10000.0, 64, np.arange(T), 2)
    out["cosn"], out["sinn"] = tables(500000.0, 32, np.arange(SEQ))
    out["cosc"], out["sinc"] = tables(500000.0, 32, 16 * np.arange(NCMP) + 31)
    out["rotm"], out["rotn"] = rotation(32, 2), rotation(16)
    return np.concatenate([np.asarray(out[k], f).reshape(P, n) for k, n in CONST.items()], axis=1)


def laid_out(x):
    import numpy as np

    x = {k: np.asarray(a) for k, a in x.items()}

    def columns(a):
        return a.reshape(-1, P).T

    def rows(a):
        return a.reshape(-1, P, a.shape[-1]).transpose(1, 0, 2).reshape(P, -1)

    def unit(a):
        a = rows(a)
        return np.pad(a, ((0, 0), (0, UNIT - a.shape[1])))

    v = {"convw": np.concatenate([columns(w) for w in x["conv_w"][0, :, 0]], axis=1),
         "kvg": columns(x["kv_norm_g"]), "ckvg": columns(x["ckv_norm_g"]), "cqg": columns(x["cq_norm_g"][0]),
         "fing": columns(x["final_norm_g"]),
         "lbl": np.concatenate([columns(a) for a in x["hgrn_lb_logits_2"]], axis=1)}
    for i in range(2):
        v[f"mix{i}"], v[f"ffn{i}"] = columns(x["norm_mix_g"][i]), columns(x["norm_ffn_g"][i])
        v[f"pre{i}"], v[f"post{i}"] = columns(x["pre_norm_2"][i]), columns(x["post_norm_2"][i])
        v[f"on{i}"] = columns(x["hgrn_out_norm_2"][i])
        for kv in "kv":
            v[f"b1{kv}{i}"] = columns(x[f"cmp_b1_{kv}_2"][i])
            v[f"pos{kv}{i}"] = x[f"cmp_pos_{kv}_2"][i].T
            v[f"w2{kv}{i}"] = x[f"cmp_w2_{kv}_2"][i]
        v[f"wng{i}"] = rows(x["w_in_2"][i][:, GATE_COLUMN:GATE_COLUMN + 24])
        v[f"wr{i}"] = rows(np.concatenate([x["w_grp"][i], x["w_exp"][i]], axis=1))
    vecs = np.concatenate([v[k].reshape(P, n) for k, n in VEC.items()], axis=1)

    w = x["conv_w_in"][0]
    dense = [unit(w[:, part * D + 256 * j:part * D + 256 * j + 256]) for j in range(4) for part in range(3)]
    dense += [unit(x["conv_w_out"][0][:, 256 * j:256 * j + 256]) for j in range(4)]
    dkv, dq = x["w_dkv"], x["w_dq"][0]
    dense += [unit(dkv[:, :256]), unit(np.concatenate([dkv[:, 256:], dkv[:, 256:], dq[:, 256:]], axis=1)), unit(dq[:, :256])]
    ukv = x["w_ukv"].reshape(256, HEADS, 256)
    dense += [unit(ukv[:, :, :P].reshape(256, -1)), unit(ukv[:, :, P:].reshape(256, -1))]
    uq = x["w_uq"][0].reshape(384, HEADS, 192)
    dense += [unit(uq[:, :, P:].reshape(384, -1)), unit(uq[:, :5, :P].reshape(384, -1)), unit(uq[:, 5:, :P].reshape(384, -1))]
    dense += [unit(x["w_o"][0][:, 256 * j:256 * j + 256]) for j in range(4)]
    for i in range(2):
        w_in, w_out = x["w_in_2"][i], x["w_out_2"][i]
        for what, n in MAKES:
            if what == "unit":
                c = COLUMNS_2[n][0]
                dense.append(unit(w_in[:, c:c + 256]))
            if what == "c1":
                w1 = x[f"cmp_w1_{'kv'[n]}_2"][i]
                dense += [unit(w1[:D * 2]), unit(w1[D * 2:])]
        dense += [unit(w_out[part * D:part * D + D, 256 * j:256 * j + 256]) for part in range(2) for j in range(4)]

    gate = x["w_gate"].reshape(2, QUADS, 4, 8, P, 256)
    up = x["w_up"].reshape(2, QUADS, 4, 8, P, 256)
    both = np.stack([gate, up], axis=5).transpose(0, 1, 3, 4, 2, 5, 6).reshape(2, QUADS, 8, P, UNIT)
    down = x["w_down"].reshape(2, QUADS, 4, 2, P, 2, 512).transpose(0, 1, 5, 3, 4, 2, 6).reshape(2, QUADS, 4, P, UNIT)
    h = np.concatenate([x["meta_tokens"], x["x"][0]], axis=0).T
    return {"h_in": rows(h), "consts_in": constants(), "vecs_in": vecs, "dense": np.stack(dense),
            "experts": np.concatenate([both, down], axis=2)}


def kernel(**inputs):
    import numpy as np
    import concourse.bacc as bacc
    from concourse.bass_utils import run_bass_kernel_spmd

    nc = bacc.Bacc("TRN2", target_bir_lowering=False, num_devices=1)
    arrays = {k: np.ascontiguousarray(a) for k, a in laid_out(inputs).items()}
    args = [nc.dram_tensor(k, a.shape, mybir.dt.from_np(a.dtype), kind="ExternalInput").ap() for k, a in arrays.items()]
    out = nc.dram_tensor("out_0", (P, DC * SEQ), F32, kind="ExternalOutput").ap()
    build(nc, *args, out)
    r = run_bass_kernel_spmd(nc, [arrays], core_ids=[0])
    return r.results[0]["out_0"].reshape(P, DC, SEQ).transpose(2, 1, 0).reshape(1, SEQ, D)
```

```python
from contextlib import ExitStack

import concourse.bass as bass
from concourse import mybir

F32 = mybir.dt.float32
BF16 = mybir.dt.bfloat16
F32R = mybir.dt.float32r
I32 = mybir.dt.int32
U32 = mybir.dt.uint32
ALU = mybir.AluOpType
ACT = mybir.ActivationFunctionType
AX = mybir.AxisListType.X

P = 128
D = 1024
DC = D // P
META = 16
SEQ = 256
T = META + SEQ
TT = 3
TP = TT * P
HEADS = 8
EPS = 1e-6
UNIT = 2048
RING = 6
PAIRS_OF_SLOTS = RING // 2
G = 8
EG = 8
NE = G * EG
QUADS = NE // 4
SLOT = 32
ROUNDS = -(-T // SLOT)
QU = 12
MLA_SCALE = 192.0 ** -0.5
NSA_SCALE = 128.0 ** -0.5
MASKED = -1e30
NCMP = 15
LEVELS = (64, 32, 16, 8, 4, 2)
CHUNK = 64
PAIRS = 2 * HEADS
LN_LEAST = 2.0 ** -63

CONV_UNITS = 16
MLA_UNITS = 12
L2_UNITS = 42
FIRST_2 = CONV_UNITS + MLA_UNITS
ARENA = 30320

F_F, F_Q, F_NQ, F_KS, F_KW, F_KC, F_VC, F_HZ, F_NZ = 0, 8, 16, 24, 26, 28, 30, 32, 40
SPLITS = dict(hq=1024, hf=1024, hi=1024, hz=1024, nq=1024, kc=256, vc=256, ks=256, vs=256, kw=256, vw=256, ng=24, nz=1024)


def units_2():
    at, first = 0, {}
    for k, n in SPLITS.items():
        first[k] = at
        at += n
    out = []
    for name, kind, to in (("hf", "f", F_F), ("hq", "f", F_Q), ("hi", "v", 0), ("kc", "f", F_KC), ("vc", "f", F_VC),
                           ("ks", "f", F_KS), ("kw", "f", F_KW), ("nq", "f", F_NQ), ("vs", "v", 4), ("vw", "v", 5),
                           ("nz", "f", F_NZ), ("hz", "f", F_HZ)):
        for u in range(SPLITS[name] // 256):
            out.append((first[name] + 256 * u, kind, to + u * (2 if kind == "f" else 1)))
    return out, first["ng"]


COLUMNS_2, GATE_COLUMN = units_2()
UNITS_2 = [(kind, to) for _, kind, to in COLUMNS_2]
U_HF, U_HI, U_KC, U_VC, U_KS, U_KW, U_NQ, U_VS, U_VW, U_NZ, U_HZ = 0, 8, 12, 13, 14, 15, 16, 20, 21, 22, 26
FIRST = [("unit", u) for u in range(U_KC)]
JOBS = [[("unit", U_KC), ("unit", U_VC)],
        [("unit", U_KS)],
        [("unit", U_KW), ("c1", 0), ("rot", U_KS)],
        [("unit", U_NQ), ("c1", 1), ("rot", U_KW)],
        [("unit", U_NQ + 1), ("c1sum", 0), ("c1", 2), ("rot", U_NQ)],
        [("unit", U_NQ + 2), ("c1", 3), ("rot", U_NQ + 1)],
        [("unit", U_NQ + 3), ("c1sum", 1), ("rot", U_NQ + 2)],
        [("unit", U_VS), ("c2", 0), ("c2", 1), ("rot", U_NQ + 3), ("crot", 0)],
        [("unit", U_VW)]]
BEFORE_HEADS = [("unit", U_NZ), ("unit", U_HZ)]
IN_HEADS = [("unit", u) for u in (U_NZ + 1, U_HZ + 1, U_NZ + 2, U_HZ + 2, U_HZ + 3, U_NZ + 3)]
GATED = {1: (0, 1), 3: (2, 3), 4: (4,), 5: (5,)}
HGRN_AT = {1: 0, 2: 1, 4: 2, 5: 3}
MAKES = FIRST + [m for job in JOBS for m in job] + BEFORE_HEADS + IN_HEADS


def tiles_2():
    at, out = 0, {}
    for what, n in MAKES:
        at += 2 if what == "unit" else 1
        out[what, n] = at
    return out, at


MADE, LAYER_TILES = tiles_2()


def fetched_2():
    at, out = 0, {}
    for what, n in MAKES:
        at += what in ("unit", "c1")
        out[what, n] = at
    return out, at


FETCHED, LAST_FETCHED = fetched_2()


def splits_2(layer):
    at = FIRST_2 + layer * L2_UNITS
    return [at + FETCHED[m] - 1 for m in MAKES if m[0] == "unit"] + [at + LAST_FETCHED + u for u in range(8)]


CONST = dict(ident=128, ones=128, iota=(ROUNDS + 1) * SLOT, rounds=ROUNDS, revidx=8, valid=3,
             stack=2 * NCMP, cmask=2 * NCMP, cvalid=2 * NCMP, reset=SEQ, lev=7 * P,
             cosm=T, sinm=T, rotm=P, cosn=SEQ, sinn=SEQ, rotn=32, cosc=NCMP, sinc=NCMP)
SMALL = dict(upper=P, mask=P)
VEC = dict(mix0=8, mix1=8, ffn0=8, ffn1=8, convw=24, kvg=8, ckvg=2, cqg=3, fing=8,
           pre0=8, pre1=8, post0=8, post1=8, lbl=16, on0=1, on1=1,
           b1k0=1, b1k1=1, b1v0=1, b1v1=1, posk0=32, posk1=32, posv0=32, posv1=32,
           w2k0=128, w2k1=128, w2v0=128, w2v1=128, wng0=192, wng1=192, wr0=576, wr1=576)


def offsets(table):
    at, out = 0, {}
    for k, n in table.items():
        out[k] = (at, n)
        at += n
    return out, at


CONST_AT, CONST_N = offsets(CONST)
SMALL_AT, SMALL_N = offsets(SMALL)
VEC_AT, VEC_N = offsets(VEC)


class Turns:

    def __init__(self, eng):
        self.eng, self.seen = eng, {}

    def next(self, sem, k=1):
        self.seen[sem.name] = self.seen.get(sem.name, 0) + k
        self.eng.wait_ge(sem, self.seen[sem.name])


class Chain(Turns):

    def __init__(self, eng, sem):
        super().__init__(eng)
        self.sem = sem

    def link(self, ins, sem=None):
        sem = sem or self.sem
        ins.then_inc(sem, 1)
        self.next(sem)


def build(nc, h_in, consts_in, vecs_in, dense, experts, out):
    with ExitStack() as ctx:
        def sb(name, shape, dt=F32):
            return ctx.enter_context(nc.sbuf_tensor(name, shape, dt))

        def sem(name):
            return ctx.enter_context(nc.semaphore(name))

        def sb_both(name, shape, split=None):
            with nc.sbuf_tensor(name + "_parts", split or shape, F32R) as parts:
                pass
            return sb(name, shape), parts

        ring, ring_parts = sb_both("ring", [P, RING, UNIT])
        consts = sb("consts", [P, CONST_N])
        vecs, vecs_parts = sb_both("vecs", [P, VEC_N])
        hT = sb("hT", [P, DC, T])
        x2_flat = sb("x2", [P, DC * T])
        x2 = x2_flat[:, 0:DC * SEQ].rearrange("p (c t) -> p c t", c=DC)
        squares = x2_flat[:, :].rearrange("p (c t) -> p c t", c=DC)
        root = sb("root", [P, T])
        eps = sb("eps", [P, 1])
        eps_root = sb("eps_root", [P, 1])
        n_iter = sb("n_iter", [P, 2], I32)
        small = {n: sb(f"{n}_bf16", [P, P], BF16) for n in ("ident", "ones", "upper", "mask")}
        chosen = sb("chosen", [P, TT, NE], BF16)
        wng_hi = sb("wng_hi", [P, VEC["wng0"]], F32R)
        n_last = sb("n_last", [P, 2], I32)
        arena, arena_parts = sb_both("arena", [P, ARENA], [P, (DC + 48 + 12) * SEQ])
        psum = ctx.enter_context(nc.psum_tensor("banks", [P, 8, 512], F32))
        flat = psum[:, :, :].rearrange("p b n -> p (b n)")

        def C(name):
            a, n = CONST_AT[name]
            return consts[:, a:a + n]

        def V(name, of=vecs):
            a, n = VEC_AT[name]
            return of[:, a:a + n]

        class Place:

            def __init__(self, at=0, of=None):
                self.at, self.of = at, arena if of is None else of

            def __call__(self, *shape):
                n = 1
                for k in shape:
                    n *= k
                v = self.of[:, self.at:self.at + n]
                self.at += n
                assert self.at <= ARENA, self.at
                if len(shape) == 2:
                    v = v.rearrange("p (a b) -> p a b", a=shape[0])
                if len(shape) == 3:
                    v = v.rearrange("p (a b c) -> p a b c", a=shape[0], b=shape[1])
                return v

        small_set = sem("small_set")
        eps_set, const_in, late_in = (sem(n) for n in ("eps_set", "const_in", "late_in"))
        tokens_in = [sem("first_tokens_in"), sem("tokens_in")]
        landed = [sem(f"landed{s}") for s in range(PAIRS_OF_SLOTS)]
        w_hi, w_ready = sem("w_hi"), sem("w_ready")
        x_hi, x_lo = sem("x_hi"), sem("x_lo")
        nrm_sq, nrm_sum, nrm_root, nrm_out = (sem(n) for n in ("nrm_sq", "nrm_sum", "nrm_root", "nrm_out"))
        dve_chain, act_chain = sem("dve_chain"), sem("act_chain")
        cv_pe, cv_c, cv_y = sem("cv_pe"), sem("cv_c"), sem("cv_y")
        pr_done, pr_add = sem("pr_done"), sem("pr_add")
        MOE = ("landed0 landed1 landed2 landed3 landed4 landed5 landed6 landed7 landed8 landed9 landed10 landed11 used "
               "st_ready stw_ready stw_done prep_done xs_ready sw_ready silu_done h_ready "
               "ht_done ht_ready ya_ready yd_ready cmb_done add_done").split()
        moe_sem = [{n: sem(f"m{layer}_{n}") for n in MOE} for layer in range(2)]
        route = {n: sem(n) for n in "x_gain lg_done r_root r_ready xr_done xr_ready dg_ready exp_done route_ready rank_done iter_ready".split()}
        ml = {n: sem(f"mla_{n}") for n in ("a_done a_copied pj_done pj_copied krot_done kr_ready rot_done q_ready sc_done "
                                           "mx_ready e_done p_ready pt_done pt_copied pv_done o_ready").split()}
        b2 = {n: sem(f"b2_{n}") for n in (
            "lb_d lb_e pj_done pj_copied ng_done gate_ready sig_done lin_ready ln_done lv_d lv_e lv_kq lv_mm lv_at "
            "av_done o_copied osq osum olog oroot o_h rope_done kp_ready crope_done cs_ready ce_done c1_exp c1_ready z_ready "
            "sc_done mx_ready e_done p_ready pt_done pta_copied ptb_copied pv_done o_n "
            "wo_done wo_copied x_new g_hi n_new n_hi n_lo oh_hi oh_lo on_hi on_lo").split()}
        stored = sem("stored")

        more = ARENA - (QU - RING) * UNIT
        more_slots = arena[:, more:].rearrange("p (s n) -> p s n", n=UNIT)
        a = Place()
        cv_yt, cv_yh, cv_n, cv_nh = a(DC, T), a(DC, T), a(DC, T), a(DC, T)
        cv_csb, cv_z, cv_t = a(2, T), a(T + 2), a(T)
        whole_small = a(SMALL_N)
        assert a.at <= more
        a = Place(0, arena_parts)
        y_lo, y_hi, x_lower, x_upper = a(DC, T), a(DC, T), a(DC, T), a(DC, T)
        cv_ns, cv_ys = [x_upper, x_lower], [y_hi, y_lo]
        a = Place(3 * DC * T)
        mo_n, mo_row = a(DC, TP), a(TT, D)
        mo_xs, mo_st, mo_stw, mo_sw = a(DC, P), a(TT, 4, SLOT), a(TT, 4, SLOT), a(TP)
        mo_silu, mo_h, mo_ht, mo_y = a(2 * P), a(2 * P), a(2, P), a(D)
        mo_rank, mo_w, mo_tmp = a(TT, NE), a(TT, NE), a(TT, NE)
        r8 = [a(TT, 8) for _ in range(10)]
        r1 = [a(TT) for _ in range(10)]
        r_c, r_gt, r_n, r_t, mo_lg = a(1), a(ROUNDS), a(1), a(TT), a(TT, 72)
        assert a.at <= more
        a = Place()
        ml_o, ml_oh = a(HEADS, T), a(HEADS, T)
        ml_kv, ml_q = a(DC, T), a(DC, T)
        ml_kn, ml_qn = ml_kv, ml_q
        upper_at = a.at
        a(DC, T), a(DC, T)
        latent_at = a.at
        ml_ckvn, _, ml_cqn, _ = a(2, T), a(2, T), a(3, T), a(3, T)
        ml_kr, ml_krz = a(T), a(2, T)
        late_at = a.at
        ml_e = [a(3 * P + T), a(3 * P + T)]
        ml_st = [(a(TT), a(TT), a(TT)) for _ in range(2)]
        assert a.at <= more, (a.at, more)
        a = Place()
        ml_ckv, ml_cq, ml_sq = a(2, T), a(3, T), a(5, T)
        assert a.at <= 2 * DC * T
        a = Place(upper_at)
        ml_v = a(TT, D)
        ml_qr = a(HEADS // 2, T)
        assert a.at <= latent_at
        a = Place(latent_at)
        ml_pt = [a(2 * T), a(2 * T)]
        a = Place(late_at)
        ml_rt = a(4, T)
        a = Place(0, arena_parts)
        o_lo, o_hi, kv_lo, q_lo, kv_hi, q_hi = (a(DC, T) for _ in range(6))
        c_lo, c_hi, d_lo, d_hi = a(2, T), a(2, T), a(3, T), a(3, T)
        ml_os, ml_kvs, ml_qs, ml_ckvs, ml_cqs = [o_hi, o_lo], [kv_hi, kv_lo], [q_hi, q_lo], [c_hi, c_lo], [d_hi, d_lo]
        a = Place()
        b_at_0 = a.at
        b_n, b_p, b_v = a(DC, SEQ), a(48, SEQ), a(6, 2, SEQ)
        over = a.at
        b_g, b_k, b_b, b_ke, b_qe = (a(HEADS, SEQ) for _ in range(5))
        b_at = a(PAIRS, P)
        n_rt = a(2, SEQ)
        n_c1, n_ce = [a(2, NCMP), a(2, NCMP)], a(2, NCMP)
        b_d = hT[:, :, :].rearrange("p c t -> p (c t)")[:, 0:HEADS * SEQ]
        c1_parts = [x[:, HEADS * SEQ:HEADS * SEQ + P] for x in (hT[:, :, :].rearrange("p c t -> p (c t)"), x2_flat)]
        ax = VEC_AT["wr0"][0]
        b_ax = vecs[:, ax:ax + HEADS * P].rearrange("p (h t) -> p h t", h=HEADS)
        a = Place(ax + HEADS * P, vecs)
        b_lb, b_lbi, b_lbt, b_bl, n_gate = a(2, 8), a(2, 8), a(2, 8), a(8), a(2, 24)
        assert a.at <= VEC_N
        a = Place(b_at_0, arena_parts)
        n_parts, p_parts, v_parts = a(DC, SEQ), a(48, SEQ), a(12, SEQ)
        b_ns = [p_parts[:, F_F:F_F + DC, :], n_parts]
        b_ohs = [p_parts[:, F_Q:F_Q + HEADS, :], p_parts[:, F_HZ:F_HZ + HEADS, :]]
        b_ons = [v_parts[:, 0:HEADS, :], p_parts[:, F_NZ:F_NZ + HEADS, :]]
        a = Place(over)
        n_kp = [a(32, 2, NCMP), a(32, 2, NCMP)]
        assert a.at <= over + HEADS * SEQ
        a = Place(over)
        n_kc, n_vc, n_crt = a(2, NCMP), a(2, P), a(2, NCMP)
        a = Place(over + HEADS * SEQ)
        n_e = [a(2, 3 * P) for _ in range(2)]
        n_pt = [a(2, 4 * P) for _ in range(2)]
        n_st = [(a(4), a(4), a(4)) for _ in range(2)]
        n_cs, n_cmx, n_csum = a(2, HEADS * NCMP), a(2 * HEADS), a(2 * HEADS)
        assert a.at <= over + 3 * HEADS * SEQ

        def wide(v):
            return v.rearrange("p a b -> p (a b)")

        block = ctx.enter_context(nc.Block())

        @block.sync
        def _(sp):
            first_c, first_v = CONST_AT["iota"][0], VEC_AT["kvg"][0]
            sp.dma_start(consts[:, 0:first_c], consts_in[:, 0:first_c]).then_inc(const_in, 16)
            sp.dma_start(vecs[:, 0:first_v], vecs_in[:, 0:first_v]).then_inc(const_in, 16)
            half = DC // 2 * T
            for n, x in enumerate(tokens_in):
                sp.dma_start(wide(hT[:, :, :])[:, n * half:n * half + half], h_in[:, n * half:n * half + half]).then_inc(x, 16)
            free = [None] * RING
            n_dense = 0

            def load_dense(*uses):
                nonlocal n_dense
                for use in uses:
                    slot = n_dense % PAIRS_OF_SLOTS
                    if free[PAIRS_OF_SLOTS + slot]:
                        sp.wait_ge(*free[PAIRS_OF_SLOTS + slot])
                    sp.dma_start(ring[:, slot, :], dense[n_dense]).then_inc(landed[slot], 16)
                    n_dense += 1
                    free[slot] = free[PAIRS_OF_SLOTS + slot] = use

            free_more = [None] * (QU - RING)

            def experts_first(layer, units):
                for u in units:
                    slot = u if u < RING else u - RING
                    use = (free if u < RING else free_more)[slot]
                    if use:
                        sp.wait_ge(*use)
                    to = ring[:, slot, :] if u < RING else more_slots[:, slot, :]
                    sp.dma_start(to, experts[layer, 0, u]).then_inc(moe_sem[layer][f"landed{u}"], 16)

            def load_experts(layer):
                m = moe_sem[layer]
                experts_first(layer, range(RING))
                sp.wait_ge(route["iter_ready"], layer + 1)
                last = sp.value_load(n_last[0:1, layer:layer + 1], min_val=QUADS - 1, max_val=QUADS * ROUNDS - 1)
                with sp.Fori(0, last) as i:
                    for u in range(QU):
                        sp.wait_ge(m["used"], i * QU + (u + 1))
                        to = ring[:, u, :] if u < RING else more_slots[:, u - RING, :]
                        sp.dma_start(to, experts[layer, (i + 1) % QUADS, u]).then_inc(m[f"landed{u}"], 16)
                for u in range(QU):
                    use = (m["used"], last * QU + (u + 1))
                    if u < RING:
                        free[u] = use
                    else:
                        free_more[u - RING] = use

            load_dense(*[(cv_pe, 2 * u + 2) for u in range(PAIRS_OF_SLOTS)])
            sp.dma_start(consts[:, first_c:], consts_in[:, first_c:CONST_N]).then_inc(late_in, 16)
            sp.dma_start(whole_small, consts_in[:, CONST_N:]).then_inc(late_in, 16)
            sp.dma_start(vecs[:, first_v:], vecs_in[:, first_v:]).then_inc(late_in, 16)
            for u in range(PAIRS_OF_SLOTS, 12):
                load_dense((cv_pe, 2 * u + 2))
                if u < PAIRS_OF_SLOTS + QU - RING:
                    experts_first(0, [RING + u - PAIRS_OF_SLOTS])
            load_dense(*[(pr_done, 2 * u + 2) for u in range(4)])
            load_experts(0)
            load_dense(*[(ml["a_done"], u + 1) for u in range(3)])
            experts_first(1, range(RING, QU))
            load_dense(*[(ml["pj_done"], n) for n in (8, 14, 18, 23, 26)])
            load_dense(*[(pr_done, 8 + 2 * u + 2) for u in range(4)])
            load_experts(1)
            for layer in range(2):
                for what, n in MAKES:
                    made = (b2["pj_done"], LAYER_TILES * layer + MADE[what, n])
                    if what in ("unit", "c1"):
                        load_dense(made)
                load_dense(*[(b2["wo_done"], 16 * layer + 2 * u + 2) for u in range(8)])
            for c in range(0, DC, 2):
                sp.wait_ge(b2["x_new"], 2 * DC + c + 2)
                sp.dma_start(out[:, c * SEQ:(c + 2) * SEQ], wide(x2[:, c:c + 2, :])).then_inc(stored, 16)
            sp.wait_ge(stored, 16 * DC // 2)

        @block.tensor
        def _(pe):
            t = Turns(pe)
            n_unit, n_res, n_tile, n_split = 0, 0, 0, 0

            def mm(o, lhsT, rhs, k, n):
                return pe.matmul(o, lhsT, rhs, start=(k == 0), stop=(k == n - 1))

            def mm3(o, lhsT, rhs, k, n):
                pe.matmul(o, lhsT[0], rhs[0], start=(k == 0), stop=False)
                pe.matmul(o, lhsT[0], rhs[1], start=False, stop=False)
                return pe.matmul(o, lhsT[1], rhs[0], start=False, stop=(k == n - 1))

            def whole_unit(a, b):
                nonlocal n_unit
                slot, n_unit = n_unit % PAIRS_OF_SLOTS, n_unit + 1
                pe.wait_ge(landed[slot], 16 * ((n_unit - 1) // PAIRS_OF_SLOTS + 1))
                return ring[:, slot, 0:a * b].rearrange("p (a b) -> p a b", a=a)

            def unit(a, b, begun=False):
                nonlocal n_unit, n_split
                slot, n_unit, n_split = n_unit % PAIRS_OF_SLOTS, n_unit + 1, n_split + 1
                pe.wait_ge(w_ready, 2 * n_split - begun)
                return [ring_parts[:, x, 0:a * b].rearrange("p (a b) -> p a b", a=a) for x in (PAIRS_OF_SLOTS + slot, slot)]

            def rest(half, k):
                if half == 0 and k == DC // 2:
                    pe.wait_ge(w_ready, 2 * n_split)

            def both(views, *index):
                return [x[(slice(None), *index)] for x in views]

            every = slice(None)

            def norm_sum(sq, n, w, bank):
                for c in range(n):
                    t.next(nrm_sq)
                    m = mm(psum[:, bank, 0:w], C("ones"), sq[:, c, :], c, n)
                m.then_inc(nrm_sum, 1)

            def keep_clock(bank, n):
                for _ in range(n):
                    mm(psum[:, bank, :], C("ones"), consts[:, 0:512], 0, 1)

            def split(n):
                for _ in range(n):
                    t.next(x_lo)
                    yield

            def logits(layer, k):
                if k == 0:
                    pe.wait_ge(moe_sem[layer]["sw_ready"], 1)
                    mm(psum[:, 0, 0:TT * 73], C("ident"), mo_sw[:, 0:TT * 73], 0, 2)
                wr = V(f"wr{layer}").rearrange("p (k n) -> p k n", k=8)
                t.next(route["x_gain"])
                for i in range(TT):
                    pe.matmul(psum[:, 0, i * 72:i * 72 + 72], mo_n[:, k, i * P:i * P + P], wr[:, k, :],
                              start=False, stop=False)
                t.next(nrm_sq)
                for i in range(TT):
                    n = min(P, T - i * P)
                    m = pe.matmul(psum[0:n, 0, TT * 72 + i:TT * 72 + i + 1], squares[:, k, i * P:i * P + n], C("ones")[:, 0:1],
                                  start=False, stop=False)
                if k == 7:
                    m = mm(psum[:, 0, 0:TT * 73], C("ident"), mo_sw[:, 0:TT * 73], 1, 2)
                return m

            def residual(layer, src):
                nonlocal n_res
                if layer == 0:
                    t.next(late_in, 48)
                    t.next(small_set, 4)
                ready = split(DC)
                for u in range(4):
                    w = unit(8, 256, begun=True)
                    for half in range(2):
                        if n_res >= 2:
                            pe.wait_ge(pr_add, n_res - 1)
                        for k in range(8):
                            rest(half, k)
                            next(ready, None)
                            m = mm3(psum[:, 6 + n_res % 2, 0:T], both(w, k, slice(half * P, half * P + P)), both(src, k, every), k, 8)
                        m.then_inc(pr_done, 1)
                        n_res += 1
                        if 2 * u + half >= 2:
                            logits(layer, 2 * u + half - 2)
                logits(layer, DC - 2)
                logits(layer, DC - 1).then_inc(route["lg_done"], 1)

            def conv():
                t.next(const_in, 32)
                norm_sum(squares, DC, T, 7)
                ready = split(DC)
                for j in range(4):
                    for part in range(3):
                        w = unit(8, 256, begun=True)
                        for half in range(2):
                            if j and part == 0:
                                pe.wait_ge(cv_y, 2 * (j - 1) + half + 1)
                            for k in range(8):
                                rest(half, k)
                                next(ready, None)
                                m = mm3(psum[:, 3 * half + part, 0:T], both(w, k, slice(half * P, half * P + P)), both(cv_ns, k, every), k, 8)
                            m.then_inc(cv_pe, 1)
                t.next(cv_y, 8)
                residual(0, cv_ys)

            def moe(layer):
                s = moe_sem[layer]
                for i in range(TT):
                    for c in range(DC):
                        at = 512 + i * D + c * P
                        m = pe.transpose(flat[:, at:at + P], mo_n[:, c, i * P:i * P + P], C("ident"))
                m.then_inc(route["xr_done"], 1)
                keep_clock(7, 3)
                pe.wait_ge(route["route_ready"], layer + 1)
                for i in range(TT + 1):
                    n = min(i, TT - 1) + 1
                    for j in range(n):
                        m = mm(psum[:, 7, i * NE:i * NE + NE], small["upper" if j == i else "ones"][:, :], chosen[:, j, :], j, n)
                m.then_inc(route["rank_done"], 1)
                pe.wait_ge(route["xr_ready"], layer + 1)

                def prep(n):
                    pe.wait_ge(s["st_ready"], n)
                    for c in range(DC):
                        for i in range(TT):
                            m = mm(flat[:, c * P:c * P + P], mo_row[:, i, c * P:c * P + P], wide(mo_st[:, i]), i, TT)
                    m.then_inc(s["prep_done"], 1)

                def combine(i):
                    pe.wait_ge(s["ya_ready"], i + 1)
                    pe.wait_ge(s["yd_ready"], i + 1)
                    pe.wait_ge(s["sw_ready"], i + 1)
                    for c in range(DC):
                        pe.wait_ge(s["add_done"], i * DC + (c if c >= 2 else 1))
                        pe.matmul(psum[:, 6 + c % 2, 0:T], mo_y[:, c * P:c * P + P], mo_sw[:, 0:T],
                                  start=True, stop=True).then_inc(s["cmb_done"], 1)

                prep(1)
                pe.wait_ge(route["iter_ready"], layer + 1)
                n = pe.value_load(n_iter[0:1, layer:layer + 1], min_val=QUADS, max_val=QUADS * ROUNDS)
                with pe.Fori(0, n) as i:
                    def weights(u):
                        pe.wait_ge(s[f"landed{u}"], i * 16 + 16)
                        slot = ring[:, u, :] if u < RING else more_slots[:, u - RING, :]
                        return slot.rearrange("p (e n) -> p e n", e=4)

                    pe.wait_ge(s["xs_ready"], i + 1)
                    for k in range(8):
                        w = weights(k)
                        for e in range(4):
                            m = pe.matmul(psum[32 * e:32 * e + 32, 3, :], mo_xs[:, k, 32 * e:32 * e + 32], w[:, e, :],
                                          start=(k == 0), stop=(k == 7), tile_position=(0, 32 * e))
                        m.then_inc(s["used"], 1)
                    prep(i + 2)
                    pe.wait_ge(s["h_ready"], i + 1)
                    for k in range(2):
                        m = pe.transpose(psum[:, 3, k * P:k * P + P], mo_h[:, k * P:k * P + P], C("ident"))
                    m.then_inc(s["ht_done"], 1)
                    combine(i)
                    pe.wait_ge(s["stw_ready"], i + 1)
                    for j in range(TT):
                        m = pe.transpose(psum[:, 2, j * P:j * P + P], wide(mo_stw[:, j]), C("ident"))
                    m.then_inc(s["stw_done"], 1)
                    pe.wait_ge(s["ht_ready"], i + 1)
                    for half in range(2):
                        for k in range(2):
                            w = weights(8 + 2 * half + k)
                            for e in range(4):
                                m = pe.matmul(psum[32 * e:32 * e + 32, 4 + half, :], mo_ht[:, k, 32 * e:32 * e + 32], w[:, e, :],
                                              start=(k == 0), stop=(k == 1), tile_position=(0, 32 * e))
                            m.then_inc(s["used"], 1)
                combine(n)

            def mla():
                norm_sum(squares, DC, T, 5)
                ready = split(DC)
                w = unit(8, 256)
                for c in range(2):
                    for k in range(8):
                        next(ready, None)
                        m = mm3(psum[:, c, 0:T], both(w, k, slice(c * P, c * P + P)), both(ml_kvs, k, every), k, 8)
                m.then_inc(ml["a_done"], 1)
                ready = split(DC)
                w = unit(8, 256)
                for c in range(2):
                    for k in range(8):
                        if c:
                            next(ready, None)
                        m = mm3(psum[:, 2 + c, 0:T], both(w, k, slice(c * P, c * P + P)), both((ml_kvs, ml_qs)[c], k, every), k, 8)
                m.then_inc(ml["a_done"], 1)
                norm_sum(ml_sq[:, 0:2], 2, T, 7)
                w = unit(8, 256)
                for c in range(2):
                    for k in range(8):
                        m = mm3(psum[:, 4 + c, 0:T], both(w, k, slice(c * P, c * P + P)), both(ml_qs, k, every), k, 8)
                m.then_inc(ml["a_done"], 1)
                t.next(ml["a_copied"])
                mm(psum[:, 6, 0:T], C("rotm"), ml_kr, 0, 1).then_inc(ml["krot_done"], 1)
                n_out = 0

                def tile(n=4):
                    nonlocal n_out
                    if n_out >= n:
                        pe.wait_ge(ml["pj_copied"], n_out - n + 1)
                    n_out += 1
                    return 7 if n == 1 else (n_out - 1) % 4

                ready = split(2)
                w = unit(2, D)
                for h in range(HEADS):
                    b = tile()
                    for k in range(2):
                        next(ready, None)
                        m = mm3(psum[:, b, 0:T], both(w, k, slice(h * P, h * P + P)), both(ml_ckvs, k, every), k, 2)
                    m.then_inc(ml["pj_done"], 1)
                norm_sum(ml_sq[:, 2:5], 3, T, 7)
                w = unit(2, D)
                for i in range(TT):
                    n = min(P, T - i * P)
                    for half in range(2):
                        b = tile()
                        for k in range(2):
                            m = mm3(psum[0:n, b, :], both(ml_ckvs, k, slice(i * P, i * P + n)), both(w, k, slice(half * 512, half * 512 + 512)), k, 2)
                        m.then_inc(ml["pj_done"], 1)
                ready = split(3)
                w = unit(3, 512)
                for h in range(HEADS // 2):
                    b = tile()
                    for k in range(3):
                        next(ready, None)
                        m = mm3(psum[:, b, 0:T], both(w, k, slice(h * P, h * P + P)), both(ml_cqs, k, every), k, 3)
                    m.then_inc(ml["pj_done"], 1)
                heads = [(h, 5) for h in range(5)] + [(h, 3) for h in range(3)]

                def queries(h, n=4):
                    nonlocal w
                    at, of = heads[h]
                    if at == 0:
                        w = unit(3, of * P)
                    b = tile(n)
                    for k in range(3):
                        m = mm3(psum[:, b, 0:T], both(w, k, slice(at * P, at * P + P)), both(ml_cqs, k, every), k, 3)
                    m.then_inc(ml["pj_done"], 1)

                queries(0)
                queries(1)
                t.next(ml["pj_copied"], 18)
                t.next(ml["kr_ready"])
                for h in range(HEADS // 2):
                    m = mm(psum[:, 4 + h, 0:T], C("rotm"), ml_qr[:, h, :], 0, 1)
                m.then_inc(ml["rot_done"], 1)
                queries(2)
                t.next(ml["pj_copied"], 3)
                t.next(ml["q_ready"])
                def scores(h):
                    if h >= 2:
                        pe.wait_ge(ml["e_done"], h - 1)
                        pe.wait_ge(ml["pj_copied"], 19 + h)
                    for i in range(TT):
                        n, keys = min(P, T - i * P), min(T, i * P + P)
                        b, at = 2 * (h % 2) + i // 2, (0, P, 0)[i]
                        o, q = psum[0:n, b, at:at + keys], slice(i * P, i * P + n)
                        mm(o, ml_qn[:, h, q], ml_kn[:, h, 0:keys], 0, 3)
                        mm(o, ml_qr[:, h // 2, q], ml_krz[:, h % 2, 0:keys], 1, 3)
                        m = pe.matmul(psum[0:n, b, at + i * P:at + i * P + n], small["ident"][:, 0:n], small["mask"][:, 0:n],
                                      start=False, stop=True)
                    m.then_inc(ml["sc_done"], 1)

                scores(0)
                scores(1)
                t.next(ml["q_ready"])
                for h in range(HEADS):
                    pe.wait_ge(ml["p_ready"], h + 1)
                    for j in range(TT):
                        n = min(P, T - j * P)
                        for i in range(j, TT):
                            rows = min(P, T - i * P)
                            at = (0, T, 2 * T - P)[j] + (i - j) * P
                            e = (0, P, 3 * P)[i] + j * P
                            m = pe.transpose(psum[0:n, 4 + h % 2, at:at + rows], ml_e[h % 2][0:rows, e:e + n],
                                             C("ident")[0:rows, 0:rows])
                    m.then_inc(ml["pt_done"], 1)
                    if h + 3 < HEADS:
                        queries(h + 3, 1)
                    if h + 2 < HEADS:
                        scores(h + 2)
                    pe.wait_ge(ml["pt_copied"], 2 * h + 2)
                    if h:
                        pe.wait_ge(ml["o_ready"], h)
                    for j in range(TT):
                        n = min(P, T - j * P)
                        at = (0, T, 2 * T - P)[j]
                        m = mm(psum[:, 6, j * P:T], ml_v[0:n, j, h * P:h * P + P], ml_pt[h % 2][0:n, at:at + T - j * P], j, TT)
                    m.then_inc(ml["pv_done"], 1)
                t.next(ml["o_ready"], HEADS)
                residual(1, ml_os)

            def layer2(layer):
                nonlocal n_tile
                first_tile = n_tile
                norm_sum(b_qe, DC, SEQ, 7)
                fresh = [True] * DC
                w = None

                def normed_2(k):
                    if fresh[k]:
                        t.next(b2["n_lo"])
                        fresh[k] = False

                def bank(only=None):
                    nonlocal n_tile
                    n_tile += 1
                    if only is None:
                        if n_tile > 4:
                            pe.wait_ge(b2["pj_copied"], n_tile - 4)
                        return (n_tile - 1 - first_tile) % 4
                    free = n_tile - (1 if only == 7 else 2)
                    pe.wait_ge(b2["pj_copied"], free)
                    return only

                def tile(u, half, only=None):
                    nonlocal w
                    if half == 0:
                        w = unit(8, 256, begun=True)
                    o = psum[:, bank(only), 0:SEQ]
                    cut = slice(half * P, half * P + P)
                    for k in range(8):
                        rest(half, k)
                        normed_2(k)
                        if UNITS_2[u][0] == "v":
                            m = mm3(o, both(b_ns, k, cut), both(w, k, every), k, 8)
                        else:
                            m = mm3(o, both(w, k, cut), both(b_ns, k, every), k, 8)
                    m.then_inc(b2["pj_done"], 1)

                def make(what, n):
                    if what == "unit":
                        tile(n, 0)
                        tile(n, 1)
                        return
                    if what == "rot":
                        pe.wait_ge(b2["pj_copied"], first_tile + MADE["unit", n])
                        src = b_p[0:32, UNITS_2[n][1]:UNITS_2[n][1] + 2, :]
                        m = mm(psum[0:32, bank(), :], C("rotn")[0:32, :], wide(src), 0, 1)
                    if what == "c1":
                        b = bank()
                        kv, part = n // 2, n % 2
                        if part == 0:
                            t.next(b2["kp_ready"])
                        v = whole_unit(16, P)
                        for k in range(16):
                            e = k % 4
                            m = pe.matmul(psum[SLOT * e:SLOT * e + 2 * NCMP, b, 0:P], wide(n_kp[kv][:, 16 * part + k]), v[:, k, :],
                                          start=(k < 4), stop=(k >= 12), tile_position=(0, SLOT * e))
                    if what == "c1sum":
                        o = psum[:, bank(), 0:2 * NCMP]
                        pe.wait_ge(b2["pj_copied"], first_tile + MADE["c1", 2 * n + 1])
                        for part in range(2):
                            m = mm(o, c1_parts[part], C("stack"), part, 2)
                    if what == "c2":
                        o = psum[:, bank(), :]
                        t.next(b2["c1_ready"])
                        if n == 0:
                            m = mm(o[:, 0:2 * NCMP], V(f"w2k{layer}"), wide(n_c1[0]), 0, 1)
                        else:
                            for g in range(2):
                                m = mm(o[0:NCMP, g * P:g * P + P], n_c1[1][:, g, :], V(f"w2v{layer}"), 0, 1)
                    if what == "crot":
                        o = psum[0:32, bank(), 0:2 * NCMP]
                        pe.wait_ge(b2["pj_copied"], first_tile + MADE["c2", 0])
                        m = mm(o, C("rotn")[0:32, :], wide(n_kc[0:32]), 0, 1)
                    m.then_inc(b2["pj_done"], 1)

                for m in FIRST[:4]:
                    make(*m)
                wng = [x.rearrange("p (k n) -> p k n", k=8) for x in (wng_hi[:, :], V(f"wng{layer}", vecs_parts))]
                for i in range(2):
                    for k in range(8):
                        m = mm3(psum[:, 4, i * 24:i * 24 + 24], both(b_ns, k, slice(i * P, i * P + P)), both(wng, k, every), k, 8)
                m.then_inc(b2["ng_done"], 1)
                for m in FIRST[4:]:
                    make(*m)
                t.next(b2["gate_ready"])
                for job in range(9):
                    for m in JOBS[job]:
                        make(*m)
                    for part in range(2):
                        heads = range(4 * part, 4 * part + 4)
                        if job:
                            pe.wait_ge(b2["lv_at"], 18 * layer + 2 * job - (part == 0 and job < 8))
                        if job < 8:
                            t.next(b2["lv_kq"])
                        keys, queries = (b_ke, b_qe) if job < 8 else (b_k, b_p[:, F_Q:F_Q + HEADS])
                        for h in heads:
                            if job == 7:
                                m = mm(flat[:, 2048 + h * P:2048 + h * P + P], b_ke[:, h, 0:P], b_qe[:, h, P:SEQ], 0, 1)
                                continue
                            for i in range(2):
                                at = 2048 + (2 * h + i) * P
                                m = mm(flat[:, at:at + P], keys[:, h, i * P:i * P + P], queries[:, h, i * P:i * P + P], 0, 1)
                        m.then_inc(b2["lv_mm"], 1)
                def scores(h):
                    if h >= 2:
                        pe.wait_ge(b2["e_done"], HEADS * layer + h - 1)
                    for br, keys in ((0, F_KS), (1, F_KW)):
                        k = b_p[:, keys + h // 4, :]
                        for i, at, n in ((0, 0, P), (1, P, SEQ)):
                            b = 2 * (h % 2) + br
                            mm(psum[:, b, at:at + n], b_p[:, F_NQ + h, i * P:i * P + P], k[:, 0:n], 0, 2)
                            m = pe.matmul(psum[:, b, at + n - P:at + n], small["ident"][:, :], small["mask"][:, :], start=False, stop=True)
                    m.then_inc(b2["sc_done"], 1)

                t.next(b2["rope_done"], 6)
                t.next(b2["crope_done"])
                pe.wait_ge(b2["pj_copied"], n_tile)
                for i in range(2):
                    for h in range(HEADS):
                        m = mm(psum[:, i, 3 * P + h * NCMP:3 * P + (h + 1) * NCMP], b_p[:, F_NQ + h, i * P:i * P + P],
                               n_kc[:, h // 4, :], 0, 1)
                scores(0)
                tile(BEFORE_HEADS[0][1], 0, 2)
                tile(BEFORE_HEADS[0][1], 1, 3)
                t.next(b2["lv_at"], 18)
                for h in range(HEADS):
                    v = [b_v[:, h // 2, i, (h % 2) * P:(h % 2) * P + P] for i in range(2)]
                    at = 2048 + h * SEQ
                    mm(flat[:, at:at + P], v[0], b_at[:, 2 * h, :], 0, 1)
                    mm(flat[:, at + P:at + SEQ], v[0], b_ax[:, h, :], 0, 2)
                    m = mm(flat[:, at + P:at + SEQ], v[1], b_at[:, 2 * h + 1, :], 1, 2)
                m.then_inc(b2["av_done"], 1)
                tile(BEFORE_HEADS[1][1], 0, 2)
                tile(BEFORE_HEADS[1][1], 1, 3)
                t.next(b2["osq"])
                for i in range(4):
                    m = mm(psum[:, 4 + i, :], C("ones"), b_d[:, i * 512:i * 512 + 512], 0, 1)
                m.then_inc(b2["osum"], 1)

                pe.wait_ge(b2["pj_copied"], n_tile)
                scores(1)
                t.next(b2["olog"])

                def part_out(u, half, source, b):
                    nonlocal w
                    if half == 0:
                        w = unit(8, 256, begun=True)
                    for k in range(8):
                        rest(half, k)
                        if source and u == half == 0:
                            t.next(b2["on_lo"])
                        m = mm3(psum[:, b, 0:SEQ], both(w, k, slice(half * P, half * P + P)),
                                both((b_ohs, b_ons)[source], k, every), 8 * source + k, 16)
                    m.then_inc(b2["wo_done"], 1)

                def beside(h, half):
                    if h < len(IN_HEADS):
                        tile(IN_HEADS[h][1], half, 7)
                    elif half:
                        if h == len(IN_HEADS):
                            t.next(b2["oh_lo"], 4)
                        u = h - len(IN_HEADS)
                        part_out(u, 0, 0, 2 * u)
                        part_out(u, 1, 0, 2 * u + 1)

                for h in range(HEADS):
                    g, n = h // 4, HEADS * layer + h
                    e, pt = n_e[h % 2], n_pt[h % 2]
                    beside(h, 0)
                    pe.wait_ge(b2["p_ready"], n + 1)
                    for br in range(2):
                        b = 4 + br
                        pe.transpose(psum[:, b, 0:P], e[:, br, 0:P], C("ident"))
                        pe.transpose(psum[:, b, P:2 * P], e[:, br, P:2 * P], C("ident"))
                        pe.transpose(psum[:, b, 2 * P:3 * P], e[:, br, 2 * P:3 * P], C("ident"))
                        m = pe.transpose(psum[0:NCMP, b, 3 * P:4 * P], n_cs[:, br, h * NCMP:h * NCMP + NCMP], C("ident"))
                    m.then_inc(b2["pt_done"], 1)
                    if h + 2 < HEADS:
                        scores(h + 2)
                    beside(h, 1)
                    pe.wait_ge(b2["pta_copied"], 2 * n + 2)
                    pe.wait_ge(b2["ptb_copied"], 2 * n + 2)
                    if h:
                        pe.wait_ge(b2["o_n"], n)
                    o = psum[:, 6, 0:SEQ]
                    cut = slice(g * P, g * P + P)
                    mm(o, b_v[:, 4, 0, cut], pt[:, 0, 0:SEQ], 0, 6)
                    mm(o, b_v[:, 5, 0, cut], pt[:, 1, 0:SEQ], 1, 6)
                    mm(o[:, P:SEQ], b_v[:, 4, 1, cut], pt[:, 0, SEQ:SEQ + P], 2, 6)
                    mm(o[:, P:SEQ], b_v[:, 5, 1, cut], pt[:, 1, SEQ:SEQ + P], 3, 6)
                    for i in range(2):
                        m = mm(o[:, i * P:i * P + P], n_vc[0:NCMP, g, :], pt[0:NCMP, i, 3 * P:4 * P], 4 + i, 6)
                    m.then_inc(b2["pv_done"], 1)
                for u in range(2, 4):
                    if u == 3:
                        t.next(b2["o_n"], HEADS)
                        pe.wait_ge(b2["pj_copied"], n_tile)
                    part_out(u, 0, 0, 2 * u)
                    part_out(u, 1, 0, 2 * u + 1)
                for u in range(4):
                    part_out(u, 0, 1, 2 * u)
                    part_out(u, 1, 1, 2 * u + 1)
                pe.wait_ge(b2["wo_copied"], DC * layer + 1)
                norm_sum(b_qe, DC, SEQ, 0)
                if layer == 0:
                    keep_clock(1, 4)

            conv()
            moe(0)
            mla()
            moe(1)
            norm_sum(squares[:, :, 0:SEQ], DC, SEQ, 0)
            keep_clock(2, 4)
            layer2(0)
            layer2(1)

        @block.scalar
        def _(act):
            t = Chain(act, act_chain)

            def square(o, i):
                act.activation(o, i, ACT.Square).then_inc(nrm_sq, 1)

            def root_table():
                act.activation(eps_root[:, :], eps[:, :], ACT.Sqrt)

            def norm_root(n, w, bank, loaded=False):
                if not loaded:
                    root_table()
                t.next(nrm_sum)
                act.activation(root[:, 0:w], psum[:, bank, 0:w], ACT.Sqrt, scale=1.0 / n, bias=eps[:, :]).then_inc(nrm_root, 1)

            def copy(o, i):
                return act.activation(o, i, ACT.Copy)

            to_split = [*range(FIRST_2), *splits_2(0), *splits_2(1)]

            def upper(last):
                while to_split and to_split[0] <= last:
                    n = to_split.pop(0)
                    slot = n % PAIRS_OF_SLOTS
                    act.wait_ge(landed[slot], 16 * (n // PAIRS_OF_SLOTS + 1))
                    copy(ring_parts[:, PAIRS_OF_SLOTS + slot, :], ring[:, slot, :]).then_inc(w_hi, 1)

            def upper_chunk(parts, whole, c):
                copy(parts[0][:, c, :], whole[:, c, :]).then_inc(x_hi, 1)

            def conv():
                for c in range(DC):
                    if c % (DC // 2) == 0:
                        t.next(tokens_in[c // (DC // 2)], 16)
                    square(squares[:, c, :], hT[:, c, :])
                t.next(eps_set)
                root_table()
                upper(0)
                norm_root(D, T, 7, loaded=True)
                upper(1)
                for c in range(DC):
                    t.next(nrm_out)
                    upper_chunk(cv_ns, cv_n, c)
                for j in range(4):
                    upper(3 * j + 3)
                    for half in range(2):
                        act.wait_ge(cv_pe, 6 * j + 3 + half)
                        copy(cv_csb[:, half, :], psum[:, 3 * half + 1, 0:T]).then_inc(cv_c, 1)
                    for half in range(2 if j else 0):
                        t.next(cv_y)
                        upper_chunk(cv_ys, cv_yt, 2 * j - 2 + half)
                    upper(3 * j + 4)
                for half in range(2):
                    t.next(cv_y)
                    upper_chunk(cv_ys, cv_yt, DC - 2 + half)

            def moe(layer):
                s = moe_sem[layer]
                after = (CONV_UNITS, FIRST_2)[layer]
                for c in range(DC):
                    upper(min(after - 2 + c // 2, after - 1))
                    t.next(pr_add)
                    square(squares[:, c, :], hT[:, c, :])
                act.wait_ge(route["lg_done"], layer + 1)
                for rows, at, n in ((P, 0, TT - 1), (T - (TT - 1) * P, TT - 1, 1)):
                    m = act.activation(r_t[0:rows, at:at + n], psum[0:rows, 0, TT * 72 + at:TT * 72 + at + n], ACT.Sqrt,
                                       scale=1.0 / D, bias=eps[0:rows, :])
                m.then_inc(route["r_root"], 1)
                for n in range(2):
                    act.wait_ge(route["dg_ready"], 2 * layer + n + 1)
                    act.activation(wide(r8[2 + 4 * n]), wide(r8[1 + 4 * n]), ACT.Exp).then_inc(route["exp_done"], 1)
                act.wait_ge(route["xr_done"], layer + 1)
                for i in range(TT):
                    m = act.activation(mo_row[:, i, :], flat[:, 512 + i * D:512 + i * D + D], ACT.Copy, scale=r_t[:, i:i + 1])
                m.then_inc(route["xr_ready"], 1)

                def tokens(n):
                    act.wait_ge(s["prep_done"], n)
                    copy(wide(mo_xs), flat[:, 0:D]).then_inc(s["xs_ready"], 1)

                tokens(1)
                act.wait_ge(route["iter_ready"], layer + 1)
                n = act.value_load(n_iter[0:1, layer:layer + 1], min_val=QUADS, max_val=QUADS * ROUNDS)
                with act.Fori(0, n) as i:
                    act.wait_ge(s["used"], i * QU + 8)
                    act.activation(mo_silu[:, :], psum[:, 3, 0:256], ACT.Silu).then_inc(s["silu_done"], 1)
                    tokens(i + 2)
                    act.wait_ge(s["stw_done"], i + 2)
                    copy(mo_sw[:, :], psum[:, 2, 0:TP]).then_inc(s["sw_ready"], 1)
                    act.wait_ge(s["used"], i * QU + 10)
                    copy(mo_y[:, 0:512], psum[:, 4, :]).then_inc(s["ya_ready"], 1)

                for c in range(DC):
                    act.wait_ge(s["add_done"], n * DC + (c + 2))
                    if layer:
                        square(squares[:, c, 0:SEQ], hT[:, c, META:T])
                    else:
                        square(squares[:, c, :], hT[:, c, :])

            def mla():
                upper(CONV_UNITS)
                norm_root(D, T, 5)
                upper(CONV_UNITS + 1)
                for parts, whole in ((ml_kvs, ml_kv), (ml_qs, ml_q)):
                    for c in range(DC):
                        t.next(nrm_out)
                        upper_chunk(parts, whole, c)
                u = CONV_UNITS
                upper(u + 2)
                t.next(ml["a_done"])
                for i in range(2):
                    copy(ml_ckv[:, i, :], psum[:, i, 0:T])
                    square(ml_sq[:, i, :], psum[:, i, 0:T])
                upper(u + 3)
                t.next(ml["a_done"])
                copy(ml_kr[:, :], psum[:, 2, 0:T])
                copy(ml_cq[:, 2, :], psum[:, 3, 0:T]).then_inc(ml["a_copied"], 1)
                norm_root(256, T, 7)
                for c in range(2):
                    t.next(nrm_out)
                    upper_chunk(ml_ckvs, ml_ckvn, c)
                upper(u + 4)
                t.next(ml["a_done"])
                t.next(ml["a_copied"])
                for i in range(2):
                    copy(ml_cq[:, i, :], psum[:, 4 + i, 0:T])
                    square(ml_sq[:, 2 + i, :], psum[:, 4 + i, 0:T])
                square(ml_sq[:, 4, :], ml_cq[:, 2, :])
                to = [(ml_kn[:, h, :], P, T) for h in range(HEADS)]
                to += [(ml_v[0:min(P, T - i * P), i, half * 512:half * 512 + 512], min(P, T - i * P), 512)
                       for i in range(TT) for half in range(2)]
                to += [(ml_qr[:, h, :], P, T) for h in range(HEADS // 2)]
                to += [(ml_qn[:, h, :], P, T) for h in range(HEADS)]
                n_out = 0

                def copy_next(only=None):
                    nonlocal n_out
                    if n_out in (3, 12, 17, 20, 24):
                        upper(u + 5 + (3, 12, 17, 20, 24).index(n_out))
                    o, rows, w = to[n_out]
                    t.next(ml["pj_done"])
                    copy(o, psum[0:rows, n_out % 4 if only is None else only, 0:w]).then_inc(ml["pj_copied"], 1)
                    n_out += 1

                def exps(h):
                    _, least, total = ml_st[h % 2]
                    t.next(ml["mx_ready"])
                    for i in range(TT):
                        n, keys = min(P, T - i * P), min(T, i * P + P)
                        b, at, to_ = 2 * (h % 2) + i // 2, (0, P, 0)[i], (0, P, 3 * P)[i]
                        m = act.activation(ml_e[h % 2][0:n, to_:to_ + keys], psum[0:n, b, at:at + keys], ACT.Exp,
                                           scale=MLA_SCALE, bias=least[0:n, i:i + 1], accum_out=total[0:n, i:i + 1])
                    m.then_inc(ml["e_done"], 1)

                for k in range(21):
                    if k == HEADS:
                        norm_root(384, T, 7)
                        for c in range(3):
                            t.next(nrm_out)
                            upper_chunk(ml_cqs, ml_cqn, c)
                    copy_next()
                exps(0)
                exps(1)
                for h in range(HEADS):
                    t.next(ml["pt_done"])
                    pt, b = ml_pt[h % 2], 4 + h % 2
                    copy(pt[:, 0:2 * T - P], psum[:, b, 0:2 * T - P]).then_inc(ml["pt_copied"], 1)
                    n = T - 2 * P
                    copy(pt[0:n, 2 * T - P:2 * T - P + n], psum[0:n, b, 2 * T - P:2 * T - P + n]).then_inc(ml["pt_copied"], 1)
                    if h + 3 < HEADS:
                        copy_next(7)
                    if h + 2 < HEADS:
                        exps(h + 2)
                    t.next(ml["pv_done"])
                    copy(ml_os[0][:, h, :], psum[:, 6, 0:T])
                    copy(ml_o[:, h, :], psum[:, 6, 0:T]).then_inc(ml["o_ready"], 1)
                    if h == HEADS - 2:
                        upper(u + 10)

            n_tile = 0

            def land(what, n, layer, halves=(0, 1), only=None):
                nonlocal n_tile
                if what in ("unit", "c1") and 0 in halves:
                    upper(FIRST_2 + L2_UNITS * layer + FETCHED[what, n] + 1)
                for half in halves if what == "unit" else (0,):
                    b = (n_tile - LAYER_TILES * layer) % 4 if only is None else only
                    t.next(b2["pj_done"])
                    n_tile += 1
                    if what == "unit":
                        kind, to = UNITS_2[n]
                        o = b_v[:, to, half, :] if kind == "v" else (b_ke if n < U_HF + 4 else b_p)[:, to + half, :]
                        m = copy(o, psum[:, b, 0:SEQ])
                    if what == "rot":
                        if n != U_KS:
                            t.next(b2["rope_done"])
                        m = copy(wide(n_rt[0:32]), psum[0:32, b, :])
                    if what == "c1":
                        for e in range(4):
                            rows = slice(SLOT * e, SLOT * e + 2 * NCMP)
                            m = copy(c1_parts[n % 2][rows, :], psum[rows, b, 0:P])
                    if what == "c1sum":
                        act.activation(wide(n_c1[n]), psum[:, b, 0:2 * NCMP], ACT.Identity, bias=V(f"b1{'kv'[n]}{layer}"))\
                           .then_inc(b2["pj_copied"], 1)
                        act.wait_ge(b2["pj_copied"], n_tile)
                        if n:
                            act.wait_ge(b2["c1_ready"], 2 * layer + 1)
                        act.activation(wide(n_ce), wide(n_c1[n]), ACT.Exp, scale=-1.0).then_inc(b2["c1_exp"], 1)
                        continue
                    if what == "c2":
                        if n == 0:
                            m = copy(wide(n_kc), psum[:, b, 0:2 * NCMP])
                        else:
                            m = copy(wide(n_vc[0:NCMP]), psum[0:NCMP, b, 0:2 * P])
                    if what == "crot":
                        m = copy(wide(n_crt[0:32]), psum[0:32, b, 0:2 * NCMP])
                    m.then_inc(b2["pj_copied"], 1)

            def layer2(layer):
                for c in range(DC):
                    t.next(b2["x_new"])
                    square(b_qe[:, c, :], x2[:, c, :])
                norm_root(D, SEQ, 7)
                for c in range(DC):
                    t.next(b2["n_new"])
                    copy(b_ns[0][:, c, :], b_n[:, c, :]).then_inc(b2["n_hi"], 1)
                if layer == 0:
                    t.next(b2["lb_d"])
                    act.activation(wide(b_lbt), wide(b_lbt), ACT.Exp).then_inc(b2["lb_e"], 1)
                for m in FIRST[:4]:
                    land(*m, layer)
                t.next(b2["lin_ready"])
                f = wide(b_ke)
                act.wait_ge(b2["pj_copied"], LAYER_TILES * layer + 8)
                act.activation(wide(b_g), f, ACT.Sigmoid)
                act.activation(wide(b_k), f, ACT.Sigmoid, scale=-1.0).then_inc(b2["sig_done"], 1)
                t.next(b2["ng_done"])
                act.activation(wide(n_gate), psum[:, 4, 0:48], ACT.Sigmoid).then_inc(b2["gate_ready"], 1)
                for m in FIRST[4:8]:
                    land(*m, layer)
                t.next(b2["lin_ready"])
                act.activation(wide(b_g), wide(b_g), ACT.Ln).then_inc(b2["ln_done"], 1)
                for m in FIRST[8:]:
                    land(*m, layer)
                half_d = [b_d[:, part * D:part * D + D] for part in range(2)]
                for job in range(9):
                    if job < 8:
                        for x in half_d:
                            t.next(b2["lv_d"])
                            act.activation(x, x, ACT.Exp).then_inc(b2["lv_e"], 1)
                    for m in JOBS[job]:
                        land(*m, layer)
                t.next(b2["rope_done"])

                def gate(units):
                    for _, u in units:
                        act.wait_ge(b2["pj_copied"], LAYER_TILES * layer + MADE["unit", u])
                        x = wide(b_p[:, UNITS_2[u][1]:UNITS_2[u][1] + 2, :])
                        act.activation(x, x, ACT.Silu).then_inc(b2["z_ready"], 1)

                def exps(h):
                    _, least, total = n_st[h % 2]
                    t.next(b2["mx_ready"])
                    for br in range(2):
                        for i, at, n in ((0, 0, P), (1, P, SEQ)):
                            c = 2 * br + i
                            m = act.activation(n_e[h % 2][:, br, at:at + n], psum[:, 2 * (h % 2) + br, at:at + n], ACT.Exp,
                                               scale=NSA_SCALE, bias=least[:, c:c + 1], accum_out=total[:, c:c + 1])
                    m.then_inc(b2["e_done"], 1)

                exps(0)
                t.next(b2["cs_ready"])
                act.activation(wide(n_cs), wide(n_cs), ACT.Exp).then_inc(b2["ce_done"], 1)
                land(*BEFORE_HEADS[0], layer, halves=(0,), only=2)
                land(*BEFORE_HEADS[0], layer, halves=(1,), only=3)
                t.next(b2["av_done"])
                copy(wide(b_ke), flat[:, 2048:4096]).then_inc(b2["o_copied"], 1)
                land(*BEFORE_HEADS[1], layer, halves=(0,), only=2)
                land(*BEFORE_HEADS[1], layer, halves=(1,), only=3)
                t.next(b2["osum"])
                act.activation(wide(b_qe), flat[:, 2048:4096], ACT.Ln, scale=1.0 / P, bias=eps[:, :]).then_inc(b2["olog"], 1)
                t.next(b2["olog"])
                act.activation(wide(b_qe), wide(b_qe), ACT.Exp, scale=-0.5).then_inc(b2["oroot"], 1)
                exps(1)
                for h in range(HEADS):
                    pt = n_pt[h % 2]
                    if h < len(IN_HEADS):
                        land(*IN_HEADS[h], layer, halves=(0,), only=7)
                    t.next(b2["pt_done"])
                    copy(pt[:, 0, 0:3 * P], psum[:, 4, 0:3 * P]).then_inc(b2["pta_copied"], 1)
                    copy(pt[0:NCMP, 0, 3 * P:4 * P], psum[0:NCMP, 4, 3 * P:4 * P]).then_inc(b2["pta_copied"], 1)
                    if h + 2 < HEADS:
                        exps(h + 2)
                    if h < len(IN_HEADS):
                        land(*IN_HEADS[h], layer, halves=(1,), only=7)
                    if h == 0:
                        gate(BEFORE_HEADS)
                    if h >= len(IN_HEADS):
                        upper(FIRST_2 + L2_UNITS * layer + LAST_FETCHED + h - len(IN_HEADS) + 2)
                    if h in GATED:
                        gate([IN_HEADS[n] for n in GATED[h]])
                    if h in HGRN_AT:
                        t.next(b2["o_h"])
                        at = HGRN_AT[h]
                        copy(b_ohs[0][:, 2 * at:2 * at + 2, :], b_p[:, F_HZ + 2 * at:F_HZ + 2 * at + 2, :]).then_inc(b2["oh_hi"], 1)
                    t.next(b2["o_n"])
                    copy(b_ons[0][:, h, :], b_p[:, F_NZ + h, :]).then_inc(b2["on_hi"], 1)
                upper(FIRST_2 + L2_UNITS * layer + LAST_FETCHED + 4)
                upper(FIRST_2 + L2_UNITS * layer + LAST_FETCHED + 5)
                for c in range(DC):
                    upper(FIRST_2 + L2_UNITS * layer + LAST_FETCHED + 6 + c // 2)
                    act.wait_ge(b2["wo_done"], 16 * layer + DC + c + 1)
                    square(b_qe[:, c, :], psum[:, c, 0:SEQ])
                    copy(b_p[:, c, :], psum[:, c, 0:SEQ]).then_inc(b2["wo_copied"], 1)
                norm_root(D, SEQ, 0)

            conv()
            moe(0)
            mla()
            moe(1)
            upper(FIRST_2)
            norm_root(D, SEQ, 0)
            upper(FIRST_2 + 1)
            layer2(0)
            layer2(1)

        @block.gpsimd
        def _(gp):
            t = Turns(gp)
            n_unit = 0

            def lower(lo, whole, hi):
                return gp.tensor_tensor(lo, whole, hi, ALU.subtract)

            def split_unit():
                nonlocal n_unit
                slot, n_unit = n_unit % PAIRS_OF_SLOTS, n_unit + 1
                t.next(w_hi)
                for at in (slice(0, UNIT // 2), slice(UNIT // 2, UNIT)):
                    lower(ring_parts[:, slot, at], ring[:, slot, at], ring_parts[:, PAIRS_OF_SLOTS + slot, at]).then_inc(w_ready, 1)

            def layer2(layer):
                nonlocal n_unit
                if layer:
                    gp.wait_ge(b2["ng_done"], layer)
                else:
                    t.next(b2["x_new"])
                gates, hi = V(f"wng{layer}"), wng_hi[:, :]
                gp.tensor_copy(hi, gates).then_inc(b2["g_hi"], 1)
                t.next(b2["g_hi"])
                lower(V(f"wng{layer}", vecs_parts), gates, hi)
                for what, n in FIRST + [m for job in JOBS for m in job] + BEFORE_HEADS + IN_HEADS[:2]:
                    if what == "c1":
                        n_unit += 1
                    if what == "unit":
                        split_unit()
                for h in range(HEADS):
                    if h in HGRN_AT:
                        t.next(b2["oh_hi"])
                        at = slice(2 * HGRN_AT[h], 2 * HGRN_AT[h] + 2)
                        lower(b_ohs[1][:, at, :], b_p[:, F_HZ + at.start:F_HZ + at.stop, :], b_ohs[0][:, at, :])\
                            .then_inc(b2["oh_lo"], 1)
                    split_unit()
                    t.next(b2["on_hi"])
                    lower(b_ons[1][:, h, :], b_p[:, F_NZ + h, :], b_ons[0][:, h, :]).then_inc(b2["on_lo"], 1)
                for _ in range(4):
                    split_unit()

            def split_chunks(parts, whole, chunks, done=None):
                for c in chunks:
                    t.next(done or x_hi)
                    lower(parts[1][:, c, :], whole[:, c, :], parts[0][:, c, :]).then_inc(x_lo, 1)

            def units(n):
                for _ in range(n):
                    split_unit()

            units(2)
            t.next(const_in, 32)
            t.next(late_in, 48)
            for n, x in small.items():
                at = SMALL_AT.get(n, (0,))[0]
                gp.tensor_copy(x[:, :], whole_small[:, at:at + P] if n in SMALL else C(n)).then_inc(small_set, 1)
            t.next(x_hi, DC)
            units(3)
            for j in range(3):
                units(3 if j < 2 else 2)
                split_chunks(cv_ys, cv_yt, (2 * j, 2 * j + 1))
            split_chunks(cv_ys, cv_yt, (DC - 2, DC - 1))
            units(3)
            units(9)
            for first, end in ((0, 2), (2, HEADS - 1), (HEADS - 1, HEADS)):
                split_chunks(ml_os, ml_o, range(first, end), ml["o_ready"])
                units(1)
            layer2(0)
            layer2(1)

        @block.vector
        def _(v):
            t = Chain(v, dve_chain)

            def norm(x, n, w, outs, hi=x_hi, lo=x_lo):
                t.next(nrm_root)
                t.link(v.reciprocal(root[:, 0:w], root[:, 0:w]))
                for o, gain, signal, parts in outs:
                    for c in range(n + 1):
                        if c < n:
                            v.scalar_tensor_tensor(o[:, c, 0:w], x[:, c, :], gain[:, c:c + 1], root[:, 0:w], ALU.mult, ALU.mult)\
                             .then_inc(signal, 1)
                        if parts and c:
                            t.next(hi)
                            v.tensor_tensor(parts[1][:, c - 1, :], o[:, c - 1, 0:w], parts[0][:, c - 1, :], ALU.subtract)\
                             .then_inc(lo, 1)
                    t.next(signal, n)

            def tt(o, a, b, op, sem=None):
                t.link(v.tensor_tensor(o, a, b, op), sem)

            def ts(o, a, s1, op1, s2=None, op2=None, sem=None):
                t.link(v.tensor_scalar(o, a, s1, s2, op1, op2) if op2 else v.tensor_scalar(o, a, s1, None, op1), sem)

            def stt(o, a, s, b, op1, op2, sem=None):
                t.link(v.scalar_tensor_tensor(o, a, s, b, op1, op2), sem)

            def red(o, a, op, sem=None):
                t.link(v.tensor_reduce(o, a, AX, op), sem)

            def rep(a, n):
                return a.unsqueeze(len(a.shape)).to_broadcast([*a.shape, n])

            def rep_mid(a, n):
                return a.unsqueeze(1).to_broadcast([a.shape[0], n, a.shape[1]])

            def residual(layer):
                s = moe_sem[layer]
                gain = V(f"ffn{layer}")
                for c in range(DC):
                    t.next(pr_done)
                    if c == 0:
                        v.memset(mo_n[:, :, T:TP], 0.0)
                        v.memset(r_t, 1.0)
                    if c == 1:
                        v.memset(mo_sw[:, :], 0.0).then_inc(s["sw_ready"], 1)
                        v.memset(mo_stw, 0.0).then_inc(s["stw_done"], 1)
                    if c == 2:
                        v.memset(mo_y[:, 0:512], 0.0).then_inc(s["ya_ready"], 1)
                        v.memset(mo_y[:, 512:1024], 0.0).then_inc(s["yd_ready"], 1)
                    tt(hT[:, c, :], hT[:, c, :], psum[:, 6 + c % 2, 0:T], ALU.add, pr_add)
                    v.tensor_scalar(mo_n[:, c, 0:T], hT[:, c, :], gain[:, c:c + 1], None, ALU.mult).then_inc(route["x_gain"], 1)

            def conv():
                t.link(v.memset(eps[:, :], EPS), eps_set)
                t.link(v.memset(cv_z[:, 0:2], 0.0))
                for x in tokens_in:
                    t.next(x, 16)
                t.next(const_in, 32)
                norm(hT[:, :, :], DC, T, [(cv_n, V("mix0"), nrm_out, cv_ns)])
                cw = V("convw").rearrange("p (k c) -> p k c", k=3)
                for j in range(4):
                    for half in range(2):
                        c = 2 * j + half
                        t.next(cv_c)
                        v.wait_ge(cv_pe, 6 * j + 5 + half)
                        tt(cv_z[:, 2:T + 2], cv_csb[:, half, :], psum[:, 3 * half + 2, 0:T], ALU.mult)
                        ts(cv_t, cv_z[:, 0:T], cw[:, 0, c:c + 1], ALU.mult)
                        for k in range(1, 3):
                            stt(cv_t, cv_z[:, k:T + k], cw[:, k, c:c + 1], cv_t, ALU.mult, ALU.add)
                        tt(cv_yt[:, c, :], cv_t, psum[:, 3 * half, 0:T], ALU.mult, cv_y)
                residual(0)

            def moe(layer):
                s = moe_sem[layer]
                if layer == 0:
                    t.next(late_in, 48)
                v.wait_ge(route["lg_done"], layer + 1)
                v.wait_ge(route["r_root"], layer + 1)
                t.link(v.reciprocal(r_t, r_t), route["r_ready"])
                lg = mo_lg
                tt(lg, psum[:, 0, 0:TT * 72].rearrange("p (t n) -> p t n", t=TT), rep(r_t, 72), ALU.mult)
                revidx = rep_mid(C("revidx"), TT)

                def first(oh, x, i):
                    stt(r8[9], x, 0.0, revidx, ALU.is_equal, ALU.mult)
                    red(r1[i], r8[9], ALU.max)
                    tt(oh, r8[9], rep(r1[i], 8), ALU.is_equal)

                gmax, gsum, pg = r1[0], r1[1], r1[2]
                red(gmax, lg[:, :, 0:8], ALU.max)
                tt(r8[1], lg[:, :, 0:8], rep(gmax, 8), ALU.subtract, route["dg_ready"])
                grp = r8[3]
                first(grp, r8[1], 9)
                part = flat_tmp.rearrange("p (t g e) -> p t g e", t=TT, g=G)
                tt(part, lg[:, :, 8:72].rearrange("p t (g e) -> p t g e", g=G), rep(grp, 8), ALU.mult)
                red(r8[4], part.rearrange("p t g e -> p t e g"), ALU.add)
                red(r1[3], r8[4], ALU.max)
                tt(r8[5], r8[4], rep(r1[3], 8), ALU.subtract, route["dg_ready"])
                prob, one, two = r8[6], r8[7], r8[8]
                first(one, r8[5], 9)
                tt(grp, grp, rep(C("valid"), 8), ALU.mult)
                t.next(route["exp_done"], 2)
                stt(prob, one, -4.0, prob, ALU.mult, ALU.add)
                red(r1[6], prob, ALU.max)
                tt(r8[0], prob, rep(r1[6], 8), ALU.subtract)
                first(two, r8[0], 9)
                tt(r8[0], one, two, ALU.add)

                def over_groups(o, src, sem=None):
                    tt(o.rearrange("p t (g e) -> p t g e", g=G), rep(grp, 8),
                       src.unsqueeze(2).to_broadcast([P, TT, G, 8]), ALU.mult, sem)

                over_groups(chosen[:, :, :], r8[0], route["route_ready"])
                red(gsum, r8[2], ALU.add)
                ts(r1[7], r1[6], 1.0, ALU.add)
                tt(r1[7], r1[7], gsum, ALU.mult)
                t.link(v.reciprocal(pg, r1[7]))
                tt(two, two, rep(r1[6], 8), ALU.mult)
                tt(one, one, two, ALU.add)
                tt(one, one, rep(pg, 8), ALU.mult)
                over_groups(mo_w, one)
                v.wait_ge(route["rank_done"], layer + 1)
                rank = psum[:, 7, 0:TT * NE].rearrange("p (t n) -> p t n", t=TT)
                stt(mo_rank, rank, 1.0, chosen[:, :, :], ALU.add, ALU.mult, s["add_done"])

                def slots(quad4, base):
                    which = rep(mo_rank[:, :, bass.ds(quad4, 4)], SLOT)
                    place = C("iota")[:, bass.ds(base, SLOT)]
                    place = place.unsqueeze(1).unsqueeze(1).to_broadcast([P, TT, 4, SLOT])
                    v.tensor_tensor(mo_st, which, place, ALU.is_equal).then_inc(s["st_ready"], 1)

                def add(i, c):
                    v.wait_ge(s["cmb_done"], i * DC + c + 1)
                    v.tensor_tensor(hT[:, c, :], hT[:, c, :], psum[:, 6 + c % 2, 0:T], ALU.add).then_inc(s["add_done"], 1)

                slots(0, 0)
                red(r_c, psum[:, 7, TT * NE:TT * NE + NE], ALU.max)
                ts(r_gt, C("rounds"), r_c[:, 0:1], ALU.is_lt)
                red(r_n, r_gt, ALU.add)
                ts(r_n, r_n, float(QUADS), ALU.mult)
                ts(r_c, r_n, -1.0, ALU.add)
                t.link(v.tensor_copy(n_last[:, layer:layer + 1], r_c))
                t.link(v.tensor_copy(n_iter[:, layer:layer + 1], r_n), route["iter_ready"])
                v.wait_ge(route["iter_ready"], layer + 1)
                n = v.value_load(n_iter[0:1, layer:layer + 1], min_val=QUADS, max_val=QUADS * ROUNDS)
                with v.Fori(0, n) as i:
                    v.wait_ge(s["st_ready"], i + 1)
                    v.wait_ge(s["stw_done"], i + 1)
                    v.tensor_tensor(mo_stw, mo_st, rep(mo_w[:, :, bass.ds((i % QUADS) * 4, 4)], SLOT), ALU.mult)\
                     .then_inc(s["stw_ready"], 1)
                    v.wait_ge(s["prep_done"], i + 1)
                    v.wait_ge(s["stw_ready"], i + 1)
                    slots(((i + 1) % QUADS) * 4, ((i + 1) // QUADS) * SLOT)
                    v.wait_ge(s["silu_done"], i + 1)
                    v.tensor_tensor(mo_h, mo_silu, psum[:, 3, 256:512], ALU.mult).then_inc(s["h_ready"], 1)
                    v.wait_ge(s["ht_done"], i + 1)
                    v.tensor_copy(wide(mo_ht), psum[:, 3, 0:256]).then_inc(s["ht_ready"], 1)
                    v.wait_ge(s["add_done"], i * DC + 1)
                    for c in range(DC):
                        add(i, c)
                    v.wait_ge(s["used"], i * QU + QU)
                    v.tensor_copy(mo_y[:, 512:1024], psum[:, 5, :]).then_inc(s["yd_ready"], 1)
                v.wait_ge(s["add_done"], n * DC + 1)
                for c in range(DC):
                    add(n, c)
                v.wait_ge(s["add_done"], n * DC + (DC + 1))

            def rope(x, rot, cos, sin, tmp, sem=None):
                tt(tmp, rot, sin, ALU.mult)
                tt(x, x, cos, ALU.mult)
                tt(x, x, tmp, ALU.add, sem)

            def mla():
                for st in ml_st:
                    for x in st:
                        v.memset(x, 1.0)
                t.link(v.memset(ml_krz, 0.0))
                t.next(x_hi, DC)
                norm(hT[:, :, :], DC, T, [(ml_kv, V("kvg"), nrm_out, ml_kvs), (ml_q, V("mix1"), nrm_out, ml_qs)])
                norm(ml_ckv, 2, T, [(ml_ckvn, V("ckvg"), nrm_out, ml_ckvs)])
                t.next(ml["krot_done"])
                rope(ml_kr, psum[:, 6, 0:T], C("cosm"), C("sinm"), ml_rt[:, 0, :])
                t.link(v.tensor_copy(ml_krz[0:64, 0, :], ml_kr[0:64, :]))
                t.link(v.tensor_copy(ml_krz[64:P, 1, :], ml_kr[64:P, :]), ml["kr_ready"])
                norm(ml_cq, 3, T, [(ml_cqn, V("cqg"), nrm_out, ml_cqs)])
                t.next(ml["rot_done"])
                for x in (slice(0, 2), slice(2, 4)):
                    rope(ml_qr[:, x], psum[:, 4 + x.start:4 + x.stop, 0:T], rep_mid(C("cosm"), 2), rep_mid(C("sinm"), 2),
                         ml_rt[:, x], ml["q_ready"])

                def maxima(h):
                    mx, least, _ = ml_st[h % 2]
                    t.next(ml["sc_done"])
                    for i in range(TT):
                        n, keys = min(P, T - i * P), min(T, i * P + P)
                        b, at = 2 * (h % 2) + i // 2, (0, P, 0)[i]
                        m = v.tensor_reduce(mx[0:n, i:i + 1], psum[0:n, b, at:at + keys], AX, ALU.max)
                    t.link(m)
                    ts(least, mx, -MLA_SCALE, ALU.mult, sem=ml["mx_ready"])

                def probs(h):
                    e, (_, _, total) = ml_e[h % 2], ml_st[h % 2]
                    t.next(ml["e_done"])
                    t.link(v.reciprocal(total, total))
                    for i in range(TT):
                        n, keys, at = min(P, T - i * P), min(T, i * P + P), (0, P, 3 * P)[i]
                        m = v.tensor_scalar(e[0:n, at:at + keys], e[0:n, at:at + keys], total[0:n, i:i + 1], None, ALU.mult)
                    t.link(m, ml["p_ready"])

                maxima(0)
                maxima(1)
                probs(0)
                for h in range(HEADS):
                    if h + 1 < HEADS:
                        probs(h + 1)
                    if h + 2 < HEADS:
                        maxima(h + 2)
                residual(1)

            def bounds():
                lg = V("lbl").rearrange("p (l c) -> p l c", l=2)
                tt(b_bl, lg[:, 0], lg[:, 1], ALU.max)
                tt(b_lbt, lg, rep_mid(b_bl, 2), ALU.subtract, b2["lb_d"])
                t.next(b2["lb_e"])
                tt(b_bl, b_lbt[:, 0], b_lbt[:, 1], ALU.add)
                t.link(v.reciprocal(b_bl, b_bl))
                tt(b_lbt, b_lbt, rep_mid(b_bl, 2), ALU.mult)
                tt(b_lb[:, 0], b_lbt[:, 0], b_lbt[:, 0], ALU.subtract)
                tt(b_lb[:, 1], b_lbt[:, 0], b_lbt[:, 1], ALU.add)
                tt(b_lb[:, 1], b_lb[:, 1], b_lbt[:, 0], ALU.subtract)
                ts(b_lb, b_lb, 0.0, ALU.max)
                ts(b_lbi, b_lb, -1.0, ALU.mult, 1.0, ALU.add)

            def layer2(layer):
                made = LAYER_TILES * layer

                def landed_by(what, n):
                    v.wait_ge(b2["pj_copied"], made + MADE[what, n])

                norm(x2, DC, SEQ, [(b_n, V(f"pre{layer}"), b2["n_new"], b_ns)], b2["n_hi"], b2["n_lo"])
                if layer == 0:
                    bounds()
                t.link(v.memset(wide(b_at), 0.0), b2["lin_ready"])
                t.next(b2["sig_done"])
                tt(b_g, b_g, rep(b_lbi[:, layer], SEQ), ALU.mult)
                tt(b_g, b_g, rep(b_lb[:, layer], SEQ), ALU.add)
                ts(b_g, b_g, LN_LEAST, ALU.max, sem=b2["lin_ready"])
                tt(b_k, b_k, rep(b_lbi[:, layer], SEQ), ALU.mult)
                t.next(b2["ln_done"])
                for h in range(HEADS):
                    m = v.tensor_tensor_scan(b_b[:, h, :], C("reset"), b_g[:, h, :], 0.0, ALU.mult, ALU.add)
                t.link(m)
                q = b_p[:, F_Q:F_Q + HEADS, :]
                landed_by("unit", 7)
                masks = C("lev").rearrange("p (j t) -> p j t", j=7).bitcast(U32)

                def decay(job, part):
                    b, d = wide(b_b[:, 4 * part:4 * part + 4, :]), b_d[:, part * D:part * D + D]
                    if job < len(LEVELS):
                        n = LEVELS[job]
                        x, o = (y.rearrange("p (k n) -> p k n", n=n) for y in (b, d))
                        ref = x[:, :, n // 2 - 1:n // 2].to_broadcast([P, D // n, n // 2])
                        v.tensor_tensor(o[:, :, 0:n // 2], ref, x[:, :, 0:n // 2], ALU.subtract)
                        tt(o[:, :, n // 2:n], x[:, :, n // 2:n], ref, ALU.subtract, b2["lv_d"])
                        return
                    end = CHUNK - 1
                    if job == 6:
                        x, o = (y.rearrange("p (k c n) -> p k c n", c=2, n=CHUNK) for y in (b, d))
                        v.tensor_tensor(o[:, :, 0], x[:, :, 0, end:].to_broadcast([P, PAIRS // 2, CHUNK]), x[:, :, 0], ALU.subtract)
                        t.link(v.tensor_copy(o[:, :, 1], x[:, :, 1]), b2["lv_d"])
                        return
                    x, o = (y.rearrange("p (h c n) -> p h c n", c=4, n=CHUNK) for y in (b, d))
                    tt(b_bl[:, 0:4], x[:, :, 0, end], x[:, :, 1, end], ALU.add)
                    v.tensor_tensor(o[:, :, 0], rep(b_bl[:, 0:4], CHUNK), x[:, :, 0], ALU.subtract)
                    v.tensor_tensor(o[:, :, 1], x[:, :, 1, end:].to_broadcast([P, 4, CHUNK]), x[:, :, 1], ALU.subtract)
                    v.tensor_copy(o[:, :, 2], x[:, :, 2])
                    tt(o[:, :, 3], x[:, :, 3], x[:, :, 2, end:].to_broadcast([P, 4, CHUNK]), ALU.add, b2["lv_d"])

                def gather(job):
                    for part in range(2):
                        t.next(b2["lv_mm"])
                        if job == 7:
                            at = 2048 + part * 4 * P
                            t.link(v.tensor_copy(wide(b_ax[:, 4 * part:4 * part + 4, :]), flat[:, at:at + 4 * P]), b2["lv_at"])
                            continue
                        mask = masks[:, job, :] if job < 7 else C("ident").bitcast(U32)
                        at = 2048 + part * D
                        t.link(v.copy_predicated(b_at[:, 8 * part:8 * part + 8, :], rep_mid(mask, 8),
                                                 flat[:, at:at + D].rearrange("p (k t) -> p k t", k=8)), b2["lv_at"])

                def rope_unit(u):
                    landed_by("rot", u)
                    x = b_p[0:32, UNITS_2[u][1]:UNITS_2[u][1] + 2, :]
                    rope(x, n_rt[0:32], rep_mid(C("cosn")[0:32, :], 2), rep_mid(C("sinn")[0:32, :], 2), n_rt[0:32], b2["rope_done"])

                def positions(kv):
                    landed_by("unit", (U_KC, U_VC)[kv])
                    x = b_p[:, (F_KC, F_VC)[kv]:(F_KC, F_VC)[kv] + 2, :]
                    pos = V(f"pos{'kv'[kv]}{layer}").rearrange("p (l o) -> p l o", l=2)
                    for part in range(2):
                        src = x[:, :, 16 * part:16 * part + 16 * NCMP].rearrange("p g (n l) -> p l g n", l=16)
                        at = pos[:, part].unsqueeze(2).unsqueeze(3).to_broadcast([P, 16, 2, NCMP])
                        m = v.tensor_tensor(n_kp[kv][:, 16 * part:16 * part + 16], src, at, ALU.add)
                    t.link(m, b2["kp_ready"])

                for job in range(9):
                    if job < 8:
                        decay(job, 0)
                        decay(job, 1)
                    if job in (1, 2):
                        positions(job - 1)
                    for what, n in JOBS[job - 1] if job else []:
                        if what == "rot":
                            rope_unit(n)
                        if what == "c1sum":
                            t.next(b2["c1_exp"])
                            ts(n_ce, n_ce, 1.0, ALU.add)
                            t.link(v.reciprocal(n_ce, n_ce))
                            tt(n_c1[n], n_c1[n], n_ce, ALU.mult, b2["c1_ready"])
                        if what == "crot":
                            landed_by("crot", 0)
                            rope(n_kc[0:32], n_crt[0:32], rep_mid(C("cosc")[0:32, :], 2), rep_mid(C("sinc")[0:32, :], 2),
                                 n_crt[0:32], b2["crope_done"])
                    if job:
                        gather(job - 1)
                    if job < 8:
                        n = (LEVELS + (P, SEQ))[job]
                        for part in range(2):
                            t.next(b2["lv_e"])
                            hs = slice(4 * part, 4 * part + 4)
                            e = b_d[:, part * D:part * D + D].rearrange("p (k n) -> p k n", n=n)
                            ke, qe, k_, q_ = (wide(x[:, hs, :]).rearrange("p (k n) -> p k n", n=n) for x in (b_ke, b_qe, b_k, q))
                            v.tensor_tensor(ke[:, :, 0:n // 2], k_[:, :, 0:n // 2], e[:, :, 0:n // 2], ALU.mult)
                            tt(qe[:, :, n // 2:n], q_[:, :, n // 2:n], e[:, :, n // 2:n], ALU.mult, b2["lv_kq"])
                gather(8)
                def maxima(h):
                    mx, least, _ = n_st[h % 2]
                    t.next(b2["sc_done"])
                    for br in range(2):
                        for i, at, n in ((0, 0, P), (1, P, SEQ)):
                            c = 2 * br + i
                            m = v.tensor_reduce(mx[:, c:c + 1], psum[:, 2 * (h % 2) + br, at:at + n], AX, ALU.max)
                    t.link(m)
                    ts(least, mx, -NSA_SCALE, ALU.mult, sem=b2["mx_ready"])

                v.wait_ge(b2["sc_done"], HEADS * layer + 1)
                ec = n_cs.rearrange("p i (h n) -> p i h n", h=HEADS)
                each = wide(n_cs).rearrange("p (k n) -> p k n", n=NCMP)
                cmask, cvalid = (C(n).rearrange("p (i n) -> p i n", i=2) for n in ("cmask", "cvalid"))
                for i in range(2):
                    scores = psum[:, i, 3 * P:3 * P + HEADS * NCMP].rearrange("p (h n) -> p h n", h=HEADS)
                    m = v.scalar_tensor_tensor(ec[:, i], scores, NSA_SCALE, rep_mid(cmask[:, i], HEADS), ALU.mult, ALU.add)
                t.link(m)
                maxima(0)
                red(n_cmx, each, ALU.max)
                tt(each, each, rep(n_cmx, NCMP), ALU.subtract, b2["cs_ready"])
                t.next(b2["ce_done"])
                for i in range(2):
                    m = v.tensor_tensor(ec[:, i], ec[:, i], rep_mid(cvalid[:, i], HEADS), ALU.mult)
                t.link(m)
                red(n_csum, each, ALU.add)
                ts(n_csum, n_csum, 1e-30, ALU.max)
                t.link(v.reciprocal(n_csum, n_csum))
                gates = n_gate.rearrange("p i (h b) -> p i h b", b=3)
                tt(n_csum.rearrange("p (i h) -> p i h", i=2), n_csum.rearrange("p (i h) -> p i h", i=2), gates[:, :, :, 0], ALU.mult)
                tt(each, each, rep(n_csum, NCMP), ALU.mult)
                t.next(b2["o_copied"])
                tt(b_d, wide(b_ke), wide(b_ke), ALU.mult, b2["osq"])
                maxima(1)

                def gated(u):
                    v.wait_ge(b2["z_ready"], 8 * layer + (BEFORE_HEADS + IN_HEADS).index(("unit", u)) + 1)

                def output(h):
                    t.next(b2["pv_done"])
                    tile = b_p[:, F_NZ + h, :]
                    gated(U_NZ + h // 2)
                    tt(tile, tile, psum[:, 6, 0:SEQ], ALU.mult, b2["o_n"])

                def probs(h):
                    e, (_, _, total) = n_e[h % 2], n_st[h % 2]
                    t.next(b2["e_done"])
                    t.link(v.reciprocal(total, total))
                    total = total.rearrange("p (b i) -> p b i", b=2)
                    tt(total, total, n_gate[:, :, 3 * h + 1:3 * h + 3].rearrange("p i b -> p b i"), ALU.mult)
                    v.tensor_tensor(e[:, :, 0:P], e[:, :, 0:P], rep(total[:, :, 0], P), ALU.mult)
                    tt(e[:, :, P:3 * P], e[:, :, P:3 * P], rep(total[:, :, 1], SEQ), ALU.mult, b2["p_ready"])

                probs(0)
                for h in range(HEADS):
                    pt = n_pt[h % 2]
                    if h == 0:
                        t.next(b2["oroot"])
                        stt(wide(b_ke), wide(b_ke), V(f"on{layer}"), wide(b_qe), ALU.mult, ALU.mult)
                    if h in HGRN_AT:
                        u = HGRN_AT[h]
                        gated(U_HZ + u)
                        hz = b_p[:, F_HZ + 2 * u:F_HZ + 2 * u + 2, :]
                        tt(hz, hz, b_ke[:, 2 * u:2 * u + 2, :], ALU.mult, b2["o_h"])
                    t.next(b2["pt_done"])
                    v.tensor_copy(pt[:, 1, 0:3 * P], psum[:, 5, 0:3 * P]).then_inc(b2["ptb_copied"], 1)
                    v.tensor_copy(pt[0:NCMP, 1, 3 * P:4 * P], psum[0:NCMP, 5, 3 * P:4 * P]).then_inc(b2["ptb_copied"], 1)
                    if h + 1 < HEADS:
                        probs(h + 1)
                    if h + 2 < HEADS:
                        maxima(h + 2)
                    output(h)
                t.next(b2["wo_copied"], DC)
                y = b_p[:, 0:DC, :]
                t.next(nrm_root)
                t.link(v.reciprocal(root[:, 0:SEQ], root[:, 0:SEQ]))
                gain = V(f"post{layer}")
                for c in range(DC + 1):
                    if c < DC:
                        v.scalar_tensor_tensor(y[:, c, :], y[:, c, :], gain[:, c:c + 1], root[:, 0:SEQ], ALU.mult, ALU.mult)\
                         .then_inc(dve_chain, 1)
                    if c:
                        t.next(dve_chain)
                        v.tensor_tensor(x2[:, c - 1, :], x2[:, c - 1, :], y[:, c - 1, :], ALU.add).then_inc(b2["x_new"], 1)
                t.next(b2["x_new"], DC)

            flat_tmp = wide(mo_tmp)
            conv()
            moe(0)
            mla()
            moe(1)
            norm(hT[:, :, META:T], DC, SEQ, [(x2, V("fing"), b2["x_new"], None)])
            for x in c1_parts:
                t.link(v.memset(x, 0.0))
            layer2(0)
            layer2(1)


def constants():
    import numpy as np

    f = np.float32
    p = np.arange(P)
    out = {}
    out["ident"] = np.eye(P)
    out["ones"] = np.ones((P, P))
    out["upper"] = np.triu(np.ones((P, P)), 1)
    out["iota"] = np.broadcast_to(1 + np.arange((ROUNDS + 1) * SLOT), (P, (ROUNDS + 1) * SLOT))
    out["rounds"] = np.broadcast_to(np.arange(ROUNDS) * SLOT, (P, ROUNDS))
    out["revidx"] = np.broadcast_to(8 - np.arange(8), (P, 8))
    out["valid"] = (p[:, None] + P * np.arange(TT) < T)
    token = p[:, None] + P * np.arange(TT)
    out["stack"] = p[:, None] % SLOT == np.arange(2 * NCMP)
    out["mask"] = np.where(p <= p[:, None], 0.0, MASKED)
    ended = 16 * np.arange(NCMP) + 31 <= token[:, :2, None]
    out["cmask"] = np.where(ended, 0.0, MASKED).reshape(P, -1)
    out["cvalid"] = ended.reshape(P, -1)
    out["reset"] = np.broadcast_to(np.arange(SEQ) % CHUNK != 0, (P, SEQ))
    levels = [(p[:, None] // n == p // n) & (p[:, None] % n < n // 2) & (p % n >= n // 2) for n in LEVELS + (P,)]
    out["lev"] = np.concatenate(levels, axis=1)

    def rotation(half, heads=1):
        m = np.zeros((P, 2 * half * heads))
        for h in range(heads):
            at = np.arange(half) + 2 * half * h
            m[at + half, at] = -1
            m[at, at + half] = 1
        return m

    def tables(theta, dim, at, heads=1):
        inv = f(theta) ** (-np.arange(0, dim, 2, dtype=f) / f(dim))
        ang = (at.astype(f)[None, :] * inv[:, None]).astype(f)
        rows = np.zeros((2, P, len(at)))
        rows[0, :dim * heads] = np.tile(np.cos(ang.astype(np.float64)), (2 * heads, 1))
        rows[1, :dim * heads] = np.tile(np.sin(ang.astype(np.float64)), (2 * heads, 1))
        return rows

    out["cosm"], out["sinm"] = tables(10000.0, 64, np.arange(T), 2)
    out["cosn"], out["sinn"] = tables(500000.0, 32, np.arange(SEQ))
    out["cosc"], out["sinc"] = tables(500000.0, 32, 16 * np.arange(NCMP) + 31)
    out["rotm"], out["rotn"] = rotation(32, 2), rotation(16)
    return np.concatenate([np.asarray(out[k], f).reshape(P, n) for k, n in (CONST | SMALL).items()], axis=1)


def laid_out(x):
    import numpy as np

    x = {k: np.asarray(a) for k, a in x.items()}

    def columns(a):
        return a.reshape(-1, P).T

    def rows(a):
        return a.reshape(-1, P, a.shape[-1]).transpose(1, 0, 2).reshape(P, -1)

    def unit(a):
        a = rows(a)
        return np.pad(a, ((0, 0), (0, UNIT - a.shape[1])))

    v = {"convw": np.concatenate([columns(w) for w in x["conv_w"][0, :, 0]], axis=1),
         "kvg": columns(x["kv_norm_g"]), "ckvg": columns(x["ckv_norm_g"]), "cqg": columns(x["cq_norm_g"][0]),
         "fing": columns(x["final_norm_g"]),
         "lbl": np.concatenate([columns(a) for a in x["hgrn_lb_logits_2"]], axis=1)}
    for i in range(2):
        v[f"mix{i}"], v[f"ffn{i}"] = columns(x["norm_mix_g"][i]), columns(x["norm_ffn_g"][i])
        v[f"pre{i}"], v[f"post{i}"] = columns(x["pre_norm_2"][i]), columns(x["post_norm_2"][i])
        v[f"on{i}"] = columns(x["hgrn_out_norm_2"][i])
        for kv in "kv":
            v[f"b1{kv}{i}"] = columns(x[f"cmp_b1_{kv}_2"][i])
            v[f"pos{kv}{i}"] = x[f"cmp_pos_{kv}_2"][i].T
            v[f"w2{kv}{i}"] = x[f"cmp_w2_{kv}_2"][i]
        v[f"wng{i}"] = rows(x["w_in_2"][i][:, GATE_COLUMN:GATE_COLUMN + 24])
        v[f"wr{i}"] = rows(np.concatenate([x["w_grp"][i], x["w_exp"][i]], axis=1))
    vecs = np.concatenate([v[k].reshape(P, n) for k, n in VEC.items()], axis=1)

    w = x["conv_w_in"][0]
    dense = [unit(w[:, part * D + 256 * j:part * D + 256 * j + 256]) for j in range(4) for part in range(3)]
    dense += [unit(x["conv_w_out"][0][:, 256 * j:256 * j + 256]) for j in range(4)]
    dkv, dq = x["w_dkv"], x["w_dq"][0]
    dense += [unit(dkv[:, :256]), unit(np.concatenate([dkv[:, 256:], dkv[:, 256:], dq[:, 256:]], axis=1)), unit(dq[:, :256])]
    ukv = x["w_ukv"].reshape(256, HEADS, 256)
    dense += [unit(ukv[:, :, :P].reshape(256, -1)), unit(ukv[:, :, P:].reshape(256, -1))]
    uq = x["w_uq"][0].reshape(384, HEADS, 192)
    dense += [unit(uq[:, :, P:].reshape(384, -1)), unit(uq[:, :5, :P].reshape(384, -1)), unit(uq[:, 5:, :P].reshape(384, -1))]
    dense += [unit(x["w_o"][0][:, 256 * j:256 * j + 256]) for j in range(4)]
    for i in range(2):
        w_in, w_out = x["w_in_2"][i], x["w_out_2"][i]
        for what, n in MAKES:
            if what == "unit":
                c = COLUMNS_2[n][0]
                dense.append(unit(w_in[:, c:c + 256]))
            if what == "c1":
                half, w1 = n % 2, x[f"cmp_w1_{'kv'[n // 2]}_2"][i]
                dense.append(unit(w1[half * D * 2:half * D * 2 + D * 2]))
        dense += [unit(w_out[part * D:part * D + D, 256 * j:256 * j + 256]) for part in range(2) for j in range(4)]

    gate = x["w_gate"].reshape(2, QUADS, 4, 8, P, 256)
    up = x["w_up"].reshape(2, QUADS, 4, 8, P, 256)
    both = np.stack([gate, up], axis=5).transpose(0, 1, 3, 4, 2, 5, 6).reshape(2, QUADS, 8, P, UNIT)
    down = x["w_down"].reshape(2, QUADS, 4, 2, P, 2, 512).transpose(0, 1, 5, 3, 4, 2, 6).reshape(2, QUADS, 4, P, UNIT)
    h = np.concatenate([x["meta_tokens"], x["x"][0]], axis=0).T
    return {"h_in": rows(h), "consts_in": constants(), "vecs_in": vecs, "dense": np.stack(dense),
            "experts": np.concatenate([both, down], axis=2)}


def kernel(**inputs):
    import numpy as np
    import concourse.bacc as bacc
    from concourse.bass_utils import run_bass_kernel_spmd

    nc = bacc.Bacc("TRN2", target_bir_lowering=False, num_devices=1)
    arrays = {k: np.ascontiguousarray(a) for k, a in laid_out(inputs).items()}
    args = [nc.dram_tensor(k, a.shape, mybir.dt.from_np(a.dtype), kind="ExternalInput").ap() for k, a in arrays.items()]
    out = nc.dram_tensor("out_0", (P, DC * SEQ), F32, kind="ExternalOutput").ap()
    build(nc, *args, out)
    r = run_bass_kernel_spmd(nc, [arrays], core_ids=[0])
    return r.results[0]["out_0"].reshape(P, DC, SEQ).transpose(2, 1, 0).reshape(1, SEQ, D)
```
